# Optimizing a Trainium2 kernel written in Bass

```python
import math
import jax, jax.numpy as jnp
from jax import lax
import numpy as np

D_MODEL = 1024
BATCH = 1
SEQ = 1024
DEPTH = 1
DEC_BATCH = 8
DEC_SEQ = 1
PAST_LEN = 1024
PAGE_SIZE = 128

H_A = 4
DK_A = 32
DV_A = 64
GATE_RANK = 16
GATE_TAU = 16.0
GLA_CHUNK = 64
H_D = 12
DH_D = 64
DIL_CONFIGS = ((128, 1), (512, 4), (2048, 16))
MAX_WINDOW = 2048
N_BUCKETS = 32
MAX_DISTANCE = 2048
N_EXPERTS = 16
N_EXPERT_GROUPS = 4
TOP_K = 2
D_FF_EXPERT = 512
EPS = 1e-6

MIX_WIDTH = H_A * DV_A + H_D * DH_D
PROJ_SIZES = (H_A * DK_A, H_A * DK_A, H_A * DV_A, GATE_RANK, H_A * DV_A, H_D * DH_D, H_D * DH_D, H_D * DH_D)
D_IN = sum(PROJ_SIZES)

kernel_name = "hymba_gla_dilated_moe_step"

def rmsnorm(x, g):
    xf = x.astype(jnp.float32)
    y = xf * lax.rsqrt(jnp.mean(xf * xf, axis=-1, keepdims=True) + EPS)
    return (y * g.astype(jnp.float32)).astype(x.dtype)

def rel_bucket(dist):
    max_exact = N_BUCKETS // 2
    d = jnp.maximum(dist, 0)
    df = jnp.maximum(d, 1).astype(jnp.float32)
    large = max_exact + (jnp.log(df / max_exact) / math.log(MAX_DISTANCE / max_exact)
                         * (N_BUCKETS - max_exact)).astype(jnp.int32)
    large = jnp.minimum(large, N_BUCKETS - 1)
    return jnp.where(d < max_exact, d, large)

def split_proj(proj):
    offs = np.cumsum(PROJ_SIZES)[:-1].tolist()
    return jnp.split(proj, offs, axis=-1)

def gla_chunked(q, k, v, log_a, s0, chunk):
    B, S, H, DK = q.shape
    n = S // chunk

    def to_chunks(t):
        return jnp.moveaxis(t.astype(jnp.float32).reshape(B, n, chunk, H, t.shape[-1]), 1, 0)

    qc, kc, vc, gc = to_chunks(q), to_chunks(k), to_chunks(v), to_chunks(log_a)
    causal = jnp.tril(jnp.ones((chunk, chunk), bool))[None, :, :, None, None]

    def step(s, inp):
        qi, ki, vi, gi = inp
        b = jnp.cumsum(gi, axis=1)
        diff = jnp.where(causal, b[:, :, None] - b[:, None, :], -jnp.inf)
        att = jnp.einsum('bthk,bshk,btshk->bhts', qi, ki, jnp.exp(diff))
        o = jnp.einsum('bhts,bshv->bthv', att, vi) + jnp.einsum('bthk,bhkv->bthv', qi * jnp.exp(b), s)
        b_last = b[:, -1]
        k_dec = ki * jnp.exp(b_last[:, None] - b)
        s_new = jnp.exp(b_last)[..., None] * s + jnp.einsum('bshk,bshv->bhkv', k_dec, vi)
        return s_new, o

    s_fin, o = lax.scan(step, s0, (qc, kc, vc, gc))
    o = jnp.moveaxis(o, 0, 1).reshape(B, S, H, -1)
    return o, s_fin

def combine_branches(outs, lses):
    w = jax.nn.softmax(jnp.stack(lses, axis=0), axis=0)
    return jnp.einsum('cbsh,cbshd->bshd', w, jnp.stack(outs, axis=0))

def dilated_prompt(q, k, v, rel_bias):
    B, S, H, D = q.shape
    scale = DH_D ** -0.5
    outs, lses = [], []
    for (w, d) in DIL_CONFIGS:
        blk = w // d
        span = d * blk
        Sp = -(-S // span) * span
        nb = Sp // span

        def split(t):
            t = jnp.pad(t, ((0, 0), (0, Sp - S), (0, 0), (0, 0))).reshape(B, Sp // d, d, H, D)
            return jnp.moveaxis(t, 2, 1).reshape(B, d, nb, blk, H, D)

        def with_prev(t):
            prev = jnp.pad(t, ((0, 0), (0, 0), (1, 0), (0, 0), (0, 0), (0, 0)))[:, :, :-1]
            return jnp.concatenate([prev, t], axis=3)

        qb = split(q)
        kw, vw = with_prev(split(k)), with_prev(split(v))
        i = jnp.arange(blk)[:, None]
        j = jnp.arange(2 * blk)[None, :]
        delta = blk + i - j
        band = (delta >= 0) & (delta <= blk)
        first = (jnp.arange(nb) == 0)[:, None, None]
        valid = band[None] & ~(first & (j < blk)[None])
        bias = jnp.moveaxis(rel_bias[rel_bucket(delta * d)], -1, 0).astype(jnp.float32)
        logits = jnp.einsum('brnqhd,brnkhd->brnhqk', qb, kw) * scale + bias[None, None, None]
        logits = jnp.where(valid[None, None, :, None], logits, -jnp.inf)
        m = jnp.max(logits, axis=-1, keepdims=True)
        p = jnp.exp(logits - m)
        den = jnp.sum(p, axis=-1, keepdims=True)
        o = jnp.einsum('brnhqk,brnkhd->brnqhd', p / den, vw)
        lse = jnp.moveaxis((m + jnp.log(den))[..., 0], -1, -2)
        o = jnp.moveaxis(o.reshape(B, d, Sp // d, H, D), 1, 2).reshape(B, Sp, H, D)[:, :S]
        lse = jnp.moveaxis(lse.reshape(B, d, Sp // d, H), 1, 2).reshape(B, Sp, H)[:, :S]
        outs.append(o)
        lses.append(lse)
    return combine_branches(outs, lses)

def dilated_sample(q, k_new, v_new, buf_k, buf_v, rel_bias):
    Bd, T, H, D = q.shape
    L = buf_k.shape[1]
    scale = DH_D ** -0.5
    k_all = jnp.concatenate([buf_k.astype(jnp.float32), k_new], axis=1)
    v_all = jnp.concatenate([buf_v.astype(jnp.float32), v_new], axis=1)
    t = jnp.arange(T)
    outs, lses = [], []
    for (w, d) in DIL_CONFIGS:
        jj = jnp.arange(w // d + 1)
        idx = L + t[:, None] - jj[None, :] * d
        valid = idx >= 0
        idxc = jnp.maximum(idx, 0)
        kg, vg = k_all[:, idxc], v_all[:, idxc]
        bias = rel_bias[rel_bucket(jj * d)].astype(jnp.float32)
        logits = jnp.einsum('bthd,btjhd->bhtj', q, kg) * scale + bias.T[None, :, None, :]
        logits = jnp.where(valid[None, None], logits, -jnp.inf)
        m = jnp.max(logits, axis=-1, keepdims=True)
        p = jnp.exp(logits - m)
        den = jnp.sum(p, axis=-1, keepdims=True)
        outs.append(jnp.einsum('bhtj,btjhd->bthd', p / den, vg))
        lses.append(jnp.transpose((m + jnp.log(den))[..., 0], (0, 2, 1)))
    return combine_branches(outs, lses)

def moe(h, router_w, router_b, wg, wu, wd):
    B, S, D = h.shape
    x = h.reshape(-1, D)
    n = x.shape[0]
    per_group = N_EXPERTS // N_EXPERT_GROUPS
    scores = jax.nn.sigmoid(jnp.matmul(x, router_w).astype(jnp.float32))
    sel = scores + router_b.astype(jnp.float32)
    group_score = lax.top_k(sel.reshape(n, N_EXPERT_GROUPS, per_group), 2)[0].sum(-1)
    gmask = jax.nn.one_hot(jnp.argmax(group_score, axis=-1), N_EXPERT_GROUPS, dtype=jnp.bool_)
    masked = jnp.where(jnp.repeat(gmask, per_group, axis=1), sel, -jnp.inf)
    _, top_idx = lax.top_k(masked, TOP_K)
    top_w = jnp.take_along_axis(scores, top_idx, axis=-1)
    top_w = top_w / jnp.sum(top_w, axis=-1, keepdims=True)
    gate = jnp.einsum('nk,nke->ne', top_w, jax.nn.one_hot(top_idx, N_EXPERTS, dtype=jnp.float32)).astype(h.dtype)
    hid = jax.nn.silu(jnp.einsum('nd,edf->nef', x, wg)) * jnp.einsum('nd,edf->nef', x, wu)
    y = jnp.einsum('nef,efd->nd', hid * gate[:, :, None], wd)
    return y.reshape(B, S, D)

def trunk(x, c, gla_state, win_k, win_v, prompt,
          w_ada, b_ada, norm1_g, norm2_g, w_in, w_gate_up, b_gate, gla_norm_g, w_o,
          rel_bias, router_w, router_b, moe_w_gate, moe_w_up, moe_w_down, final_norm_g):
    B, S, _ = x.shape
    cs = jax.nn.silu(c)
    new_s, new_k, new_v = [], [], []
    for l in range(DEPTH):
        mod = (jnp.matmul(cs, w_ada[l]) + b_ada[l])[:, None, :]
        sh1, sc1, g1, sh2, sc2, g2 = jnp.split(mod, 6, axis=-1)
        h = rmsnorm(x, norm1_g[l]) * (1 + sc1) + sh1
        q_a, k_a, v_a, g_lr, r_a, q_d, k_d, v_d = split_proj(jnp.matmul(h, w_in[l]))
        q_a = q_a.reshape(B, S, H_A, DK_A) * (DK_A ** -0.5)
        k_a = k_a.reshape(B, S, H_A, DK_A)
        v_a = v_a.reshape(B, S, H_A, DV_A)
        log_a = jax.nn.log_sigmoid((jnp.matmul(g_lr, w_gate_up[l]) + b_gate[l]).astype(jnp.float32)) / GATE_TAU
        log_a = log_a.reshape(B, S, H_A, DK_A)
        if prompt:
            s0 = jnp.zeros((B, H_A, DK_A, DV_A), jnp.float32)
        else:
            s0 = gla_state[l].astype(jnp.float32)
        o_a, s_fin = gla_chunked(q_a, k_a, v_a, log_a, s0, math.gcd(S, GLA_CHUNK))
        o_a = rmsnorm(o_a, gla_norm_g[l].reshape(H_A, DV_A)).astype(x.dtype).reshape(B, S, H_A * DV_A)
        o_a = o_a * jax.nn.silu(r_a)
        q_d = q_d.reshape(B, S, H_D, DH_D).astype(jnp.float32)
        k_d = k_d.reshape(B, S, H_D, DH_D).astype(jnp.float32)
        v_d = v_d.reshape(B, S, H_D, DH_D).astype(jnp.float32)
        if prompt:
            o_d = dilated_prompt(q_d, k_d, v_d, rel_bias)
            keep = min(MAX_WINDOW, S)
            new_k.append(k_d[:, S - keep:].astype(x.dtype))
            new_v.append(v_d[:, S - keep:].astype(x.dtype))
        else:
            o_d = dilated_sample(q_d, k_d, v_d, win_k[l], win_v[l], rel_bias)
            new_k.append(k_d.astype(x.dtype))
            new_v.append(v_d.astype(x.dtype))
        new_s.append(s_fin.astype(x.dtype))
        mix = jnp.concatenate([o_a, o_d.astype(x.dtype).reshape(B, S, H_D * DH_D)], axis=-1)
        x = x + g1 * jnp.matmul(mix, w_o[l])
        h = rmsnorm(x, norm2_g[l]) * (1 + sc2) + sh2
        x = x + g2 * moe(h, router_w, router_b, moe_w_gate[l], moe_w_up[l], moe_w_down[l])
    y = rmsnorm(x, final_norm_g)
    return y, jnp.stack(new_s), jnp.stack(new_k), jnp.stack(new_v)

def setup_inputs(seed: int = 0) -> dict:
    key = jax.random.key(seed)
    ks = jax.random.split(key, 32)
    f32 = jnp.float32
    win = min(MAX_WINDOW, PAST_LEN)

    def nrm(k, shape, s):
        return jax.random.normal(k, shape, f32) * s

    return {
        "x_prompt": nrm(ks[0], (BATCH, SEQ, D_MODEL), 1.0),
        "x_sample": nrm(ks[1], (DEC_BATCH, DEC_SEQ, D_MODEL), 1.0),
        "state_gla": nrm(ks[2], (DEPTH, DEC_BATCH, H_A, DK_A, DV_A), 1.0),
        "cache_win_k": nrm(ks[3], (DEPTH, DEC_BATCH, win, H_D, DH_D), 1.0),
        "cache_win_v": nrm(ks[4], (DEPTH, DEC_BATCH, win, H_D, DH_D), 1.0),
        "c_prompt": nrm(ks[5], (BATCH, D_MODEL), 1.0),
        "c_sample": nrm(ks[6], (DEC_BATCH, D_MODEL), 1.0),
        "w_ada": nrm(ks[7], (DEPTH, D_MODEL, 6 * D_MODEL), 0.3 * D_MODEL ** -0.5),
        "b_ada": nrm(ks[8], (DEPTH, 6 * D_MODEL), 0.02),
        "norm1_g": 1.0 + nrm(ks[9], (DEPTH, D_MODEL), 0.02),
        "norm2_g": 1.0 + nrm(ks[10], (DEPTH, D_MODEL), 0.02),
        "w_in": nrm(ks[11], (DEPTH, D_MODEL, D_IN), D_MODEL ** -0.5),
        "w_gate_up": nrm(ks[12], (DEPTH, GATE_RANK, H_A * DK_A), GATE_RANK ** -0.5),
        "b_gate": nrm(ks[13], (DEPTH, H_A * DK_A), 0.1),
        "gla_norm_g": 1.0 + nrm(ks[14], (DEPTH, H_A * DV_A), 0.02),
        "w_o": nrm(ks[15], (DEPTH, MIX_WIDTH, D_MODEL), MIX_WIDTH ** -0.5),
        "rel_bias": nrm(ks[16], (N_BUCKETS, H_D), 0.5),
        "router_w": nrm(ks[17], (D_MODEL, N_EXPERTS), D_MODEL ** -0.5),
        "router_b": nrm(ks[18], (N_EXPERTS,), 0.01),
        "moe_w_gate": nrm(ks[19], (DEPTH, N_EXPERTS, D_MODEL, D_FF_EXPERT), D_MODEL ** -0.5),
        "moe_w_up": nrm(ks[20], (DEPTH, N_EXPERTS, D_MODEL, D_FF_EXPERT), D_MODEL ** -0.5),
        "moe_w_down": nrm(ks[21], (DEPTH, N_EXPERTS, D_FF_EXPERT, D_MODEL), D_FF_EXPERT ** -0.5),
        "final_norm_g": 1.0 + nrm(ks[22], (D_MODEL,), 0.02),
    }

def reference(x_prompt, x_sample, state_gla, cache_win_k, cache_win_v, c_prompt, c_sample,
              w_ada, b_ada, norm1_g, norm2_g, w_in, w_gate_up, b_gate, gla_norm_g, w_o,
              rel_bias, router_w, router_b, moe_w_gate, moe_w_up, moe_w_down, final_norm_g):
    y_prompt, gla_state_p, win_k_p, win_v_p = trunk(
        x_prompt, c_prompt, None, None, None, True,
        w_ada, b_ada, norm1_g, norm2_g, w_in, w_gate_up, b_gate, gla_norm_g, w_o,
        rel_bias, router_w, router_b, moe_w_gate, moe_w_up, moe_w_down, final_norm_g)
    y_sample, gla_state_s, new_k_s, new_v_s = trunk(
        x_sample, c_sample, state_gla, cache_win_k, cache_win_v, False,
        w_ada, b_ada, norm1_g, norm2_g, w_in, w_gate_up, b_gate, gla_norm_g, w_o,
        rel_bias, router_w, router_b, moe_w_gate, moe_w_up, moe_w_down, final_norm_g)
    return (y_prompt, y_sample, gla_state_p, win_k_p, win_v_p, gla_state_s, new_k_s, new_v_s)


_drawn_inputs = setup_inputs


def setup_inputs(seed=0):
    import zlib

    import numpy as np

    out = dict(_drawn_inputs(seed))
    spreads = {}
    factors = {'cache_win_k': 3.79,
     'cache_win_v': 3.056,
     'gla_norm_g': 38.232,
     'rel_bias': 3.68,
     'final_norm_g': 7.814,
     'norm2_g': 4.261}
    for name, (base, spread) in spreads.items():
        noise = np.random.default_rng([zlib.crc32(name.encode()), seed]).standard_normal(out[name].shape)
        drawn = base * np.exp(spread * noise) if base else spread * noise
        out[name] = __import__('jax').numpy.asarray(drawn.astype(out[name].dtype))
    for name, factor in factors.items():
        out[name] = (out[name] * factor).astype(out[name].dtype)
    return out
```

```python
import concourse.bass as bass
from concourse import mybir
from contextlib import ExitStack

F32 = mybir.dt.float32
I32 = mybir.dt.int32
U32 = mybir.dt.uint32
ALU = mybir.AluOpType
ACT = mybir.ActivationFunctionType
AX_X = mybir.AxisListType.X

P = 128
D = 1024
KC = D // P
S = 1024
NB = 8
PT = S // P
NT = PT + 1
TOK = S + NB
HA, DK, DV = 4, 32, 64
RANK = 16
HD, DH = 12, 64
PAIRS = HD // 2
GW = 2 * HA * DK + 2 * HA * DV + RANK
QW = HD * DH
NE, NG, PG = 16, 4, 4
FF = 512
MT = (2 * TOK - NE) // P + NE
SLOTS = MT * P
EPS = 1e-6
X_LOADS = ((NT + 1) // 2, NT // 2)
GN = S + P - 1
CK = 256
NEG = -1e30

_cols = {}
_at = 0
for _name, _w in (("ident", P), ("ones", P), ("cum_mid", P), ("cum", P), ("cum_rest", P), ("strict", P),
                  ("blk", HA * DV), ("oh", GN), ("ohs", CK + 1), ("seq8", NB), ("diag8", NB * HD),
                  ("eprio", NE), ("gprio", NG), ("thr", NT), ("before", NE * NE), ("tile", MT), ("srows", 1), ("tokid", NT),
                  ("eps", 1), ("one", 1)):
    _cols[_name] = (_at, _w)
    _at += _w
CONST_COLS = _at

A_CONST = 0
A_SMALL = (CONST_COLS + 31) // 32 * 32
A_MOD = A_SMALL + 2048
A_G2 = A_MOD + 6 * D
A_F = A_G2 + D
A_HT = A_F
A_X1 = A_F
A_MIX = A_F + NT * D
A_T = A_MIX + KC * TOK
ARENA = 53120
A_MOE = A_MIX


class Steps:

    def __init__(self, eng, sem):
        self.eng, self.sem, self.n, self.at, self.turn, self.per = eng, sem, 0, 0, None, 0

    def value(self):
        return self.n if self.turn is None else self.turn * self.per + self.n

    def done(self, ins, wait=True):
        ins.then_inc(self.sem, 1)
        self.n += 1
        if wait:
            self.eng.wait_ge(self.sem, self.value())

    def enter(self, turn, per):
        self.turn, self.per, self.at = turn, per, self.n

    def leave(self, turns):
        assert self.n - self.at == self.per, (self.n - self.at, self.per)
        self.turn = None
        self.n = self.at + turns * self.per


def build(nc, x_prompt, x_sample, state_gla, cache_win_k, cache_win_v, c_prompt, c_sample, w_ada, b_ada, norm1_g,
          norm2_g, w_in, w_gate_up, b_gate, gla_norm_g, w_o, rel_bias, router_w, router_b, moe_w_gate, moe_w_up,
          moe_w_down, final_norm_g, consts, y_prompt, y_sample, gla_state_p, win_k_p, win_v_p, gla_state_s,
          new_k_s, new_v_s):
    xp = x_prompt.rearrange("a s d -> (a s) d")
    xs = x_sample.rearrange("a s d -> (a s) d")
    yp = y_prompt.rearrange("a s d -> (a s) d")
    ys = y_sample.rearrange("a s d -> (a s) d")
    w_ada_v = w_ada.rearrange("l (k p) n -> p (l k) n", p=P)
    w_in_v = w_in.rearrange("l (k p) n -> p (l k) n", p=P)
    w_o_v = w_o.rearrange("l (k p) n -> p (l k) n", p=P)
    wg_flat = moe_w_gate.rearrange("l e d f -> (l e d) f")
    wu_flat = moe_w_up.rearrange("l e d f -> (l e d) f")
    wd_flat = moe_w_down.rearrange("l e f d -> (l e f) d")
    kp_v = win_k_p.rearrange("l b (t p) h d -> p (l b t) (h d)", p=P)
    vp_v = win_v_p.rearrange("l b (t p) h d -> p (l b t) (h d)", p=P)
    ck = cache_win_k.rearrange("l b s h d -> (l b) s (h d)")
    cv = cache_win_v.rearrange("l b s h d -> (l b) s (h d)")
    sgla = state_gla.rearrange("l b h k v -> (h k) (l b) v")
    sgla_out = gla_state_s.rearrange("l b h k v -> (h k) (l b) v")

    dist_bias = nc.dram_tensor("dist_bias", [HD * GN], F32, kind="Internal").ap()
    h2_rows = nc.dram_tensor("h2_rows", [TOK, D], F32, kind="Internal").ap()
    slot_token = nc.dram_tensor("slot_token", [SLOTS, 1], U32, kind="Internal").ap()
    slot_rows = nc.dram_tensor("slot_rows", [SLOTS, D], F32, kind="Internal").ap()

    with ExitStack() as ctx:
        def sem(name):
            return ctx.enter_context(nc.semaphore(name))

        arena = ctx.enter_context(nc.sbuf_tensor("arena", [P, ARENA], F32))
        banks = ctx.enter_context(nc.psum_tensor("banks", [P, 8 * 512], F32))
        ids = ctx.enter_context(nc.sbuf_tensor("ids", [P, 2 * NT + NT + 2], U32))
        etab = ctx.enter_context(nc.sbuf_tensor("etab", [1, MT], I32))
        gidx = ctx.enter_context(nc.sbuf_tensor("gidx", [P, 2], U32))

        def V(off, cols, rows=P):
            return arena[0:rows, off:off + cols]

        def C(name, rows=P):
            o, w = _cols[name]
            return V(A_CONST + o, w, rows)

        def bank(b, cols=512, rows=P, n=1):
            return banks[0:rows, 512 * b:512 * b + cols]

        _s = [A_SMALL]

        def small(cols):
            _s[0] += cols
            assert _s[0] <= A_MOD
            return _s[0] - cols

        ident = C("ident")
        o_relx = small(HD)
        o_relr = small(NB * HD)
        o_sbias = small(CK + 1)
        o_gng = small(HA * DV)
        o_csT = small(KC * 33)
        o_ss = small(NT * HA)
        o_rs = small(NT * HA)
        o_den = small(2 * PT)
        o_rden = small(2 * PT)
        o_mx = small(2)
        o_nmx = small(2)
        o_w12 = small(2 * NT)
        o_wgu = small(HA * DK)
        o_stat = small(4)
        o_rb = small(NE)
        relx, relr, sbias = V(o_relx, HD, 33), V(o_relr, NB * HD, 33), V(o_sbias, CK + 1, NB * HD)
        gng = V(o_gng, HA * DV)
        csT = V(o_csT, KC * 33).rearrange("p (k m) -> p k m", k=KC)
        ss, rs = V(o_ss, NT * HA), V(o_rs, NT * HA)
        den, mx, nmx = V(o_den, 2 * PT), V(o_mx, 2), V(o_nmx, 2)
        rden = V(o_rden, 2 * PT)
        w12 = V(o_w12, 2 * NT)
        mod = V(A_MOD, 6 * D, 33)
        SH1, SC1, G1, SH2, SC2, G2 = range(6)
        hT = V(A_HT, KC * TOK).rearrange("p (k n) -> p k n", k=KC)
        mixT = V(A_MIX, KC * TOK).rearrange("p (k n) -> p k n", k=KC)

        def modrow(i, rows=33):
            return mod[0:rows, i * D:(i + 1) * D]

        def rows_of(t):
            return P if t < PT else NB

        crow = V(A_T, D, 33)
        csig = V(A_T + D, D, 33)
        wa = [V(A_T + 2 * D + s * 4096, 4096).rearrange("p (k n) -> p k n", k=KC) for s in range(3)]
        ba = [V(A_T + 2 * D + 3 * 4096 + s * 512, 512, 33) for s in range(3)]
        nrm = V(A_T + 2 * D + 3 * 4096 + 1536, 2 * D, 33)
        o_x = A_T + 2 * D + 3 * 4096 + 1536 + 2 * D
        xt = [V(o_x + s * D, D) for s in range(2)]
        bias_rows = V(A_MIX, GN, HD)
        bcA1, bcS1, sqj = V(A_MIX + 2 * D, D), V(A_MIX + 3 * D, D), V(A_MIX + 4 * D, D)

        wG = V(A_T, KC * GW).rearrange("p (k n) -> p k n", k=KC)
        proj = V(A_T + KC * GW, NT * GW).rearrange("p (t n) -> p t n", t=NT)
        g0 = A_T + KC * GW + NT * GW
        o_T1, o_L, o_E = g0, g0 + D, g0 + 2 * D
        T1, L = V(o_T1, D), V(o_L, D)
        E = [V(o_E + i * D, D) for i in range(4)]
        k2T, q4T = V(g0 + 6 * D, D), V(g0 + 7 * D, D)
        attS = [V(g0 + 8 * D + s * 512, 512) for s in range(2)]
        state = [V(g0 + 9 * D + s * 256, 256) for s in range(2)]
        dstate = V(g0 + 9 * D + 512, 256)
        g1 = g0 + 9 * D + 768
        o_sc3 = g1
        sS = V(A_CONST + _cols["oh"][0], NB * DV).rearrange("p (b v) -> p b v", b=NB)
        sc3 = V(o_sc3, 3 * NB)
        eblast = V(g1 + 24, PT)
        assert g1 + 32 <= ARENA, (g1, ARENA)
        oG = V(A_T, NT * 256).rearrange("p (t n) -> p t n", t=NT)
        tG = V(A_T + NT * 256, NT * 256).rearrange("p (t n) -> p t n", t=NT)
        blkq = [V(A_T + 2 * NT * 256 + s * 512, 512) for s in range(2)]
        qz = V(A_T + 2 * NT * 256 + 1024, HA * NB * NB)
        o_st = A_T + 2 * NT * 256 + 1024 + HA * NB * NB
        sT1, sL, sA = V(o_st, P, NB), V(o_st + P, P, NB), V(o_st + 2 * P, P, NB)
        kz = V(o_T1, NB * P, NB).rearrange("q (b n) -> q b n", b=NB)
        glT = V(A_MIX, TOK, 32)

        a0 = A_T
        wP = V(a0, KC * 384).rearrange("p (k g n) -> p k g n", k=KC, g=3); a0 += KC * 384
        qkv = V(a0, NT * 384).rearrange("p (t n) -> p t n", t=NT); a0 += NT * 384
        qT, kT = V(a0, D), V(a0 + D, D); a0 += 2 * D
        strip = V(a0, 2 * D).rearrange("p (h n) -> p h n", h=2); a0 += 2 * D
        sB = [V(a0 + s * D, D) for s in range(2)]; a0 += 2 * D
        pB = [V(a0 + s * D, D) for s in range(2)]; a0 += 2 * D
        pTB = [V(a0 + s * D, D) for s in range(2)]; a0 += 2 * D
        oB = V(a0, D).rearrange("p (t n) -> p t n", t=PT); a0 += D
        sq = V(a0, 3 * QW, NB).rearrange("p (g n) -> p g n", g=3); a0 += 3 * QW
        assert a0 <= ARENA
        o_sa = A_T
        vC = [V(o_sa + b * 1536, 1536).rearrange("p (c n) -> p c n", c=2) for b in range(NB)]
        o_sb2 = o_sa + NB * 1536
        kCb = [V(o_sb2 + s * 1536, 1536).rearrange("p (c n) -> p c n", c=2) for s in range(2)]
        prod = V(o_sb2 + 3072, 1536)
        assert o_sb2 + 3072 + 1536 <= a0 - 3 * QW
        o_sc = A_HT
        ohb = V(o_sc, NB * P, NB).rearrange("q (b n) -> q b n", b=NB)
        lg = V(o_sc + 1024, 192).rearrange("p (c n) -> p c n", c=2)
        selfp = V(o_sc + 1216, QW, NB)
        selfl = V(o_sc + 1984, HD, NB)
        selfd = V(o_sc + 1996, NB * HD, NB)
        srow = V(o_sc + 2092, CK + 1, NB * HD)
        spT = V(o_sc + 2349, 192).rearrange("p (c n) -> p c n", c=2)
        pself = V(o_sc + 2541, NB, NB * HD)
        pselfT = V(o_sc + 2549, NB * HD, NB)

        a1 = A_T
        wO = V(a1, KC * D).rearrange("p (k n) -> p k n", k=KC); a1 += KC * D
        xr = [V(a1 + s * D, D) for s in range(2)]; a1 += 2 * D
        h2 = [V(a1 + s * D, D) for s in range(2)]; a1 += 2 * D
        h2T = V(a1, D).rearrange("p (k n) -> p k n", k=KC); a1 += D
        rw = V(a1, KC * NE).rearrange("p (k n) -> p k n", k=KC); a1 += KC * NE
        bcG1, bcA2, bcS2 = (V(a1 + i * D, D) for i in range(3)); a1 += 3 * D
        sqj2 = V(a1, D); a1 += D

        def R(cols):
            nonlocal a1
            a1 += cols
            assert a1 <= ARENA
            return V(a1 - cols, cols)
        RE = NT * NE
        sco, sel, msel, tA, tB, one1, one2, both = (R(RE) for _ in range(8))
        pair6 = R(NT * NG * 6)
        gsc, gsel, gm = R(NT * NG), R(NT * NG), R(NT)
        rank, cnt, base = R(RE), R(RE), R(RE)
        nE, tE, offE = R(NE), R(NE), R(NE)
        cmp9, cmpE = R(NE * NT), R(NE * NE)
        slotf = R(2 * NT)
        s12 = R(2 * NT)
        etf, ecmp = R(MT), R(MT * NE)
        zero_i = R(SLOTS // P)
        X1 = V(A_X1, NT * D).rearrange("p (t n) -> p t n", t=NT)
        g2b = V(A_G2, D)

        m0 = A_MOE
        mwg, mwu, mwd = [], [], []
        for s in range(2):
            mwg.append(V(m0, KC * FF).rearrange("p (k n) -> p k n", k=KC)); m0 += KC * FF
            mwu.append(V(m0, KC * FF).rearrange("p (k n) -> p k n", k=KC)); m0 += KC * FF
            mwd.append(V(m0, 4 * D).rearrange("p (k n) -> p k n", k=4)); m0 += 4 * D
        xg = [V(m0 + s * D, D) for s in range(2)]; m0 += 2 * D
        xgT = V(m0, D).rearrange("p (k n) -> p k n", k=KC); m0 += D
        sg, hidT = V(m0, FF), V(m0 + FF, FF).rearrange("p (k n) -> p k n", k=4); m0 += 2 * FF
        hid = V(m0, FF); m0 += FF
        yM = [V(m0 + s * D, D) for s in range(2)]; m0 += 2 * D
        assert m0 <= ARENA, m0
        c0 = A_MOE
        yA = [V(c0 + s * D, D) for s in range(2)]
        yB = [V(c0 + (2 + s) * D, D) for s in range(2)]
        fng = V(c0 + 4 * D, D)
        sqj3 = V(c0 + 5 * D, D)

        const_in = sem("const_in"); crow_in = sem("crow_in"); vec_in = sem("vec_in")
        cleared = sem("cleared"); neg_exp_c = sem("neg_exp_c"); silu_c = sem("silu_c"); csT_ps = sem("csT_ps")
        csT_ok = sem("csT_ok"); ada_in = [sem(f"ada_in{s}") for s in range(3)]; ada_ps = sem("ada_ps")
        ada_added = sem("ada_added"); mod_ok = sem("mod_ok"); bc1_ok = sem("bc1_ok"); bc2_ok = sem("bc2_ok")
        bias_ps = sem("bias_ps"); bias_ok = sem("bias_ok")
        x_in = [sem(f"x_in{s}") for s in range(2)]; x_ssq = sem("x_ssq"); h_ok = sem("h_ok"); hT_ps = sem("hT_ps")
        hT_ok = sem("hT_ok"); act_link = sem("act_link"); dve_link = sem("dve_link"); pool_link = sem("pool_link")
        wG_in = sem("wG_in"); gproj_ps = sem("gproj_ps"); gprojA = sem("gprojA"); gprojB = sem("gprojB")
        gl_ps = sem("gl_ps"); gl_ok = sem("gl_ok"); z_ps = sem("z_ps"); lnz_ok = sem("lnz_ok"); loga_ok = sem("loga_ok")
        cum_ps = sem("cum_ps"); edec_ok = sem("edec_ok"); scaled_ok = sem("scaled_ok"); gT_ps = sem("gT_ps")
        k2T_ok = sem("k2T_ok"); q4T_ok = sem("q4T_ok"); blk_ok = sem("blk_ok"); att_ps = sem("att_ps")
        att_cp = sem("att_cp"); att_ok = sem("att_ok"); og_ps = sem("og_ps"); ds_ps = sem("ds_ps")
        state_ok = sem("state_ok"); og_cp = sem("og_cp"); gout = sem("gout")
        sc3_ps = sem("sc3_ps"); sc3_ok = sem("sc3_ok"); kv_ps = sem("kv_ps"); snew_ok = sem("snew_ok")
        so_ps = sem("so_ps"); osq_ok = sem("osq_ok"); ossq_ok = sem("ossq_ok"); ostd_ok = sem("ostd_ok")
        rexp_ok = sem("rexp_ok"); og_ok = sem("og_ok"); ogT_ps = sem("ogT_ps"); ogT_ok = sem("ogT_ok")
        wP_in = sem("wP_in"); strip_in = sem("strip_in"); pair_dve = sem("pair_dve"); pair_act = sem("pair_act")
        qkv_ps = sem("qkv_ps"); qkv_ok = sem("qkv_ok"); kv_out = sem("kv_out"); sq_ok = sem("sq_ok")
        qkT_ps = sem("qkT_ps"); qT_ok = sem("qT_ok"); kT_ok = sem("kT_ok"); s_ps = sem("s_ps"); s_read = sem("s_read")
        m_ok = sem("m_ok"); p_ok = sem("p_ok"); pt_ps = sem("pt_ps"); pt0_ok = sem("pt0_ok"); pt1_ok = sem("pt1_ok")
        o_ps = sem("o_ps"); o_ok = sem("o_ok"); oT_ps = sem("oT_ps"); wP_free = sem("wP_free")
        kc_in = [sem(f"kc_in{s}") for s in range(2)]; vc_in = sem("vc_in")
        ohb_ok = sem("ohb_ok"); qb_ps = sem("qb_ps"); slog_ok = sem("slog_ok"); sprod = sem("sprod")
        selfd_ok = sem("selfd_ok"); slT_ps = sem("slT_ps"); smax_ok = sem("smax_ok"); sexp_ok = sem("sexp_ok")
        sp_ok = sem("sp_ok"); spT_ps = sem("spT_ps"); spT_ok = sem("spT_ok"); sov_ps = sem("sov_ps")
        smix_ok = sem("smix_ok")
        wO_in = sem("wO_in")
        op_ps = sem("op_ps"); x1_ok = sem("x1_ok"); x1_std = sem("x1_std"); h2_ok = sem("h2_ok")
        h2_out = [sem(f"h2_out{s}") for s in range(2)]; h2T_ps = sem("h2T_ps"); h2T_ok = sem("h2T_ok"); lr_ps = sem("lr_ps")
        rexp2 = sem("rexp2"); both_ok = sem("both_ok"); rank_ps = sem("rank_ps"); route_ok = sem("route_ok")
        zero_ok = sem("zero_ok"); st_zero = sem("st_zero"); st_out = sem("st_out")
        gi_in = [sem(f"gi_in{s}") for s in range(2)]; xg_in = [sem(f"xg_in{s}") for s in range(2)]
        mgu_in = [sem(f"mgu_in{s}") for s in range(2)]; md_in = [sem(f"md_in{s}") for s in range(2)]
        xgT_ps = sem("xgT_ps"); xgT_ok = sem("xgT_ok"); g_ps = sem("g_ps"); u_ps = sem("u_ps")
        gexp_ok = sem("gexp_ok"); hid_ok = sem("hid_ok"); hidT_ps = sem("hidT_ps"); hidT_ok = sem("hidT_ok")
        y_ps = sem("y_ps"); yA_cp = sem("yA_cp"); yB_cp = sem("yB_cp"); yrow_out = [sem(f"yrow_out{s}") for s in range(2)]
        ya_in = [sem(f"ya_in{s}") for s in range(2)]; x2_ok = sem("x2_ok"); x2_std = sem("x2_std")
        y_ok = sem("y_ok"); y_out = [sem(f"y_out{s}") for s in range(2)]
        stage_done = [sem(f"stage_done{i}") for i in range(6)]

        block = ctx.enter_context(nc.Block())

        def stage_end(eng, i):
            eng.drain().then_inc(stage_done[i], 1)
            eng.wait_ge(stage_done[i], 5)

        @block.sync
        def _(sp):
            sp.dma_start(V(A_CONST, CONST_COLS), consts).then_inc(const_in, 16)
            sp.wait_ge(cleared, 3)
            sp.dma_start(crow[0:NB], c_sample).then_inc(crow_in, 16)
            sp.dma_start(crow[32:33], c_prompt).then_inc(crow_in, 16)
            sp.dma_start(relx[0:32], rel_bias).then_inc(crow_in, 16)

            def load_ada(j, s):
                sp.dma_start(wa[s], w_ada_v[:, :, bass.ds(j * 512, 512)]).then_inc(ada_in[s], 16)
                sp.dma_start(ba[s], b_ada[0:1, bass.ds(j * 512, 512)].partition_broadcast(33)).then_inc(ada_in[s], 16)
            for s in range(3):
                load_ada(s, s)
            sp.dma_start(nrm[:, 0:D], norm1_g[0:1, :].partition_broadcast(33)).then_inc(vec_in, 16)
            sp.dma_start(nrm[:, D:2 * D], norm2_g[0:1, :].partition_broadcast(33)).then_inc(vec_in, 16)
            sp.dma_start(gng, gla_norm_g[0:1, :].partition_broadcast(P)).then_inc(vec_in, 16)
            sp.dma_start(V(o_wgu, P, RANK), w_gate_up[0]).then_inc(vec_in, 16)
            sp.dma_start(arena[RANK:RANK + 1, o_wgu:o_wgu + P], b_gate[0:1, :]).then_inc(vec_in, 16)
            rb_v = router_b.rearrange("(a n) -> a n", a=1)
            sp.dma_start(V(o_rb, NE), rb_v.partition_broadcast(P)).then_inc(vec_in, 16)
            with sp.Fori(0, 3) as i:
                for s in range(3):
                    sp.wait_ge(ada_added, i * 3 + (s + 1))
                    sp.nop(nofuse=True)
                    load_ada(i * 3 + (s + 3), s)
            for t in range(NT):
                if t >= 2:
                    sp.wait_ge(hT_ps, t - 1)
                sp.dma_start(xt[t % 2][0:rows_of(t)], xp[t * P:(t + 1) * P] if t < PT else xs).then_inc(x_in[t % 2], 16)
            sp.wait_ge(bias_ok, 3)
            sp.dma_start(dist_bias.rearrange("(h n) -> h n", h=HD), bias_rows).then_inc(gout, 16)
            sp.wait_ge(gout, 16)
            stage_end(sp, 0)

            sp.dma_start(wG, w_in_v[:, :, 0:GW]).then_inc(wG_in, 16)
            sp.dma_start(sS, sgla).then_inc(wG_in, 16)
            sp.wait_ge(state_ok, 1 + PT)
            for h in range(HA):
                sp.dma_start(gla_state_p[0, 0, h], state[PT % 2][32 * h:32 * h + 32, DV * h:DV * h + DV]).then_inc(gout, 16)
            sp.wait_ge(snew_ok, 5)
            sp.dma_start(sgla_out, sS).then_inc(gout, 16)
            sp.wait_ge(gout, 16 * (HA + 2))
            stage_end(sp, 1)

            w_pair = w_in_v[:, :, GW:GW + 3 * QW].rearrange("p k (g n) -> p k g n", g=3)
            nc.sync.sem_inc(kv_out, 16)
            with sp.Fori(0, PAIRS) as c:
                sp.wait_ge(wP_free, c + 1)
                sp.nop(nofuse=True)
                sp.dma_start(wP[:, :, 0], w_pair[:, :, 0, bass.ds(c * P, P)]).then_inc(wP_in, 16)
                sp.dma_start(wP[:, :, 1], w_pair[:, :, 1, bass.ds(c * P, P)]).then_inc(wP_in, 16)
                sp.dma_start(wP[:, :, 2], w_pair[:, :, 2, bass.ds(c * P, P)]).then_inc(wP_in, 16)
                sp.wait_ge(pair_dve, c + 1)
                sp.nop(nofuse=True)
                for hh in range(2):
                    v = dist_bias[bass.ds(c * (2 * GN) + hh * GN, D)]
                    sp.dma_start(strip[:, hh], bass.AP(tensor=v.tensor, offset=v.offset, ap=[[1, P], [1, D]]))\
                      .then_inc(strip_in, 16)
                sp.wait_ge(qkv_ok, c * NT + NT)
                sp.nop(nofuse=True)
                sp.dma_start(kp_v[:, :, bass.ds(c * P, P)], qkv[:, 0:PT, 128:256]).then_inc(kv_out, 16)
                sp.dma_start(vp_v[:, :, bass.ds(c * P, P)], qkv[:, 0:PT, 256:384]).then_inc(kv_out, 16)
            sp.wait_ge(kv_out, 32 * PAIRS + 16)
            sp.wait_ge(sq_ok, PAIRS)
            sp.dma_start(new_k_s.rearrange("l b s h d -> (l b s) (h d)"), sq[:, 1]).then_inc(kv_out, 16)
            sp.dma_start(new_v_s.rearrange("l b s h d -> (l b s) (h d)"), sq[:, 2]).then_inc(kv_out, 16)
            stage_end(sp, 2)

            def load_cache(dst, src, b, s_in):
                sp.dma_start(dst[:, 0], src[b, 896:1024]).then_inc(s_in, 16)
                sp.dma_start(dst[0:96, 1], src[b, 512:896].rearrange("(n r) d -> n r d", r=4)[:, 0]).then_inc(s_in, 16)
                sp.dma_start(dst[96:128, 1], src[b, 0:512].rearrange("(n r) d -> n r d", r=16)[:, 0]).then_inc(s_in, 16)
            for b in range(NB):
                if b >= 2:
                    sp.wait_ge(sprod, b - 1)
                load_cache(kCb[b % 2], ck, b, kc_in[b % 2])
            for b in range(NB):
                load_cache(vC[b], cv, b, vc_in)
            sp.wait_ge(kv_out, 32 * PAIRS + 48)
            stage_end(sp, 3)

            sp.dma_start(wO, w_o_v).then_inc(wO_in, 16)
            sp.dma_start(rw, router_w.rearrange("(k p) n -> p k n", p=P)).then_inc(wO_in, 16)
            for t in range(NT):
                if t >= 2:
                    sp.wait_ge(x1_ok, t - 1)
                sp.dma_start(xr[t % 2][0:rows_of(t)], xp[t * P:(t + 1) * P] if t < PT else xs).then_inc(x_in[t % 2], 16)
                if t >= 1:
                    sp.wait_ge(h2_ok, t)
                    sp.dma_start(h2_rows[(t - 1) * P:t * P], h2[(t - 1) % 2]).then_inc(h2_out[(t - 1) % 2], 16)
            sp.wait_ge(h2_ok, NT)
            sp.dma_start(h2_rows[S:TOK], h2[PT % 2][0:NB]).then_inc(h2_out[PT % 2], 16)
            sp.wait_ge(zero_ok, 1)
            sp.dma_start(slot_token.rearrange("(p n) a -> p (n a)", p=P), zero_i.bitcast(U32)).then_inc(st_zero, 16)
            sp.wait_ge(h2_out[0], 16 * ((NT + 1) // 2))
            sp.wait_ge(h2_out[1], 16 * (NT // 2))
            sp.wait_ge(st_zero, 16)
            stage_end(sp, 4)

            with sp.Fori(0, MT // 2) as i:
                for s in range(2):
                    sp.wait_ge(u_ps, i * 2 + (s + 1))
                    sp.nop(nofuse=True)
                    e = sp.value_load(etab[0:1, bass.ds(i * 2 + s, 1)], min_val=0, max_val=NE - 1)
                    sp.dma_start(mwg[s], wg_flat[bass.ds(e * D, D), :].rearrange("(k p) n -> p k n", p=P)).then_inc(mgu_in[s], 16)
                    sp.dma_start(mwu[s], wu_flat[bass.ds(e * D, D), :].rearrange("(k p) n -> p k n", p=P)).then_inc(mgu_in[s], 16)
                    sp.wait_ge(y_ps, i * 2 + (s + 1))
                    sp.nop(nofuse=True)
                    sp.dma_start(mwd[s], wd_flat[bass.ds(e * FF, FF), :].rearrange("(k p) n -> p k n", p=P)).then_inc(md_in[s], 16)
            stage_end(sp, 5)
            sp.dma_start(fng, final_norm_g.rearrange("(a n) -> a n", a=1).partition_broadcast(P)).then_inc(vec_in, 16)
            for t in range(NT):
                sp.wait_ge(y_ok, t + 1)
                sp.dma_start(yp[t * P:(t + 1) * P] if t < PT else ys, yA[t % 2][0:rows_of(t)]).then_inc(y_out[t % 2], 16)
            sp.wait_ge(y_out[0], 16 * ((NT + 1) // 2))
            sp.wait_ge(y_out[1], 16 * (NT // 2))

        @block.gpsimd
        def _(pool):
            pl = Steps(pool, pool_link)
            bc = Steps(pool, bc1_ok)
            pool.wait_ge(mod_ok, 2)
            bc.done(nc.gpsimd.partition_broadcast(bcA1, modrow(SC1)[32:33]), wait=False)
            bc.done(nc.gpsimd.partition_broadcast(bcS1, modrow(SH1)[32:33]), wait=False)
            stage_end(pool, 0)
            for t in range(PT):
                pool.wait_ge(att_cp, t + 1)
                v = attS[t % 2].rearrange("p (h n) -> p h n", h=HA)
                nc.gpsimd.affine_select(out=v, in_=v, pattern=[[0, HA], [1, P]], compare_op=ALU.is_ge, fill=0.0,
                                        base=0, channel_multiplier=-1).then_inc(att_ok, 1)
            stage_end(pool, 1)
            stage_end(pool, 2)
            stage_end(pool, 3)
            b2 = Steps(pool, bc2_ok)
            b2.done(nc.gpsimd.partition_broadcast(bcG1, modrow(G1)[32:33]), wait=False)
            b2.done(nc.gpsimd.partition_broadcast(bcA2, modrow(SC2)[32:33]), wait=False)
            b2.done(nc.gpsimd.partition_broadcast(bcS2, modrow(SH2)[32:33]), wait=False)
            b2.done(nc.gpsimd.partition_broadcast(g2b, modrow(G2)[32:33]), wait=False)
            nc.gpsimd.memset(zero_i, 0.0).then_inc(zero_ok, 1)
            pool.wait_ge(st_zero, 16)
            pool.wait_ge(route_ok, 1)
            for t in range(NT):
                n = rows_of(t)
                for j in range(2):
                    nc.gpsimd.indirect_dma_start(
                        slot_token, bass.IndirectOffsetOnAxis(ap=ids[0:n, 2 * t + j:2 * t + j + 1], axis=0),
                        ids[0:n, 2 * NT + t:2 * NT + t + 1], None).then_inc(st_out, 16)
            pool.wait_ge(st_out, 32 * NT)
            stage_end(pool, 4)
            with pool.Fori(0, MT // 2) as i:
                for s in range(2):
                    pool.wait_ge(xgT_ps, i * 2 + (s + 1))
                    pool.dma_start(gidx[:, s:s + 1], slot_token[bass.ds(i * (2 * P) + s * P, P), :]).then_inc(gi_in[s], 16)
                    pool.wait_ge(gi_in[s], i * 16 + 16)
                    pool.nop(nofuse=True)
                    nc.gpsimd.indirect_dma_start(
                        xg[s], None, h2_rows, bass.IndirectOffsetOnAxis(ap=gidx[:, s:s + 1], axis=0)).then_inc(xg_in[s], 16)
            stage_end(pool, 5)
            for t in range(NT):
                n = rows_of(t)
                if t >= 2:
                    pool.wait_ge(y_out[t % 2], 16 * (t // 2))
                for j, dst in ((0, yA), (1, yB)):
                    nc.gpsimd.indirect_dma_start(
                        dst[t % 2][0:n], None, slot_rows,
                        bass.IndirectOffsetOnAxis(ap=ids[0:n, 2 * t + j:2 * t + j + 1], axis=0)).then_inc(ya_in[t % 2], 16)

        @block.scalar
        def _(act):
            lk = Steps(act, act_link)
            A = nc.scalar.activation
            eps = C("eps")

            act.wait_ge(const_in, 16)
            act.wait_ge(crow_in, 48)
            A(csig, crow, ACT.Exp, scale=-1.0).then_inc(neg_exp_c, 1)
            act.wait_ge(csT_ps, 1)
            A(csT.rearrange("p k m -> p (k m)"), bank(7, KC * 33), ACT.Copy).then_inc(csT_ok, 1)
            for t in range(NT):
                n = rows_of(t)
                act.wait_ge(x_in[t % 2], 16 * (t // 2 + 1))
                lk.done(A(sqj[0:n], xt[t % 2][0:n], ACT.Square, accum_out=ss[0:n, t:t + 1]))
                A(rs[0:n, t:t + 1], ss[0:n, t:t + 1], ACT.Sqrt, scale=1.0 / D, bias=eps[0:n]).then_inc(x_ssq, 1)
                if t >= 1:
                    store_hT = t - 1
                    act.wait_ge(hT_ps, store_hT + 1)
                    b = 2 * (store_hT % 2)
                    A(hT[:, :, store_hT * P:store_hT * P + P], banks[:, 512 * b:512 * b + 1024].rearrange("p (k n) -> p k n", k=KC),
                      ACT.Copy).then_inc(hT_ok, 1)
            act.wait_ge(hT_ps, NT)
            A(hT[:, :, S:TOK], bank(2 * (PT % 2), KC * NB).rearrange("p (k n) -> p k n", k=KC), ACT.Copy).then_inc(hT_ok, 1)
            stage_end(act, 0)

            for t in range(NT):
                n = rows_of(t)
                act.wait_ge(gproj_ps, t + 1)
                A(proj[0:n, t, 0:512], bank(4 + 2 * (t % 2), 512, n), ACT.Copy).then_inc(gprojA, 1)
            act.wait_ge(z_ps, 1)
            z = banks[:, 0:D]
            lk.done(A(T1, z, ACT.Abs))
            lk.done(A(sT1, bank(2, P, NB), ACT.Abs))
            lk.done(A(T1, T1, ACT.Exp, scale=-1.0))
            lk.done(A(sT1, sT1, ACT.Exp, scale=-1.0))
            lk.done(A(T1, T1, ACT.Ln, bias=C("one")))
            A(sT1, sT1, ACT.Ln, bias=C("one", NB)).then_inc(lnz_ok, 1)
            act.wait_ge(cum_ps, 1)
            ed = Steps(act, edec_ok)
            ed.done(A(E[0], banks[:, 0:D], ACT.Exp), wait=False)
            ed.done(A(E[1], banks[:, 0:D], ACT.Exp, scale=-1.0), wait=False)
            ed.done(A(E[2], banks[:, 1024:1024 + D], ACT.Exp), wait=False)
            ed.done(A(E[3], banks[:, 2048:2048 + D], ACT.Exp), wait=False)
            ed.done(A(eblast, bank(6, PT), ACT.Exp), wait=False)
            ed.done(A(sA, sL, ACT.Exp), wait=False)
            act.wait_ge(gT_ps, 1)
            A(k2T, banks[:, 0:D], ACT.Copy).then_inc(k2T_ok, 1)
            for t in range(PT):
                act.wait_ge(att_ps, t + 1)
                if t >= 2:
                    act.wait_ge(og_ps, t - 1)
                A(attS[t % 2], bank(t % 2), ACT.Copy).then_inc(att_cp, 1)
                act.wait_ge(og_ps, t + 1)
                A(oG[:, t], bank(2 + t % 2, 256), ACT.Copy).then_inc(og_cp, 1)
            act.wait_ge(so_ps, 1)
            act.wait_ge(cleared, 5)
            A(oG[0:NB, PT], bank(0, 256, NB), ACT.Copy).then_inc(og_cp, 1)
            act.wait_ge(og_cp, NT)
            lk.done(A(tG.rearrange("p t n -> p (t n)"), oG.rearrange("p t n -> p (t n)"), ACT.Square))
            nc.scalar.sem_inc(osq_ok, 1)
            act.wait_ge(ossq_ok, 1)
            A(rs, ss, ACT.Sqrt, scale=1.0 / DV, bias=eps).then_inc(ostd_ok, 1)
            A(tG, proj[:, :, 528:784], ACT.Exp, scale=-1.0).then_inc(rexp_ok, 1)
            act.wait_ge(ogT_ps, 1)
            for c in range(2):
                lk.done(A(mixT[:, c, 0:S], banks[:, 1024 * c:1024 * c + D], ACT.Copy), wait=False)
                lk.done(A(mixT[:, c, S:TOK], bank(4 + c, NB), ACT.Copy), wait=False)
            stage_end(act, 1)

            nc.scalar.sem_inc(pair_act, 1)
            with act.Fori(0, PAIRS) as c:
                lk.enter(c, 1)
                for t in range(NT):
                    n = rows_of(t)
                    if t == 0:
                        act.wait_ge(kv_out, c * 32 + 16)
                        act.wait_ge(oT_ps, c + 1)
                    act.wait_ge(qkv_ps, c * NT + (t + 1))
                    A(qkv[0:n, t], bank(t % 4, 384, n), ACT.Copy).then_inc(qkv_ok, 1)
                act.wait_ge(qkv_ok, c * NT + NT)
                A(sq[:, :, bass.ds(c * P, P)], qkv[0:NB, PT].rearrange("p (g n) -> p g n", g=3), ACT.Copy).then_inc(sq_ok, 1)
                act.wait_ge(qkT_ps, c + 1)
                A(kT, banks[:, 512 * 6:512 * 8], ACT.Copy).then_inc(kT_ok, 1)

                def exp_tile(a):
                    i = a % PT
                    n = (i + 1) * P
                    act.wait_ge(m_ok, c * 16 + (a + 1))
                    if a >= 2:
                        act.wait_ge(pt_ps, c * 16 + (a - 1))
                    A(pB[a % 2][:, 0:n], sB[a % 2][:, 0:n], ACT.Exp, bias=nmx[:, a % 2:a % 2 + 1],
                      accum_out=den[:, a:a + 1]).then_inc(p_ok, 1)
                exp_tile(0)
                for a in range(16):
                    if a < 15:
                        exp_tile(a + 1)
                    n = min(a % PT + 1, 4) * P
                    act.wait_ge(pt_ps, c * 16 + (a + 1))
                    if a >= 2:
                        act.wait_ge(o_ps, c * 16 + (a - 1))
                    A(pTB[a % 2][:, 0:n], bank(4, n), ACT.Copy).then_inc(pt0_ok, 1)
                act.wait_ge(oT_ps, c + 2)
                lk.done(A(mixT[:, bass.ds(c + 2, 1), 0:512].rearrange("p a (t n) -> p (a t) n", t=4),
                          bank(4).rearrange("p (t n) -> p t n", t=4)[:, :, ::-1], ACT.Copy))
                nc.scalar.sem_inc(pair_act, 1)
                lk.leave(PAIRS)
            stage_end(act, 2)

            act.wait_ge(smax_ok, 1)
            A(srow, srow, ACT.Exp, bias=V(o_stat + 1, 1, NB * HD), accum_out=V(o_stat + 2, 1, NB * HD)).then_inc(sexp_ok, 1)
            act.wait_ge(spT_ps, 1)
            lk.done(A(spT.rearrange("p c n -> p (c n)"), bank(6, 192), ACT.Copy), wait=False)
            A(pselfT, bank(7, NB * HD, NB), ACT.Copy).then_inc(spT_ok, 1)
            stage_end(act, 3)

            for t in range(NT):
                n = rows_of(t)
                act.wait_ge(x1_ok, t + 1)
                lk.done(A(sqj2[0:n], X1[0:n, t], ACT.Square, accum_out=ss[0:n, t:t + 1]))
                A(rs[0:n, t:t + 1], ss[0:n, t:t + 1], ACT.Sqrt, scale=1.0 / D, bias=eps[0:n]).then_inc(x1_std, 1)
                act.wait_ge(h2T_ps, t + 1)
                if t >= 1:
                    act.wait_ge(lr_ps, t)
                w = n
                A(h2T[:, :, 0:w], banks[:, 2048:2048 + KC * w].rearrange("p (k n) -> p k n", k=KC), ACT.Copy).then_inc(h2T_ok, 1)
            act.wait_ge(lr_ps, NT)
            A(sco[:, 0:PT * NE], bank(6, PT * NE), ACT.Exp, scale=-1.0).then_inc(rexp2, 1)
            act.wait_ge(cleared, 6)
            A(sco[0:NB, PT * NE:RE], bank(7, NE, NB), ACT.Exp, scale=-1.0).then_inc(rexp2, 1)
            stage_end(act, 4)

            nc.scalar.sem_inc(yA_cp, 1)
            nc.scalar.sem_inc(yrow_out[0], 16)
            nc.scalar.sem_inc(yrow_out[1], 16)
            with act.Fori(0, MT // 2) as i:
                for s in range(2):
                    t1 = i * 2 + (s + 1)
                    act.wait_ge(xgT_ps, t1 + 2)
                    A(xgT.rearrange("p k n -> p (k n)"), banks[:, 0:D], ACT.Copy).then_inc(xgT_ok, 1)
                    act.wait_ge(g_ps, t1)
                    A(sg, bank(2), ACT.Exp, scale=-1.0).then_inc(gexp_ok, 1)
                    act.wait_ge(hidT_ps, t1 + 1)
                    A(hidT.rearrange("p k n -> p (k n)"), bank(4), ACT.Copy).then_inc(hidT_ok, 1)
                    act.wait_ge(y_ps, t1 + 2)
                    act.wait_ge(yrow_out[s], i * 16 + 16)
                    A(yM[s][:, 0:512], bank(5), ACT.Copy).then_inc(yA_cp, 1)
                    act.wait_ge(yA_cp, t1 + 1)
                    act.wait_ge(yB_cp, t1 + 1)
                    act.dma_start(slot_rows[bass.ds(i * (2 * P) + s * P, P), :], yM[s]).then_inc(yrow_out[s], 16)
            act.wait_ge(yrow_out[0], 16 * (MT // 2) + 16)
            act.wait_ge(yrow_out[1], 16 * (MT // 2) + 16)
            stage_end(act, 5)
            for t in range(NT):
                n = rows_of(t)
                act.wait_ge(x2_ok, t + 1)
                lk.done(A(sqj3[0:n], X1[0:n, t], ACT.Square, accum_out=ss[0:n, t:t + 1]))
                A(rs[0:n, t:t + 1], ss[0:n, t:t + 1], ACT.Sqrt, scale=1.0 / D, bias=eps[0:n]).then_inc(x2_std, 1)

        @block.vector
        def _(dve):
            v = nc.vector
            lk = Steps(dve, dve_link)
            cl = Steps(dve, cleared)
            cl.done(v.memset(crow, 0.0), wait=False)
            cl.done(v.memset(arena[32:33, o_relx:o_relx + HD], 1.0), wait=False)
            cl.done(v.memset(V(A_HT, TOK, 32), 0.0), wait=False)
            dve.wait_ge(neg_exp_c, 1)
            lk.done(v.tensor_scalar(csig, csig, 1.0, None, ALU.add))
            lk.done(v.reciprocal(csig, csig))
            v.tensor_tensor(crow, crow, csig, ALU.mult).then_inc(silu_c, 1)
            dve.wait_ge(crow_in, 48)
            bo = Steps(dve, bias_ok)
            v.tensor_copy(relr.rearrange("p (b h) -> p b h", b=NB), relx.unsqueeze(1).broadcast_to([33, NB, HD]))\
             .then_inc(bias_ps, 1)
            dve.wait_ge(bias_ps, 2)
            bo.done(v.tensor_copy(bias_rows[:, 0:D], banks[0:HD, 0:D]), wait=False)
            bo.done(v.tensor_copy(bias_rows[:, D:GN], banks[0:HD, D:GN]), wait=False)
            bo.done(v.tensor_copy(sbias, banks[0:NB * HD, 1536:1536 + CK + 1]), wait=False)
            ad = Steps(dve, ada_added)
            with dve.Fori(0, 4) as i:
                ad.enter(i, 3)
                for s in range(3):
                    dve.wait_ge(ada_ps, i * 3 + (s + 1))
                    ad.done(v.tensor_tensor(mod[:, bass.ds(i * 1536 + s * 512, 512)], bank(4 + s, 512, 33), ba[s], ALU.add), wait=False)
                ad.leave(4)
            dve.wait_ge(ada_added, 12)
            dve.wait_ge(vec_in, 96)
            mo = Steps(dve, mod_ok)
            mo.done(v.scalar_tensor_tensor(out=modrow(SC1), in0=modrow(SC1), scalar=1.0, in1=nrm[:, 0:D], op0=ALU.add, op1=ALU.mult))
            mo.done(v.scalar_tensor_tensor(out=modrow(SC2), in0=modrow(SC2), scalar=1.0, in1=nrm[:, D:2 * D], op0=ALU.add, op1=ALU.mult))
            for t in range(NT):
                n = rows_of(t)
                x = xt[t % 2][0:n]
                dve.wait_ge(x_ssq, t + 1)
                lk.done(v.reciprocal(rs[0:n, t:t + 1], rs[0:n, t:t + 1]))
                if t == 0:
                    dve.wait_ge(bc1_ok, 2)
                ga, sh = (bcA1, bcS1) if t < PT else (modrow(SC1, NB), modrow(SH1, NB))
                lk.done(v.scalar_tensor_tensor(out=x, in0=x, scalar=rs[0:n, t:t + 1], in1=ga, op0=ALU.mult, op1=ALU.mult))
                v.tensor_tensor(x, x, sh, ALU.add).then_inc(h_ok, 1)
            stage_end(dve, 0)

            cl.done(v.memset(proj[:, PT], 0.0), wait=False)
            lk.done(v.memset(glT, 1.0), wait=False)
            lk.done(v.memset(state[0], 0.0), wait=False)
            dve.wait_ge(cleared, 4)
            for t in range(NT):
                n = rows_of(t)
                dve.wait_ge(gproj_ps, t + 1)
                v.tensor_copy(proj[0:n, t, 512:GW], bank(5 + 2 * (t % 2), GW - 512, n)).then_inc(gprojB, 1)
            lk.done(v.memset(blkq[0], 0.0), wait=False)
            lk.done(v.memset(blkq[1], 0.0), wait=False)
            lk.done(v.memset(qz, 0.0), wait=False)
            cl.done(v.memset(oG[:, PT], 0.0), wait=False)
            dve.wait_ge(gl_ps, 1)
            dve.wait_ge(dve_link, lk.n)
            lk.done(v.tensor_copy(glT[0:RANK, 0:S], banks[0:RANK, 0:S]), wait=False)
            v.tensor_copy(glT[0:RANK, S:TOK], bank(2, NB, RANK)).then_inc(gl_ok, 1)
            dve.wait_ge(gl_ok, 1)
            dve.wait_ge(dve_link, lk.n)
            nc.vector.sem_inc(gl_ok, 1)
            dve.wait_ge(lnz_ok, 1)
            lk.done(v.tensor_scalar(L, banks[:, 0:D], 0.0, 1.0 / 16, ALU.min, ALU.mult), wait=False)
            lk.done(v.tensor_scalar(sL, bank(2, P, NB), 0.0, 1.0 / 16, ALU.min, ALU.mult))
            lo = Steps(dve, loga_ok)
            lo.done(v.scalar_tensor_tensor(out=L, in0=T1, scalar=-1.0 / 16, in1=L, op0=ALU.mult, op1=ALU.add))
            lo.done(v.scalar_tensor_tensor(out=sL, in0=sT1, scalar=-1.0 / 16, in1=sL, op0=ALU.mult, op1=ALU.add))
            E3 = [e.rearrange("p (t n) -> p t n", t=PT) for e in E]
            qv, kv = proj[:, 0:PT, 0:P], proj[:, 0:PT, P:2 * P]
            so = Steps(dve, scaled_ok)
            for n_, (e, src, is_q) in enumerate(((0, qv, 1), (1, kv, 0), (2, kv, 0), (3, qv, 1))):
                dve.wait_ge(edec_ok, e + 1)
                if is_q:
                    so.done(v.scalar_tensor_tensor(out=E3[e], in0=src, scalar=DK ** -0.5, in1=E3[e], op0=ALU.mult, op1=ALU.mult), wait=False)
                else:
                    so.done(v.tensor_tensor(E3[e], src, E3[e], ALU.mult), wait=False)
            dve.wait_ge(gT_ps, 1)
            v.tensor_copy(q4T, banks[:, 1024:1024 + D]).then_inc(q4T_ok, 1)
            nc.vector.sem_inc(state_ok, 1)
            dve.wait_ge(edec_ok, 5)
            for t in range(PT):
                if t >= 2:
                    dve.wait_ge(att_ps, t - 1)
                for h in range(HA):
                    lk.done(v.tensor_copy(blkq[t % 2][32 * h:32 * h + 32, P * h:P * h + P],
                                          banks[32 * h:32 * h + 32, 2048 + t * P:2048 + t * P + P]), wait=False)
                dve.wait_ge(dve_link, lk.n)
                nc.vector.sem_inc(blk_ok, 1)
                dve.wait_ge(ds_ps, t + 1)
                lk.done(v.tensor_tensor(dstate, bank(7, 256), C("blk"), ALU.mult))
                if t >= 1:
                    dve.wait_ge(og_ps, t)
                v.scalar_tensor_tensor(out=state[(t + 1) % 2], in0=state[t % 2], scalar=eblast[:, t:t + 1], in1=dstate,
                                       op0=ALU.mult, op1=ALU.add).then_inc(state_ok, 1)
                dve.wait_ge(state_ok, t + 2)
            dve.wait_ge(sc3_ps, 1)
            v.tensor_copy(sc3, bank(0, 3 * NB)).then_inc(sc3_ok, 1)
            dve.wait_ge(sc3_ok, 1)
            lk.done(v.tensor_tensor(kz, proj[0:NB, PT, P:2 * P].unsqueeze(1).broadcast_to([NB, NB, P]),
                                    ident[0:NB, 0:NB].unsqueeze(2).broadcast_to([NB, NB, P]), ALU.mult))
            qzv = qz.rearrange("p (h n) -> p h n", h=HA)
            for h in range(HA):
                lk.done(v.tensor_scalar(qzv[32 * h:32 * h + 32, h, 0:64:9], sc3[32 * h:32 * h + 32, 2 * NB:3 * NB], DK ** -0.5, None, ALU.mult))
            nc.vector.sem_inc(sc3_ok, 1)
            dve.wait_ge(wG_in, 32)
            sn = Steps(dve, snew_ok)
            sn.done(v.tensor_tensor(sS, sS, sc3[:, 0:NB].unsqueeze(2).broadcast_to([P, NB, DV]), ALU.mult))
            dve.wait_ge(kv_ps, 1)
            kvp = banks[:, 2048:4096].rearrange("p (b n) -> p b n", b=NB)
            for h in range(HA):
                r = slice(32 * h, 32 * h + 32)
                sn.done(v.tensor_tensor(sS[r], sS[r], kvp[r, :, DV * h:DV * h + DV], ALU.add), wait=False)
            dve.wait_ge(osq_ok, 1)
            v.tensor_reduce(ss, tG.rearrange("p t (h n) -> p (t h) n", h=HA), AX_X, ALU.add).then_inc(ossq_ok, 1)
            dve.wait_ge(ostd_ok, 1)
            lk.done(v.reciprocal(rs, rs))
            o4 = oG.rearrange("p t (h n) -> p (t h) n", h=HA)
            lk.done(v.tensor_tensor(o4, o4, rs.unsqueeze(2).broadcast_to([P, NT * HA, DV]), ALU.mult))
            lk.done(v.tensor_tensor(oG, oG, gng.unsqueeze(1).broadcast_to([P, NT, HA * DV]), ALU.mult))
            dve.wait_ge(rexp_ok, 1)
            lk.done(v.tensor_scalar(tG, tG, 1.0, None, ALU.add))
            lk.done(v.reciprocal(tG, tG))
            lk.done(v.tensor_tensor(tG, tG, proj[:, :, 528:784], ALU.mult))
            v.tensor_tensor(oG, oG, tG, ALU.mult).then_inc(og_ok, 1)
            stage_end(dve, 1)

            nc.vector.sem_inc(pair_dve, 1)
            with dve.Fori(0, PAIRS) as c:
                lk.enter(c, 16)
                dve.wait_ge(qkT_ps, c + 1)
                v.tensor_scalar(qT.rearrange("p (t n) -> p t n", t=PT)[:, :, ::-1],
                                banks[:, 512 * 4:512 * 6].rearrange("p (t n) -> p t n", t=PT), DH ** -0.5, None,
                                ALU.mult).then_inc(qT_ok, 1)

                def bias_max(a):
                    hh, i = a // PT, a % PT
                    n = (i + 1) * P
                    b = 2 * (a % 2)
                    dve.wait_ge(s_ps, c * 16 + (a + 1))
                    if a == 0:
                        dve.wait_ge(strip_in, c * 32 + 32)
                    if a >= 2:
                        dve.wait_ge(p_ok, c * 16 + (a - 1))
                    dve.nop(nofuse=True)
                    v.tensor_tensor_reduce(sB[a % 2][:, 0:n], banks[:, 512 * b:512 * b + n], strip[:, hh, P * (PT - 1 - i):D],
                                           1.0, -3e38, ALU.add, ALU.max, mx[:, a % 2:a % 2 + 1]).then_inc(s_read, 1)
                    dve.wait_ge(s_read, c * 16 + (a + 1))
                    v.tensor_scalar(nmx[:, a % 2:a % 2 + 1], mx[:, a % 2:a % 2 + 1], -1.0, None, ALU.mult).then_inc(m_ok, 1)

                def scale_out(a):
                    hh, i = a // PT, a % PT
                    dve.wait_ge(p_ok, c * 16 + (a + 1))
                    lk.done(v.reciprocal(rden[:, a:a + 1], den[:, a:a + 1]))
                    dve.wait_ge(o_ps, c * 16 + (a + 1))
                    v.tensor_scalar(oB[:, i, DH * hh:DH * hh + DH], bank(6 + a % 2, DH), rden[:, a:a + 1], None,
                                    ALU.mult).then_inc(o_ok, 1)
                bias_max(0)
                for a in range(16):
                    if a < 15:
                        if a >= 1:
                            dve.wait_ge(m_ok, c * 16 + (a + 1) - 1)
                        bias_max(a + 1)
                    if a >= 1:
                        scale_out(a - 1)
                    nb = a % PT + 1 - 4
                    if nb > 0:
                        dve.wait_ge(pt_ps, c * 16 + (a + 1))
                        if a >= 2:
                            dve.wait_ge(o_ps, c * 16 + (a - 1))
                        v.tensor_copy(pTB[a % 2][:, 512:512 + nb * P], bank(5, nb * P)).then_inc(pt1_ok, 1)
                scale_out(15)
                dve.wait_ge(oT_ps, c + 2)
                v.tensor_copy(mixT[:, bass.ds(c + 2, 1), 512:1024].rearrange("p a (t n) -> p (a t) n", t=4),
                              bank(5).rearrange("p (t n) -> p t n", t=4)[:, :, ::-1]).then_inc(pair_dve, 1)
                lk.leave(PAIRS)
            stage_end(dve, 2)

            v.tensor_copy(ohb, ident[0:NB, 0:NB].unsqueeze(2).broadcast_to([NB, NB, P])).then_inc(ohb_ok, 1)
            lk.done(v.tensor_tensor(selfp, sq[:, 0], sq[:, 1], ALU.mult))
            lk.done(v.tensor_reduce(selfl, selfp.rearrange("p (h d) -> p h d", h=HD), AX_X, ALU.add))
            v.tensor_tensor(selfd.rearrange("p (b h) -> p b h", b=NB), selfl.unsqueeze(1).broadcast_to([NB, NB, HD]),
                            C("diag8", NB).rearrange("p (b h) -> p b h", b=NB), ALU.mult).then_inc(selfd_ok, 1)
            for b in range(NB):
                dve.wait_ge(kc_in[b % 2], 48 * (b // 2 + 1))
                dve.wait_ge(qb_ps, b + 1)
                if b >= 1:
                    dve.wait_ge(slog_ok, b)
                q = banks[:, 1024 * (b % 2):1024 * (b % 2) + QW]
                v.tensor_tensor(prod.rearrange("p (c n) -> p c n", c=2), kCb[b % 2], q.unsqueeze(1).broadcast_to([P, 2, QW]),
                                ALU.mult).then_inc(sprod, 1)
                dve.wait_ge(sprod, b + 1)
                v.tensor_reduce(lg[:, :, HD * b:HD * b + HD], prod.rearrange("p (c h d) -> p c h d", c=2, h=HD), AX_X,
                                ALU.add).then_inc(slog_ok, 1)
            dve.wait_ge(slT_ps, 1)
            n = NB * HD
            lk.done(v.scalar_tensor_tensor(out=srow[:, 0:CK], in0=bank(4, CK, n), scalar=DH ** -0.5, in1=sbias[:, 0:CK],
                                           op0=ALU.mult, op1=ALU.add), wait=False)
            lk.done(v.scalar_tensor_tensor(out=srow[:, CK:CK + 1], in0=bank(5, 1, n), scalar=DH ** -0.5,
                                           in1=sbias[:, CK:CK + 1], op0=ALU.mult, op1=ALU.add))
            st = [V(o_stat + i, 1, n) for i in range(4)]
            lk.done(v.tensor_reduce(st[0], srow, AX_X, ALU.max))
            v.tensor_scalar(st[1], st[0], -1.0, None, ALU.mult).then_inc(smax_ok, 1)
            dve.wait_ge(sexp_ok, 1)
            lk.done(v.reciprocal(st[3], st[2]))
            lk.done(v.tensor_scalar(srow, srow, st[3], None, ALU.mult))
            v.tensor_tensor(pself, srow[:, CK:CK + 1].broadcast_to([n, NB]), C("seq8", n), ALU.mult).then_inc(sp_ok, 1)
            dve.wait_ge(sov_ps, 1)
            so3 = bank(0, 96).rearrange("p (c b j) -> p c b j", c=PAIRS, b=NB)
            lk.done(v.tensor_copy(mixT[0:64, 2:KC, S:TOK], so3[0:64, :, :, 0]), wait=False)
            v.tensor_copy(mixT[64:128, 2:KC, S:TOK], so3[64:128, :, :, 1]).then_inc(smix_ok, 1)
            stage_end(dve, 3)

            for t in range(NT):
                n = rows_of(t)
                dve.wait_ge(op_ps, t + 1)
                if t == 0:
                    dve.wait_ge(bc2_ok, 4)
                dve.wait_ge(x_in[t % 2], 16 * (X_LOADS[t % 2] + t // 2 + 1))
                g, ga, sh = (bcG1, bcA2, bcS2) if t < PT else (modrow(G1, NB), modrow(SC2, NB), modrow(SH2, NB))
                b = 2 * (t % 2)
                lk.done(v.tensor_tensor(X1[0:n, t], banks[0:n, 512 * b:512 * b + D], g, ALU.mult))
                v.tensor_tensor(X1[0:n, t], X1[0:n, t], xr[t % 2][0:n], ALU.add).then_inc(x1_ok, 1)
                dve.wait_ge(x1_std, t + 1)
                lk.done(v.reciprocal(rs[0:n, t:t + 1], rs[0:n, t:t + 1]))
                if t >= 2:
                    dve.wait_ge(h2_out[t % 2], 16 * (t // 2))
                    dve.wait_ge(h2T_ps, t - 1)
                h = h2[t % 2][0:n]
                lk.done(v.scalar_tensor_tensor(out=h, in0=X1[0:n, t], scalar=rs[0:n, t:t + 1], in1=ga, op0=ALU.mult, op1=ALU.mult))
                v.tensor_tensor(h, h, sh, ALU.add).then_inc(h2_ok, 1)
                dve.wait_ge(h2_ok, t + 1)
            cl.done(v.memset(sco[:, PT * NE:RE], 1.0), wait=False)
            v4 = lambda a: a.rearrange("p (t g e) -> p (t g) e", t=NT, g=NG)
            v3 = lambda a: a.rearrange("p (t e) -> p t e", t=NT)
            bcE = lambda a, k: a.unsqueeze(2).broadcast_to([P, a.shape[1], k])
            dve.wait_ge(rexp2, 2)
            lk.done(v.tensor_scalar(sco, sco, 1.0, None, ALU.add))
            lk.done(v.reciprocal(sco, sco))
            lk.done(v.tensor_tensor(v3(sel), v3(sco), V(o_rb, NE).unsqueeze(1).broadcast_to([P, NT, NE]), ALU.add))
            p6 = pair6.rearrange("p (g j) -> p g j", j=6)
            s4 = v4(sel)
            lk.done(v.tensor_tensor(p6[:, :, 0:3], s4[:, :, 0:3], s4[:, :, 1:4], ALU.add), wait=False)
            lk.done(v.tensor_tensor(p6[:, :, 3:5], s4[:, :, 0:2], s4[:, :, 2:4], ALU.add), wait=False)
            lk.done(v.tensor_tensor(p6[:, :, 5:6], s4[:, :, 0:1], s4[:, :, 3:4], ALU.add))
            lk.done(v.tensor_reduce(gsc, p6, AX_X, ALU.max))
            g3 = lambda a: a.rearrange("p (t g) -> p t g", t=NT)
            prio_g = C("gprio").unsqueeze(1).broadcast_to([P, NT, NG])
            prio_e = C("eprio").unsqueeze(1).broadcast_to([P, NT, NE])
            lk.done(v.tensor_reduce(gm, g3(gsc), AX_X, ALU.max))
            lk.done(v.tensor_tensor(g3(gsel), g3(gsc), bcE(gm, NG), ALU.is_equal))
            lk.done(v.tensor_tensor(g3(gsel), g3(gsel), prio_g, ALU.mult))
            lk.done(v.tensor_reduce(gm, g3(gsel), AX_X, ALU.max))
            lk.done(v.tensor_tensor(g3(gsel), bcE(gm, NG), prio_g, ALU.is_equal))
            lk.done(v.tensor_tensor(v4(msel), v4(sel), bcE(gsel, PG), ALU.mult))
            lk.done(v.tensor_scalar(gsel, gsel, 1.0, 1e30, ALU.subtract, ALU.mult))
            lk.done(v.tensor_tensor(v4(msel), v4(msel), bcE(gsel, PG), ALU.add))
            for one in (one1, one2):
                lk.done(v.tensor_reduce(gm, v3(msel), AX_X, ALU.max))
                lk.done(v.tensor_tensor(v3(tA), v3(msel), bcE(gm, NE), ALU.is_equal))
                lk.done(v.tensor_tensor(v3(tA), v3(tA), prio_e, ALU.mult))
                lk.done(v.tensor_reduce(gm, v3(tA), AX_X, ALU.max))
                lk.done(v.tensor_tensor(v3(one), bcE(gm, NE), prio_e, ALU.is_equal))
                if one is one1:
                    lk.done(v.tensor_scalar(tA, one, -2e30, None, ALU.mult))
                    lk.done(v.tensor_tensor(msel, msel, tA, ALU.add))
            bt = Steps(dve, both_ok)
            lk.done(v.tensor_tensor(both, one1, one2, ALU.add))
            lk.done(v.tensor_scalar(both[:, PT * NE:RE], both[:, PT * NE:RE], C("srows"), None, ALU.mult))
            nc.vector.sem_inc(both_ok, 1)
            w12v = w12.rearrange("p (t j) -> p t j", j=2)
            for j, one in enumerate((one1, one2)):
                lk.done(v.tensor_tensor(tA, sco, one, ALU.mult))
                lk.done(v.tensor_reduce(w12v[:, :, j:j + 1], v3(tA), AX_X, ALU.add))
            lk.done(v.tensor_reduce(gm, w12v, AX_X, ALU.add))
            lk.done(v.reciprocal(gm, gm))
            lk.done(v.tensor_tensor(w12v, w12v, bcE(gm, 2), ALU.mult))
            dve.wait_ge(rank_ps, 1)
            lk.done(v.tensor_copy(rank, bank(0, RE)), wait=False)
            lk.done(v.tensor_copy(cnt, bank(1, RE)), wait=False)
            lk.done(v.memset(base[:, 0:NE], 0.0))
            for t in range(PT):
                lk.done(v.tensor_tensor(base[:, (t + 1) * NE:(t + 2) * NE], base[:, t * NE:(t + 1) * NE], cnt[:, t * NE:(t + 1) * NE], ALU.add))
            lk.done(v.tensor_tensor(nE, base[:, PT * NE:RE], cnt[:, PT * NE:RE], ALU.add))
            c9 = cmp9.rearrange("p (e t) -> p e t", e=NE)
            lk.done(v.tensor_tensor(c9, bcE(nE, NT), C("thr").unsqueeze(1).broadcast_to([P, NE, NT]), ALU.is_gt))
            lk.done(v.tensor_reduce(tE, c9, AX_X, ALU.add))
            cE = cmpE.rearrange("p (e f) -> p e f", e=NE)
            lk.done(v.tensor_tensor(cE, tE.unsqueeze(1).broadcast_to([P, NE, NE]), C("before").rearrange("p (e f) -> p e f", e=NE), ALU.mult))
            lk.done(v.tensor_reduce(offE, cE, AX_X, ALU.add))
            lk.done(v.tensor_tensor(rank, rank, base, ALU.add))
            lk.done(v.tensor_scalar(nE, offE, float(P), None, ALU.mult))
            lk.done(v.tensor_tensor(v3(rank), v3(rank), nE.unsqueeze(1).broadcast_to([P, NT, NE]), ALU.add))
            sl = slotf.rearrange("p (t j) -> p t j", j=2)
            for j, one in enumerate((one1, one2)):
                lk.done(v.tensor_tensor(tA, rank, one, ALU.mult))
                lk.done(v.tensor_reduce(sl[:, :, j:j + 1], v3(tA), AX_X, ALU.add))
            lk.done(v.tensor_copy(ids[:, 0:2 * NT], slotf))
            lk.done(v.tensor_copy(ids[:, 2 * NT:3 * NT], C("tokid")))
            lk.done(v.tensor_tensor(offE, offE, tE, ALU.add))
            ec = ecmp.rearrange("p (m e) -> p m e", m=MT)
            lk.done(v.tensor_tensor(ec, bcE(C("tile"), NE), offE.unsqueeze(1).broadcast_to([P, MT, NE]), ALU.is_ge))
            lk.done(v.tensor_reduce(etf, ec, AX_X, ALU.add))
            lk.done(v.tensor_scalar(etf, etf, float(NE - 1), None, ALU.min))
            v.tensor_copy(etab[0:1], etf[0:1]).then_inc(route_ok, 1)
            stage_end(dve, 4)

            nc.vector.sem_inc(yB_cp, 1)
            with dve.Fori(0, MT // 2) as i:
                lk.enter(i, 6)
                lk_base = lk.at
                for s in range(2):
                    t1 = i * 2 + (s + 1)
                    dve.wait_ge(gexp_ok, t1)
                    lk.done(v.tensor_scalar(sg, sg, 1.0, None, ALU.add))
                    lk.done(v.reciprocal(sg, sg))
                    lk.done(v.tensor_tensor(sg, sg, bank(2), ALU.mult))
                    dve.wait_ge(u_ps, t1 + 2)
                    dve.wait_ge(hidT_ps, t1)
                    v.tensor_tensor(hid, sg, bank(3), ALU.mult).then_inc(hid_ok, 1)
                    dve.wait_ge(y_ps, t1 + 2)
                    dve.wait_ge(yrow_out[s], i * 16 + 16)
                    v.tensor_copy(yM[s][:, 512:D], bank(6)).then_inc(yB_cp, 1)
                lk.leave(MT // 2)
            stage_end(dve, 5)
            dve.wait_ge(vec_in, 112)
            for t in range(NT):
                n = rows_of(t)
                ya, yb = yA[t % 2][0:n], yB[t % 2][0:n]
                dve.wait_ge(ya_in[t % 2], 32 * (t // 2 + 1))
                lk.done(v.tensor_scalar(ya, ya, w12[0:n, 2 * t:2 * t + 1], None, ALU.mult))
                lk.done(v.scalar_tensor_tensor(out=ya, in0=yb, scalar=w12[0:n, 2 * t + 1:2 * t + 2], in1=ya, op0=ALU.mult, op1=ALU.add))
                lk.done(v.tensor_tensor(ya, ya, g2b if t < PT else modrow(G2, NB), ALU.mult))
                v.tensor_tensor(X1[0:n, t], X1[0:n, t], ya, ALU.add).then_inc(x2_ok, 1)
                dve.wait_ge(x2_std, t + 1)
                lk.done(v.reciprocal(rs[0:n, t:t + 1], rs[0:n, t:t + 1]))
                v.scalar_tensor_tensor(out=ya, in0=X1[0:n, t], scalar=rs[0:n, t:t + 1], in1=fng[0:n], op0=ALU.mult,
                                       op1=ALU.mult).then_inc(y_ok, 1)

        @block.tensor
        def _(pe):
            mm, tr = nc.tensor.matmul, nc.tensor.transpose
            pe.wait_ge(const_in, 16)
            pe.wait_ge(crow_in, 48)
            pe.wait_ge(cleared, 2)
            pe.wait_ge(bias_ps, 1)
            oh, ohs = C("oh", 33), C("ohs", 33)
            for o in range(0, GN, 512):
                w = min(512, GN - o)
                mm(banks[0:HD, o:o + w], relx, oh[:, o:o + w], start=True, stop=True)
            mm(banks[0:NB * HD, 1536:1536 + CK + 1], relr, ohs, start=True, stop=True).then_inc(bias_ps, 1)
            pe.wait_ge(silu_c, 1)
            for k in range(KC):
                last = tr(bank(7, KC * 33)[:, k * 33:(k + 1) * 33], crow[:, k * P:(k + 1) * P], ident[0:33, 0:33])
            last.then_inc(csT_ps, 1)
            pe.wait_ge(csT_ok, 1)
            with pe.Fori(0, 4) as i:
                for s in range(3):
                    pe.wait_ge(ada_in[s], i * 32 + 32)
                    for k in range(KC):
                        last = mm(bank(4 + s, 512, 33), csT[:, k], wa[s][:, k], start=(k == 0), stop=(k == KC - 1))
                    last.then_inc(ada_ps, 1)
            pe.wait_ge(bias_ok, 3)
            for t in range(NT):
                n = rows_of(t)
                pe.wait_ge(h_ok, t + 1)
                if t >= 2:
                    pe.wait_ge(hT_ok, t - 1)
                b = 2 * (t % 2)
                for k in range(KC):
                    last = tr(banks[:, 512 * b + n * k:512 * b + n * k + n], xt[t % 2][0:n, k * P:(k + 1) * P], ident[0:n, 0:n])
                last.then_inc(hT_ps, 1)
            stage_end(pe, 0)

            pe.wait_ge(wG_in, 32)
            for t in range(NT):
                n = rows_of(t)
                if t >= 2:
                    pe.wait_ge(gprojA, t - 1)
                    pe.wait_ge(gprojB, t - 1)
                b = 4 + 2 * (t % 2)
                for o, w, bb in ((0, 512, b), (512, GW - 512, b + 1)):
                    for k in range(KC):
                        last = mm(bank(bb, w, n), hT[:, k, t * P:t * P + n], wG[:, k, o:o + w], start=(k == 0), stop=(k == KC - 1))
                last.then_inc(gproj_ps, 1)
            pe.wait_ge(gprojB, NT)
            pe.wait_ge(gprojA, NT)
            for t in range(PT):
                tr(banks[0:RANK, t * P:(t + 1) * P], proj[:, t, 512:528], ident)
            tr(bank(2, NB, RANK), proj[0:NB, PT, 512:528], ident[0:NB, 0:NB]).then_inc(gl_ps, 1)
            pe.wait_ge(gl_ok, 2)
            wgu = V(o_wgu, P, RANK + 1)
            pe.wait_ge(vec_in, 96)
            for t in range(PT):
                mm(banks[:, t * P:(t + 1) * P], glT[0:RANK + 1, t * P:(t + 1) * P], wgu, start=True, stop=True)
            mm(bank(2, P, NB), glT[0:RANK + 1, S:TOK], wgu, start=True, stop=True).then_inc(z_ps, 1)
            pe.wait_ge(loga_ok, 2)
            for j, name in enumerate(("cum_mid", "cum_rest", "cum")):
                for h in range(2):
                    mm(bank(2 * j + h), C(name), L[:, 512 * h:512 * h + 512], start=True, stop=True)
            for t in range(PT):
                last = mm(bank(6, PT)[:, t:t + 1], L[:, t * P:(t + 1) * P], C("ones")[:, 0:1], start=True, stop=True)
            last.then_inc(cum_ps, 1)
            pe.wait_ge(scaled_ok, 4)
            pe.wait_ge(edec_ok, 6)
            for t in range(PT):
                tr(banks[:, t * P:(t + 1) * P], E[1][:, t * P:(t + 1) * P], ident)
            for t in range(PT):
                tr(banks[:, 1024 + t * P:1024 + (t + 1) * P], E[3][:, t * P:(t + 1) * P], ident)
            for t in range(PT):
                last = tr(banks[:, 2048 + t * P:2048 + (t + 1) * P], E[0][:, t * P:(t + 1) * P], ident)
            last.then_inc(gT_ps, 1)
            pe.wait_ge(k2T_ok, 1)
            pe.wait_ge(q4T_ok, 1)
            for t in range(PT):
                pe.wait_ge(blk_ok, t + 1)
                if t >= 2:
                    pe.wait_ge(att_cp, t - 1)
                mm(bank(t % 2), k2T[:, t * P:(t + 1) * P], blkq[t % 2], start=True, stop=True).then_inc(att_ps, 1)
                if t >= 1:
                    pe.wait_ge(state_ok, t + 1)
                mm(bank(7, 256), E[2][:, t * P:(t + 1) * P], proj[:, t, 256:512], start=True, stop=True).then_inc(ds_ps, 1)
                pe.wait_ge(att_ok, t + 1)
                pe.wait_ge(state_ok, t + 1)
                if t >= 2:
                    pe.wait_ge(og_cp, t - 1)
                ob = bank(2 + t % 2, 256)
                mm(ob, q4T[:, t * P:(t + 1) * P], state[t % 2], start=True, stop=True, skip_group_check=True)
                for h in range(HA):
                    last = mm(ob[:, DV * h:DV * h + DV], attS[t % 2][:, P * h:P * h + P], proj[:, t, 256 + DV * h:256 + DV * h + DV],
                              start=False, stop=True, skip_group_check=True)
                last.then_inc(og_ps, 1)
            pe.wait_ge(att_cp, PT)
            for j, src in enumerate((sA, proj[0:NB, PT, P:2 * P], proj[0:NB, PT, 0:P])):
                last = tr(bank(0, 3 * NB)[:, j * NB:(j + 1) * NB], src, ident[0:NB, 0:NB])
            last.then_inc(sc3_ps, 1)
            pe.wait_ge(sc3_ok, 2)
            pe.wait_ge(state_ok, PT + 1)
            for b in range(NB):
                last = mm(banks[:, 2048 + 256 * b:2048 + 256 * b + 256], kz[:, b], proj[0:NB, PT, 256:512], start=True, stop=True)
            last.then_inc(kv_ps, 1)
            pe.wait_ge(snew_ok, 5)
            for h in range(HA):
                for b in range(NB):
                    last = mm(bank(0, 256, NB)[:, DV * h:DV * h + DV], qz[:, (h * NB + b) * NB:(h * NB + b + 1) * NB], sS[:, b],
                              start=(b == 0), stop=(b == NB - 1))
            last.then_inc(so_ps, 1)
            pe.wait_ge(og_ok, 1)
            for c in range(2):
                for t in range(PT):
                    tr(banks[:, 1024 * c + t * P:1024 * c + (t + 1) * P], oG[:, t, c * P:(c + 1) * P], ident)
                last = tr(bank(4 + c, NB), oG[0:NB, PT, c * P:(c + 1) * P], ident[0:NB, 0:NB])
            last.then_inc(ogT_ps, 1)
            stage_end(pe, 1)

            nc.tensor.sem_inc(wP_free, 1)
            nc.tensor.sem_inc(oT_ps, 1)
            with pe.Fori(0, PAIRS) as c:
                pe.wait_ge(pair_dve, c + 1)
                pe.wait_ge(pair_act, c + 1)
                pe.wait_ge(wP_in, c * 48 + 48)
                for t in range(NT):
                    n = rows_of(t)
                    if t >= 4:
                        pe.wait_ge(qkv_ok, c * NT + (t - 3))
                    for k in range(KC):
                        last = mm(bank(t % 4, 384, n), hT[:, k, t * P:t * P + n], wP[:, k].rearrange("p g n -> p (g n)"),
                                  start=(k == 0), stop=(k == KC - 1))
                    last.then_inc(qkv_ps, 1)
                nc.tensor.drain().then_inc(wP_free, 1)
                pe.wait_ge(qkv_ok, c * NT + NT)
                for j in range(2):
                    for t in range(PT):
                        last = tr(banks[:, 2048 + 1024 * j + t * P:2048 + 1024 * j + (t + 1) * P], qkv[:, t, j * P:(j + 1) * P], ident)
                last.then_inc(qkT_ps, 1)

                def scores(a):
                    hh, i = a // PT, a % PT
                    r = slice(DH * hh, DH * hh + DH)
                    if a == 0:
                        pe.wait_ge(qT_ok, c + 1)
                        pe.wait_ge(kT_ok, c + 1)
                    if a >= 2:
                        pe.wait_ge(s_read, c * 16 + (a - 1))
                    for o in range(0, (i + 1) * P, 512):
                        w = min(512, (i + 1) * P - o)
                        b = 2 * (a % 2)
                        last = mm(banks[:, 512 * b + o:512 * b + o + w], qT[r, i * P:(i + 1) * P], kT[r, o:o + w], start=True, stop=True)
                    last.then_inc(s_ps, 1)

                def turn(a):
                    i = a % PT
                    pe.wait_ge(p_ok, c * 16 + (a + 1))
                    for j in range(i + 1):
                        last = tr(banks[:, 2048 + j * P:2048 + (j + 1) * P], pB[a % 2][:, j * P:(j + 1) * P], ident)
                    last.then_inc(pt_ps, 1)

                def values(a):
                    hh, i = a // PT, a % PT
                    pe.wait_ge(pt0_ok, c * 16 + (a + 1))
                    if i >= 4:
                        pe.wait_ge(pt1_ok, c * 8 + (hh * 4 + i - 3))
                    if a >= 2:
                        pe.wait_ge(o_ok, c * 16 + (a - 1))
                    for j in range(i + 1):
                        last = mm(bank(6 + a % 2, DH), pTB[a % 2][:, j * P:(j + 1) * P], qkv[:, j, 256 + DH * hh:256 + DH * hh + DH],
                                  start=(j == 0), stop=(j == i))
                    last.then_inc(o_ps, 1)
                scores(0)
                scores(1)
                for a in range(16):
                    if a >= 1:
                        values(a - 1)
                    turn(a)
                    if a + 2 < 16:
                        scores(a + 2)
                values(15)
                pe.wait_ge(o_ok, c * 16 + 16)
                for t in range(PT):
                    last = tr(banks[:, 2048 + t * P:2048 + (t + 1) * P], oB[:, t], ident)
                last.then_inc(oT_ps, 1)
            stage_end(pe, 2)

            pe.wait_ge(ohb_ok, 1)
            for b in range(NB):
                if b >= 2:
                    pe.wait_ge(sprod, b - 1)
                o = 1024 * (b % 2)
                mm(banks[:, o:o + 512], ohb[:, b], sq[:, 0, 0:512], start=True, stop=True)
                mm(banks[:, o + 512:o + QW], ohb[:, b], sq[:, 0, 512:QW], start=True, stop=True).then_inc(qb_ps, 1)
            pe.wait_ge(slog_ok, NB)
            pe.wait_ge(selfd_ok, 1)
            n = NB * HD
            for j in range(2):
                tr(bank(4, CK, n)[:, j * P:(j + 1) * P], lg[:, j], ident)
            mm(bank(5, 1, n), selfd, C("ones", NB)[:, 0:1], start=True, stop=True).then_inc(slT_ps, 1)
            pe.wait_ge(sp_ok, 1)
            for j in range(2):
                tr(bank(6, 2 * n)[:, j * n:(j + 1) * n], srow[:, j * P:(j + 1) * P], ident[0:n, 0:n])
            tr(bank(7, n, NB), pself, ident[0:n, 0:n]).then_inc(spT_ps, 1)
            pe.wait_ge(spT_ok, 1)
            pe.wait_ge(vc_in, 48 * NB)
            for c in range(PAIRS):
                rhs = pselfT.rearrange("p (b h) -> p b h", b=NB)[:, :, 2 * c:2 * c + 2]
                mm(bank(0, 96)[:, 16 * c:16 * c + 16], sq[:, 2, c * P:(c + 1) * P], rhs, start=(c == 0), stop=True, skip_group_check=True)
            for b in range(NB):
                for c in range(PAIRS):
                    for j in range(2):
                        o = 16 * c + 2 * b
                        last = mm(bank(0, 96)[:, o:o + 2], vC[b][:, j, c * P:(c + 1) * P], spT[:, j, HD * b + 2 * c:HD * b + 2 * c + 2],
                                  start=False, stop=(j == 1), skip_group_check=True)
            last.then_inc(sov_ps, 1)
            stage_end(pe, 3)

            pe.wait_ge(wO_in, 32)

            def project(t):
                n = rows_of(t)
                if t >= 2:
                    pe.wait_ge(x1_ok, t - 1)
                b = 2 * (t % 2)
                for h in range(2):
                    for k in range(KC):
                        last = mm(bank(b + h, 512, n), mixT[:, k, t * P:t * P + n], wO[:, k, 512 * h:512 * h + 512], start=(k == 0), stop=(k == KC - 1))
                last.then_inc(op_ps, 1)

            def route(t):
                n = rows_of(t)
                pe.wait_ge(h2_ok, t + 1)
                if t >= 1:
                    pe.wait_ge(h2T_ok, t)
                for k in range(KC):
                    last = tr(banks[:, 2048 + n * k:2048 + n * k + n], h2[t % 2][0:n, k * P:(k + 1) * P], ident[0:n, 0:n])
                last.then_inc(h2T_ps, 1)
                pe.wait_ge(h2T_ok, t + 1)
                out = bank(6, PT * NE)[:, t * NE:(t + 1) * NE] if t < PT else bank(7, NE, NB)
                for k in range(KC):
                    last = mm(out, h2T[:, k, 0:n], rw[:, k], start=(k == 0), stop=(k == KC - 1))
                last.then_inc(lr_ps, 1)
            project(0)
            for t in range(NT):
                if t + 1 < NT:
                    project(t + 1)
                route(t)
            pe.wait_ge(both_ok, 1)
            mm(bank(0, RE), C("strict"), both, start=True, stop=True)
            mm(bank(1, RE), C("ones"), both, start=True, stop=True).then_inc(rank_ps, 1)
            stage_end(pe, 4)

            nc.tensor.sem_inc(u_ps, 2)
            nc.tensor.sem_inc(y_ps, 2)
            nc.tensor.sem_inc(xgT_ps, 2)
            nc.tensor.sem_inc(hidT_ps, 1)
            with pe.Fori(0, MT // 2) as i:
                for s in range(2):
                    t0 = i * 2 + s
                    pe.wait_ge(xg_in[s], i * 16 + 16)
                    for k in range(KC):
                        last = tr(banks[:, k * P:(k + 1) * P], xg[s][:, k * P:(k + 1) * P], ident)
                    last.then_inc(xgT_ps, 1)
                    pe.wait_ge(xgT_ok, t0 + 1)
                    pe.wait_ge(mgu_in[s], i * 32 + 32)
                    for bb, w, sig in ((2, mwg, g_ps), (3, mwu, u_ps)):
                        for k in range(KC):
                            last = mm(bank(bb), xgT[:, k], w[s][:, k], start=(k == 0), stop=(k == KC - 1))
                        last.then_inc(sig, 1)
                    pe.wait_ge(hid_ok, t0 + 1)
                    for k in range(4):
                        last = tr(bank(4)[:, k * P:(k + 1) * P], hid[:, k * P:(k + 1) * P], ident)
                    last.then_inc(hidT_ps, 1)
                    pe.wait_ge(hidT_ok, t0 + 1)
                    pe.wait_ge(md_in[s], i * 16 + 16)
                    pe.wait_ge(yA_cp, t0 + 1)
                    pe.wait_ge(yB_cp, t0 + 1)
                    for h in range(2):
                        for k in range(4):
                            last = mm(bank(5 + h), hidT[:, k], mwd[s][:, k, 512 * h:512 * h + 512], start=(k == 0), stop=(k == 3))
                    last.then_inc(y_ps, 1)
            stage_end(pe, 5)


def shape_constants():
    import math
    import numpy as np
    t = np.zeros((P, CONST_COLS), np.float32)

    def put(name, a, rows=P):
        o, w = _cols[name]
        t[:rows, o:o + w] = np.asarray(a, np.float32).reshape(rows, w)
    r, c = np.arange(P)[:, None], np.arange(P)[None, :]
    put("ident", r == c)
    put("ones", np.ones((P, P)))
    put("cum_mid", (r <= c).astype(np.float32) - (r <= P // 2 - 1))
    put("cum", r <= c)
    put("cum_rest", r > c)
    put("strict", r < c)
    put("blk", r // DK == np.arange(HA * DV)[None, :] // DV)

    def columns(dist):
        d = np.maximum(dist, 0)
        df = np.maximum(d, 1).astype(np.float32)
        large = 16 + (np.log(df / np.float32(16)) / np.float32(math.log(128.0)) * np.float32(16)).astype(np.int32)
        bucket = np.where(d < 16, d, np.minimum(large, 31))
        count = (dist <= 128).astype(int) + ((dist <= 512) & (dist % 4 == 0)) + (dist % 16 == 0)
        count = np.where(dist >= 0, count, 0)
        out = np.zeros((33, dist.size), np.float32)
        out[bucket, np.arange(dist.size)] = 1.0
        out[32] = np.where(count > 0, np.log(np.maximum(count, 1)), NEG)
        return out
    put("oh", columns(S - 1 - np.arange(GN)), 33)
    pos = np.concatenate([np.arange(896, 1024), np.arange(512, 896, 4), np.arange(0, 512, 16), [1024]])
    put("ohs", columns(1024 - pos), 33)
    n = NB * HD
    put("seq8", np.arange(n)[:, None] // HD == np.arange(NB)[None, :], n)
    put("diag8", np.arange(NB)[:, None] == np.arange(n)[None, :] // HD, NB)
    put("eprio", np.tile(NE - np.arange(NE), (P, 1)))
    put("gprio", np.tile(NG - np.arange(NG), (P, 1)))
    put("thr", np.tile(P * np.arange(NT), (P, 1)))
    put("before", np.tile((np.arange(NE)[None, :] < np.arange(NE)[:, None]).reshape(1, -1), (P, 1)))
    put("tile", np.tile(np.arange(MT), (P, 1)))
    put("srows", r < NB)
    put("tokid", np.arange(NT)[None, :] * P + np.arange(P)[:, None])
    put("eps", np.full((P, 1), EPS))
    put("one", np.ones((P, 1)))
    return t


_INS = ["x_prompt", "x_sample", "state_gla", "cache_win_k", "cache_win_v", "c_prompt", "c_sample", "w_ada", "b_ada",
        "norm1_g", "norm2_g", "w_in", "w_gate_up", "b_gate", "gla_norm_g", "w_o", "rel_bias", "router_w", "router_b",
        "moe_w_gate", "moe_w_up", "moe_w_down", "final_norm_g"]
_OUTS = [(1, 1024, 1024), (8, 1, 1024), (1, 1, 4, 32, 64), (1, 1, 1024, 12, 64), (1, 1, 1024, 12, 64),
         (1, 8, 4, 32, 64), (1, 8, 1, 12, 64), (1, 8, 1, 12, 64)]


def kernel(**inputs):
    import numpy as _np
    import concourse.bacc as _bacc
    from concourse import mybir as _mybir
    from concourse.bass_utils import run_bass_kernel_spmd as _run

    nc = _bacc.Bacc("TRN2", target_bir_lowering=False, num_devices=1)
    arrays, args = {}, []
    for name in _INS:
        a = _np.ascontiguousarray(inputs[name])
        arrays[f"in_{name}_dram"] = a
        args.append(nc.dram_tensor(f"in_{name}_dram", a.shape, _mybir.dt.from_np(a.dtype), kind="ExternalInput").ap())
    table = shape_constants()
    arrays["in_consts_dram"] = table
    args.append(nc.dram_tensor("in_consts_dram", table.shape, _mybir.dt.float32, kind="ExternalInput").ap())
    for i, shape in enumerate(_OUTS):
        args.append(nc.dram_tensor(f"out_{i}_dram", shape, _mybir.dt.float32, kind="ExternalOutput").ap())
    build(nc, *args)
    r = _run(nc, [arrays], core_ids=[0])
    return tuple(r.results[0][f"out_{i}_dram"] for i in range(len(_OUTS)))
```

```python
import concourse.bass as bass
from concourse import mybir
from contextlib import ExitStack

F32 = mybir.dt.float32
F16 = mybir.dt.float16
I32 = mybir.dt.int32
U32 = mybir.dt.uint32
ALU = mybir.AluOpType
ACT = mybir.ActivationFunctionType
AX_X = mybir.AxisListType.X

P = 128
D = 1024
KC = D // P
S = 1024
NB = 8
PT = S // P
NT = PT + 1
TOK = S + NB
HA, DK, DV = 4, 32, 64
RANK = 16
HD, DH = 12, 64
PAIRS = HD // 2
GW = 2 * HA * DK + 2 * HA * DV + RANK
QW = HD * DH
NE, NG, PG = 16, 4, 4
FF = 512
MT = 2 * TOK // P + NE
SLOTS = MT * P
PIECE = 2048
EPS = 1e-6
X_LOADS = ((NT + 1) // 2, NT // 2)
GN = S + P - 1
CK = 256
NEG = -1e30
WS = 1024.0
STEP_PROJ = {3 + n: (n, (0, 1)) for n in range(5)} | {8 + n: (5 + n // 2, (n % 2,)) for n in range(8)}

_cols = {}
_at = 0
for _name, _w in (("ident", P), ("ones", P), ("cum_mid", P), ("cum", P), ("cum_rest", P), ("strict", P),
                  ("blk", HA * DV), ("oh", GN), ("ohs", CK + 1), ("seq8", NB), ("diag8", NB * HD),
                  ("eprio", NE), ("gprio", NG), ("thr", NT), ("before", NE * NE), ("srows", 1), ("tokid", NT),
                  ("eps", 1), ("one", 1)):
    _cols[_name] = (_at, _w)
    _at += _w
CONST_COLS = _at

A_CONST = 0
A_SMALL = (CONST_COLS + 31) // 32 * 32
A_MOD = A_SMALL + 1184
A_G2 = A_MOD + 6 * D
A_F = A_G2 + D
A_HT = A_F
A_X1 = A_F
A_MIX = A_F + NT * D
A_T = A_MIX + KC * TOK
ARENA = 53120
A_MOE = A_MIX
A_STAGE = ARENA - 3 * PIECE


class Steps:

    def __init__(self, eng, sem):
        self.eng, self.sem, self.n, self.at, self.turn, self.per = eng, sem, 0, 0, None, 0

    def value(self):
        return self.n if self.turn is None else self.turn * self.per + self.n

    def done(self, ins, wait=True):
        ins.then_inc(self.sem, 1)
        self.n += 1
        if wait:
            self.eng.wait_ge(self.sem, self.value())

    def enter(self, turn, per):
        self.turn, self.per, self.at = turn, per, self.n

    def leave(self, turns):
        assert self.n - self.at == self.per, (self.n - self.at, self.per)
        self.turn = None
        self.n = self.at + turns * self.per


def build(nc, x_prompt, x_sample, state_gla, cache_win_k, cache_win_v, c_prompt, c_sample, w_ada, b_ada, norm1_g,
          norm2_g, w_in, w_gate_up, b_gate, gla_norm_g, w_o, rel_bias, router_w, router_b, moe_w_gate, moe_w_up,
          moe_w_down, final_norm_g, consts, y_prompt, y_sample, gla_state_p, win_k_p, win_v_p, gla_state_s,
          new_k_s, new_v_s):
    xp = x_prompt.rearrange("a s d -> (a s) d")
    xs = x_sample.rearrange("a s d -> (a s) d")
    yp = y_prompt.rearrange("a s d -> (a s) d")
    ys = y_sample.rearrange("a s d -> (a s) d")
    w_ada_v = w_ada.rearrange("l (k p) n -> p (l k) n", p=P)
    w_in_v = w_in.rearrange("l (k p) n -> p (l k) n", p=P)
    w_o_v = w_o.rearrange("l (k p) n -> p (l k) n", p=P)
    wg_flat = moe_w_gate.rearrange("l e d f -> (l e d) f")
    wu_flat = moe_w_up.rearrange("l e d f -> (l e d) f")
    wd_flat = moe_w_down.rearrange("l e f d -> (l e f) d")
    kp_v = win_k_p.rearrange("l b (t p) h d -> p (l b t) (h d)", p=P)
    vp_v = win_v_p.rearrange("l b (t p) h d -> p (l b t) (h d)", p=P)
    ck = cache_win_k.rearrange("l b s h d -> (l b) s (h d)")
    cv = cache_win_v.rearrange("l b s h d -> (l b) s (h d)")
    sgla = state_gla.rearrange("l b h k v -> (h k) (l b) v")
    sgla_out = gla_state_s.rearrange("l b h k v -> (h k) (l b) v")

    dist_bias = nc.dram_tensor("dist_bias", [HD * GN], F32, kind="Internal").ap()
    h2_rows = nc.dram_tensor("h2_rows", [TOK, D], F32, kind="Internal").ap()
    slot_token = nc.dram_tensor("slot_token", [SLOTS + P, 1], U32, kind="Internal").ap()
    slot_rows = nc.dram_tensor("slot_rows", [SLOTS, D], F32, kind="Internal").ap()

    with ExitStack() as ctx:
        def sem(name):
            return ctx.enter_context(nc.semaphore(name))

        arena = ctx.enter_context(nc.sbuf_tensor("arena", [P, ARENA], F32))
        banks = ctx.enter_context(nc.psum_tensor("banks", [P, 8 * 512], F32))
        ids = ctx.enter_context(nc.sbuf_tensor("ids", [P, 2 * NT + NT + 2], U32))
        etab = ctx.enter_context(nc.sbuf_tensor("etab", [1, NE + 1], I32))
        gidx = ctx.enter_context(nc.sbuf_tensor("gidx", [P, 1], U32))

        def V(off, cols, rows=P):
            return arena[0:rows, off:off + cols]

        def C(name, rows=P):
            o, w = _cols[name]
            return V(A_CONST + o, w, rows)

        def bank(b, cols=512, rows=P, n=1):
            return banks[0:rows, 512 * b:512 * b + cols]

        _s = [A_SMALL]

        def small(cols):
            _s[0] += cols
            assert _s[0] <= A_MOD
            return _s[0] - cols

        ident = C("ident")
        o_relx = small(HD)
        o_relr = small(NB * HD)
        o_sbias = small(CK + 1)
        o_gng = small(HA * DV)
        o_csT = small(KC * 33)
        o_ss = small(NT * HA)
        o_rs = small(NT * HA)
        o_den = small(2 * PT)
        o_rden = small(2 * PT)
        o_mx = small(2)
        o_nmx = small(2)
        o_w12 = small(2 * NT)
        o_wgu = small(HA * DK)
        o_stat = small(4)
        o_rb = small(NE)
        relx, relr, sbias = V(o_relx, HD, 33), V(o_relr, NB * HD, 33), V(o_sbias, CK + 1, NB * HD)
        gng = V(o_gng, HA * DV)
        csT = V(o_csT, KC * 33).rearrange("p (k m) -> p k m", k=KC)
        ss, rs = V(o_ss, NT * HA), V(o_rs, NT * HA)
        den, mx, nmx = V(o_den, 2 * PT), V(o_mx, 2), V(o_nmx, 2)
        rden = V(o_rden, 2 * PT)
        w12 = V(o_w12, 2 * NT)
        mod = V(A_MOD, 6 * D, 33)
        SH1, SC1, G1, SH2, SC2, G2 = range(6)
        hTh = V(A_HT, KC * TOK // 2).bitcast(F16).rearrange("p (k n) -> p k n", k=KC)
        hTl = V(A_HT + KC * TOK // 2, KC * TOK // 2).bitcast(F16).rearrange("p (k n) -> p k n", k=KC)
        mixT = V(A_MIX, KC * TOK).rearrange("p (k n) -> p k n", k=KC)

        def modrow(i, rows=33):
            return mod[0:rows, i * D:(i + 1) * D]

        def rows_of(t):
            return P if t < PT else NB

        crow = V(A_T, D, 33)
        csig = V(A_T + D, D, 33)
        wa = [V(A_T + 2 * D + s * 4096, 4096).rearrange("p (k n) -> p k n", k=KC) for s in range(3)]
        ba = [V(A_T + 2 * D + 3 * 4096 + s * 512, 512, 33) for s in range(3)]
        nrm = V(A_T + 2 * D + 3 * 4096 + 1536, 2 * D, 33)
        o_x = A_T + 2 * D + 3 * 4096 + 1536 + 2 * D
        xt = [V(o_x + s * D, D) for s in range(2)]
        bias_rows = V(A_MIX, GN, HD)
        bcA1, bcS1, sqj = V(A_MIX + 2 * D, D), V(A_MIX + 3 * D, D), V(A_MIX + 4 * D, D)

        wGh = V(A_T, KC * GW // 2).bitcast(F16).rearrange("p (k n) -> p k n", k=KC)
        wGl = V(A_T + KC * GW // 2, KC * GW // 2).bitcast(F16).rearrange("p (k n) -> p k n", k=KC)
        proj = V(A_T + KC * GW, NT * GW).rearrange("p (t n) -> p t n", t=NT)
        g0 = A_T + KC * GW + NT * GW
        wG = V(g0, KC * GW).rearrange("p (k n) -> p k n", k=KC)
        o_T1, o_L, o_E = g0, g0 + D, g0 + 2 * D
        T1, L = V(o_T1, D), V(o_L, D)
        E = [V(o_E + i * D, D) for i in range(4)]
        k2T, q4T = V(g0 + 6 * D, D), V(g0 + 7 * D, D)
        attS = [V(g0 + 8 * D + s * 512, 512) for s in range(2)]
        state = [V(g0 + 9 * D + s * 256, 256) for s in range(2)]
        dstate = V(g0 + 9 * D + 512, 256)
        g1 = g0 + 9 * D + 768
        o_sc3 = g1
        sS = V(A_CONST + _cols["oh"][0], NB * DV).rearrange("p (b v) -> p b v", b=NB)
        sc3 = V(o_sc3, 3 * NB)
        eblast = V(g1 + 24, PT)
        assert g1 + 32 <= ARENA, (g1, ARENA)
        oG = V(A_T, NT * 256).rearrange("p (t n) -> p t n", t=NT)
        tG = V(A_T + NT * 256, NT * 256).rearrange("p (t n) -> p t n", t=NT)
        blkq = [V(A_T + 2 * NT * 256 + s * 512, 512) for s in range(2)]
        qz = V(A_T + 2 * NT * 256 + 1024, HA * NB * NB)
        o_st = A_T + 2 * NT * 256 + 1024 + HA * NB * NB
        sT1, sL, sA = V(o_st, P, NB), V(o_st + P, P, NB), V(o_st + 2 * P, P, NB)
        kz = V(o_T1, NB * P, NB).rearrange("q (b n) -> q b n", b=NB)
        glT = V(A_MIX, TOK, 32)

        a0 = A_T
        wP = V(a0, KC * 384).rearrange("p (k g n) -> p k g n", k=KC, g=3); a0 += KC * 384
        wPh = V(a0, KC * 192).bitcast(F16).rearrange("p (k n) -> p k n", k=KC); a0 += KC * 192
        wPl = V(a0, KC * 192).bitcast(F16).rearrange("p (k n) -> p k n", k=KC); a0 += KC * 192
        qkv = V(a0, NT * 384).rearrange("p (t n) -> p t n", t=NT); a0 += NT * 384
        vcur = V(a0, D).rearrange("p (t n) -> p t n", t=PT); a0 += D
        qT, kT = V(a0, D), V(a0 + D, D); a0 += 2 * D
        strip = V(a0, 2 * D).rearrange("p (h n) -> p h n", h=2); a0 += 2 * D
        sB = [V(a0 + s * D, D) for s in range(2)]; a0 += 2 * D
        pB = [V(a0 + s * D, D) for s in range(2)]; a0 += 2 * D
        pTB = [V(a0 + s * D, D) for s in range(2)]; a0 += 2 * D
        oB = V(a0, D).rearrange("p (t n) -> p t n", t=PT); a0 += D
        assert a0 <= ARENA
        zeros = V(ARENA - 512, 512)
        assert a0 <= ARENA - 512
        sqk = V(A_MOD, 2 * QW, NB).rearrange("p (g n) -> p g n", g=2)
        sqv = V(A_G2, QW, NB)
        o_sa = A_T
        vC = [V(o_sa + b * 1536, 1536).rearrange("p (c n) -> p c n", c=2) for b in range(NB)]
        o_sb2 = o_sa + NB * 1536
        kCb = [V(o_sb2 + s * 1536, 1536).rearrange("p (c n) -> p c n", c=2) for s in range(2)]
        prod = V(o_sb2 + 3072, 1536)
        assert o_sb2 + 3072 + 1536 <= ARENA
        o_sc = A_HT
        ohb = V(o_sc, NB * P, NB).rearrange("q (b n) -> q b n", b=NB)
        lg = V(o_sc + 1024, 192).rearrange("p (c n) -> p c n", c=2)
        selfp = V(o_sc + 1216, QW, NB)
        selfl = V(o_sc + 1984, HD, NB)
        selfd = V(o_sc + 1996, NB * HD, NB)
        srow = V(o_sc + 2092, CK + 1, NB * HD)
        spT = V(o_sc + 2349, 192).rearrange("p (c n) -> p c n", c=2)
        pself = V(o_sc + 2541, NB, NB * HD)
        pselfT = V(o_sc + 2549, NB * HD, NB)

        a1 = A_T
        wO = V(a1, KC * D).rearrange("p (k n) -> p k n", k=KC); a1 += KC * D
        xr = [V(a1 + s * D, D) for s in range(2)]; a1 += 2 * D
        h2 = [V(a1 + s * D, D) for s in range(2)]; a1 += 2 * D
        h2T = V(a1, D).rearrange("p (k n) -> p k n", k=KC); a1 += D
        rw = V(a1, KC * NE).rearrange("p (k n) -> p k n", k=KC); a1 += KC * NE
        bcG1, bcA2, bcS2 = (V(a1 + i * D, D) for i in range(3)); a1 += 3 * D
        sqj2 = V(a1, D); a1 += D

        assert a1 <= A_STAGE, (a1, A_STAGE, A_T, A_MOD, A_SMALL, _s)
        free = [[A_MOD, A_MOD + 2 * D], [A_CONST + _cols["oh"][0], A_CONST + _cols["oh"][0] + GN]]

        def R(cols):
            r = next(r for r in free if r[1] - r[0] >= cols)
            r[0] += cols
            return V(r[0] - cols, cols)
        RE = NT * NE
        sco, sel, msel, tA, tB, one1, one2, both = (R(RE) for _ in range(8))
        pair6 = R(NT * NG * 6)
        gsc, gsel, gm = R(NT * NG), R(NT * NG), R(NT)
        rank, cnt, base = R(RE), R(RE), R(RE)
        nE, tE, offE = R(NE), R(NE), R(NE)
        cmp9, cmpE = R(NE * NT), R(NE * NE)
        slotf = R(2 * NT)
        s12 = R(2 * NT)
        zero_i = R(SLOTS // P + 1)
        X1 = V(A_X1, NT * D).rearrange("p (t n) -> p t n", t=NT)
        g2b = V(A_G2, D)

        m0 = A_MOE
        w_hi, w_lo = [], []
        for s in range(2):
            for parts in (w_hi, w_lo):
                parts.append([V(m0 + i * PIECE, PIECE).bitcast(F16) for i in range(3)])
                m0 += 3 * PIECE
        sg, hid = V(m0, FF), V(m0 + FF, FF)
        hidTh = V(m0 + 2 * FF, FF // 2).bitcast(F16).rearrange("p (k n) -> p k n", k=4)
        hidTl = V(m0 + 2 * FF + FF // 2, FF // 2).bitcast(F16).rearrange("p (k n) -> p k n", k=4)
        assert m0 + 3 * FF <= A_STAGE
        stage = [V(A_STAGE + r * PIECE, PIECE) for r in range(3)]
        xg = V(A_MOD, D)
        xgTh = V(A_MOD + D, D // 2).bitcast(F16).rearrange("p (k n) -> p k n", k=KC)
        xgTl = V(A_MOD + D + D // 2, D // 2).bitcast(F16).rearrange("p (k n) -> p k n", k=KC)
        yM = V(A_MOD + 2 * D, D)
        c0 = A_MOE
        yA = [V(c0 + s * D, D) for s in range(2)]
        yB = [V(c0 + (2 + s) * D, D) for s in range(2)]
        fng = V(c0 + 4 * D, D)
        sqj3 = V(c0 + 5 * D, D)

        const_in = sem("const_in"); crow_in = sem("crow_in"); vec_in = sem("vec_in")
        cleared = sem("cleared"); neg_exp_c = sem("neg_exp_c"); silu_c = sem("silu_c"); csT_ps = sem("csT_ps")
        csT_ok = sem("csT_ok"); ada_in = [sem(f"ada_in{s}") for s in range(3)]; ada_ps = sem("ada_ps")
        ada_added = sem("ada_added"); mod_ok = sem("mod_ok"); bc1_ok = sem("bc1_ok"); bc2_ok = sem("bc2_ok")
        bias_ps = sem("bias_ps"); bias_ok = sem("bias_ok")
        x_in = [sem(f"x_in{s}") for s in range(2)]; x_ssq = sem("x_ssq"); h_ok = sem("h_ok"); hT_ps = sem("hT_ps")
        hT_ok = sem("hT_ok"); act_link = sem("act_link"); dve_link = sem("dve_link"); pool_link = sem("pool_link")
        wG_in = sem("wG_in"); gproj_ps = sem("gproj_ps"); gprojA = sem("gprojA"); gprojB = sem("gprojB")
        gl_ps = sem("gl_ps"); gl_ok = sem("gl_ok"); z_ps = sem("z_ps"); lnz_ok = sem("lnz_ok"); loga_ok = sem("loga_ok")
        cum_ps = sem("cum_ps"); edec_ok = sem("edec_ok"); scaled_ok = sem("scaled_ok"); gT_ps = sem("gT_ps")
        k2T_ok = sem("k2T_ok"); q4T_ok = sem("q4T_ok"); blk_ok = sem("blk_ok"); att_ps = sem("att_ps")
        att_cp = sem("att_cp"); att_ok = sem("att_ok"); og_ps = sem("og_ps"); ds_ps = sem("ds_ps")
        state_ok = sem("state_ok"); og_cp = sem("og_cp"); gout = sem("gout")
        sc3_ps = sem("sc3_ps"); sc3_ok = sem("sc3_ok"); kv_ps = sem("kv_ps"); snew_ok = sem("snew_ok")
        so_ps = sem("so_ps"); osq_ok = sem("osq_ok"); ossq_ok = sem("ossq_ok"); ostd_ok = sem("ostd_ok")
        rexp_ok = sem("rexp_ok"); og_ok = sem("og_ok"); ogT_ps = sem("ogT_ps"); ogT_ok = sem("ogT_ok")
        wP_in = sem("wP_in"); strip_in = [sem(f"strip_in{h}") for h in range(2)]; pair_dve = sem("pair_dve"); pair_act = sem("pair_act")
        qkv_ps = sem("qkv_ps"); qkv_ok = sem("qkv_ok"); kv_out = sem("kv_out"); sq_ok = sem("sq_ok")
        qkT_ps = sem("qkT_ps"); qT_ok = sem("qT_ok"); kT_ok = sem("kT_ok"); s_ps = sem("s_ps"); s_read = sem("s_read")
        m_ok = sem("m_ok"); p_ok = sem("p_ok"); pt_ps = sem("pt_ps"); pt0_ok = sem("pt0_ok"); pt1_ok = sem("pt1_ok")
        o_ps = sem("o_ps"); o_ok = sem("o_ok"); oT_ps = sem("oT_ps"); whi_ok = sem("whi_ok"); wlo_ok = sem("wlo_ok"); v_ok = sem("v_ok")
        hT_hi = sem("hT_hi")
        kc_in = [sem(f"kc_in{s}") for s in range(2)]; vc_in = sem("vc_in")
        ohb_ok = sem("ohb_ok"); qb_ps = sem("qb_ps"); slog_ok = sem("slog_ok"); sprod = sem("sprod")
        selfd_ok = sem("selfd_ok"); slT_ps = sem("slT_ps"); smax_ok = sem("smax_ok"); sexp_ok = sem("sexp_ok")
        sp_ok = sem("sp_ok"); spT_ps = sem("spT_ps"); spT_ok = sem("spT_ok"); sov_ps = sem("sov_ps")
        smix_ok = sem("smix_ok")
        wO_in = sem("wO_in")
        op_ps = sem("op_ps"); x1_ok = sem("x1_ok"); x1_std = sem("x1_std"); h2_ok = sem("h2_ok")
        h2_out = [sem(f"h2_out{s}") for s in range(2)]; h2T_ps = sem("h2T_ps"); h2T_ok = sem("h2T_ok"); lr_ps = sem("lr_ps")
        rexp2 = sem("rexp2"); both_ok = sem("both_ok"); rank_ps = sem("rank_ps"); route_ok = sem("route_ok")
        zero_ok = sem("zero_ok"); st_zero = sem("st_zero"); st_out = sem("st_out")
        gi_in = sem("gi_in"); xg_in = sem("xg_in"); piece_in = [sem(f"piece_in{r}") for r in range(3)]
        phi_ok = sem("phi_ok"); plo_ok = sem("plo_ok")
        xgT_ps = sem("xgT_ps"); xgT_hi = sem("xgT_hi"); xgT_ok = sem("xgT_ok"); g_ps = sem("g_ps"); u_ps = sem("u_ps")
        gexp_ok = sem("gexp_ok"); hid_ok = sem("hid_ok"); hidT_ps = sem("hidT_ps"); hidT_hi = sem("hidT_hi")
        hidT_ok = sem("hidT_ok"); y_ps = sem("y_ps"); yA_cp = sem("yA_cp"); yB_cp = sem("yB_cp"); yrow_out = sem("yrow_out")
        ya_in = [sem(f"ya_in{s}") for s in range(2)]; mix_link = sem("mix_link"); rows_zero = sem("rows_zero"); x2_ok = sem("x2_ok"); x2_std = sem("x2_std")
        y_ok = sem("y_ok"); y_out = [sem(f"y_out{s}") for s in range(2)]
        stage_done = sem("stage_done")

        block = ctx.enter_context(nc.Block())

        def stage_end(eng, i):
            eng.drain().then_inc(stage_done, 1)
            eng.wait_ge(stage_done, 5 * (i + 1))

        @block.sync
        def _(sp):
            sp.dma_start(V(A_CONST, CONST_COLS), consts).then_inc(const_in, 16)
            sp.wait_ge(cleared, 3)
            sp.dma_start(crow[0:NB], c_sample).then_inc(crow_in, 16)
            sp.dma_start(crow[32:33], c_prompt).then_inc(crow_in, 16)
            sp.dma_start(relx[0:32], rel_bias).then_inc(crow_in, 16)

            def load_ada(j, s):
                sp.dma_start(wa[s], w_ada_v[:, :, bass.ds(j * 512, 512)]).then_inc(ada_in[s], 16)
                sp.dma_start(ba[s], b_ada[0:1, bass.ds(j * 512, 512)].partition_broadcast(33)).then_inc(ada_in[s], 16)
            for s in range(3):
                load_ada(s, s)
            sp.dma_start(nrm[:, 0:D], norm1_g[0:1, :].partition_broadcast(33)).then_inc(vec_in, 16)
            sp.dma_start(nrm[:, D:2 * D], norm2_g[0:1, :].partition_broadcast(33)).then_inc(vec_in, 16)
            sp.dma_start(gng, gla_norm_g[0:1, :].partition_broadcast(P)).then_inc(vec_in, 16)
            sp.dma_start(V(o_wgu, P, RANK), w_gate_up[0]).then_inc(vec_in, 16)
            sp.dma_start(arena[RANK:RANK + 1, o_wgu:o_wgu + P], b_gate[0:1, :]).then_inc(vec_in, 16)
            rb_v = router_b.rearrange("(a n) -> a n", a=1)
            sp.dma_start(V(o_rb, NE), rb_v.partition_broadcast(P)).then_inc(vec_in, 16)
            with sp.Fori(0, 3) as i:
                for s in range(3):
                    sp.wait_ge(ada_added, i * 3 + (s + 1))
                    sp.nop(nofuse=True)
                    load_ada(i * 3 + (s + 3), s)
            for t in range(NT):
                if t >= 2:
                    sp.wait_ge(hT_ps, t - 1)
                sp.dma_start(xt[t % 2][0:rows_of(t)], xp[t * P:(t + 1) * P] if t < PT else xs).then_inc(x_in[t % 2], 16)
            sp.wait_ge(bias_ok, 3)
            sp.dma_start(dist_bias.rearrange("(h n) -> h n", h=HD), bias_rows).then_inc(gout, 16)
            sp.wait_ge(gout, 16)
            stage_end(sp, 0)

            sp.dma_start(wG, w_in_v[:, :, 0:GW]).then_inc(wG_in, 16)
            sp.dma_start(sS, sgla).then_inc(wG_in, 16)
            sp.wait_ge(state_ok, 1 + PT)
            for h in range(HA):
                sp.dma_start(gla_state_p[0, 0, h], state[PT % 2][32 * h:32 * h + 32, DV * h:DV * h + DV]).then_inc(gout, 16)
            sp.wait_ge(snew_ok, 5)
            sp.dma_start(sgla_out, sS).then_inc(gout, 16)
            sp.wait_ge(gout, 16 * (HA + 2))
            stage_end(sp, 1)

            w_pair = w_in_v[:, :, GW:GW + 3 * QW].rearrange("p k (g n) -> p k g n", g=3)
            sp.sem_inc(kv_out, 16)

            def load_w(c):
                for g in range(3):
                    sp.dma_start(wP[:, :, g], w_pair[:, :, g, bass.ds(c * P, P)]).then_inc(wP_in, 16)

            def load_strip(c, hh):
                v = dist_bias[bass.ds(c * (2 * GN) + hh * GN, D)]
                sp.dma_start(strip[:, hh], bass.AP(tensor=v.tensor, offset=v.offset, ap=[[1, P], [1, D]]))\
                  .then_inc(strip_in[hh], 16)

            def pair_dmas(c, last, more):
                sp.wait_ge(qkv_ok, c * NT + NT)
                sp.nop(nofuse=True)
                sp.dma_start(kp_v[:, :, bass.ds(c * P, P)], qkv[:, 0:PT, 128:256]).then_inc(kv_out, 16)
                sp.dma_start(vp_v[:, :, bass.ds(c * P, P)], qkv[:, 0:PT, 256:384]).then_inc(kv_out, 16)
                if last:
                    return
                sp.wait_ge(s_read, c * 16 + 8)
                sp.nop(nofuse=True)
                load_strip(c + 1, 0)
                if more:
                    sp.wait_ge(wlo_ok, c * 2 + 5)
                    sp.nop(nofuse=True)
                    load_w(c + 2)
                sp.wait_ge(s_read, c * 16 + 16)
                sp.nop(nofuse=True)
                load_strip(c + 1, 1)
            load_w(0)
            load_strip(0, 0)
            load_strip(0, 1)
            sp.wait_ge(wlo_ok, 3)
            load_w(1)
            sp.wait_ge(cleared, 6)
            for h in range(2):
                sp.dma_start(slot_rows[NE * P:, 512 * h:512 * h + 512].rearrange("(t p) n -> p t n", p=P),
                             zeros.unsqueeze(1).broadcast_to([P, MT - NE, 512])).then_inc(rows_zero, 16)
            with sp.Fori(0, PAIRS - 2) as c:
                pair_dmas(c, False, True)
            pair_dmas(PAIRS - 2, False, False)
            pair_dmas(PAIRS - 1, True, False)
            sp.wait_ge(kv_out, 32 * PAIRS + 16)
            sp.wait_ge(rows_zero, 32)
            sp.wait_ge(sq_ok, 2 * PAIRS)
            sp.dma_start(new_k_s.rearrange("l b s h d -> (l b s) (h d)"), sqk[:, 1]).then_inc(kv_out, 16)
            sp.dma_start(new_v_s.rearrange("l b s h d -> (l b s) (h d)"), sqv).then_inc(kv_out, 16)
            stage_end(sp, 2)

            def load_cache(dst, src, b, s_in):
                sp.dma_start(dst[:, 0], src[b, 896:1024]).then_inc(s_in, 16)
                sp.dma_start(dst[0:96, 1], src[b, 512:896].rearrange("(n r) d -> n r d", r=4)[:, 0]).then_inc(s_in, 16)
                sp.dma_start(dst[96:128, 1], src[b, 0:512].rearrange("(n r) d -> n r d", r=16)[:, 0]).then_inc(s_in, 16)
            for b in range(NB):
                if b >= 2:
                    sp.wait_ge(sprod, b - 1)
                load_cache(kCb[b % 2], ck, b, kc_in[b % 2])
            for b in range(NB):
                load_cache(vC[b], cv, b, vc_in)
            sp.wait_ge(kv_out, 32 * PAIRS + 48)
            stage_end(sp, 3)

            def load_piece(e, p):
                if p < 4:
                    src = (wg_flat, wu_flat)[p // 2][bass.ds(e * D + (p % 2) * (D // 2), D // 2), :]
                else:
                    src = wd_flat[bass.ds(e * FF + (p % 2) * (FF // 2), FF // 2), :]
                n = FF if p < 4 else D
                sp.dma_start(stage[p % 3].rearrange("p (k n) -> p k n", n=n), src.rearrange("(k p) n -> p k n", p=P))\
                  .then_inc(piece_in[p % 3], 16)

            sp.dma_start(wO, w_o_v).then_inc(wO_in, 16)
            sp.dma_start(rw, router_w.rearrange("(k p) n -> p k n", p=P)).then_inc(wO_in, 16)
            for t in range(NT):
                if t >= 2:
                    sp.wait_ge(x1_ok, t - 1)
                sp.dma_start(xr[t % 2][0:rows_of(t)], xp[t * P:(t + 1) * P] if t < PT else xs).then_inc(x_in[t % 2], 16)
                if t >= 1:
                    sp.wait_ge(h2_ok, t)
                    sp.dma_start(h2_rows[(t - 1) * P:t * P], h2[(t - 1) % 2]).then_inc(h2_out[(t - 1) % 2], 16)
            sp.wait_ge(h2_ok, NT)
            sp.dma_start(h2_rows[S:TOK], h2[PT % 2][0:NB]).then_inc(h2_out[PT % 2], 16)
            for p in range(3):
                load_piece(0, p)
            sp.wait_ge(zero_ok, 1)
            sp.dma_start(slot_token.rearrange("(p n) a -> p (n a)", p=P), zero_i.bitcast(U32)).then_inc(st_zero, 16)
            sp.wait_ge(h2_out[0], 16 * ((NT + 1) // 2))
            sp.wait_ge(h2_out[1], 16 * (NT // 2))
            sp.wait_ge(st_zero, 16)
            stage_end(sp, 4)

            with sp.Fori(0, NE - 1) as e:
                for p in range(6):
                    sp.wait_ge(plo_ok, e * 6 + (p + 1))
                    sp.nop(nofuse=True)
                    load_piece(e + (p + 3) // 6, (p + 3) % 6)
            for p in range(3, 6):
                sp.wait_ge(plo_ok, (NE - 1) * 6 + p - 2)
                load_piece(NE - 1, p)
            stage_end(sp, 5)
            sp.dma_start(fng, final_norm_g.rearrange("(a n) -> a n", a=1).partition_broadcast(P)).then_inc(vec_in, 16)
            for t in range(NT):
                sp.wait_ge(y_ok, t + 1)
                sp.dma_start(yp[t * P:(t + 1) * P] if t < PT else ys, yA[t % 2][0:rows_of(t)]).then_inc(y_out[t % 2], 16)
            sp.wait_ge(y_out[0], 16 * ((NT + 1) // 2))
            sp.wait_ge(y_out[1], 16 * (NT // 2))

        @block.gpsimd
        def _(pool):
            pl = Steps(pool, pool_link)
            bc = Steps(pool, bc1_ok)
            pool.wait_ge(mod_ok, 2)
            bc.done(nc.gpsimd.partition_broadcast(bcA1, modrow(SC1)[32:33]), wait=False)
            bc.done(nc.gpsimd.partition_broadcast(bcS1, modrow(SH1)[32:33]), wait=False)
            stage_end(pool, 0)
            for t in range(PT):
                pool.wait_ge(att_cp, t + 1)
                v = attS[t % 2].rearrange("p (h n) -> p h n", h=HA)
                nc.gpsimd.affine_select(out=v, in_=v, pattern=[[0, HA], [1, P]], compare_op=ALU.is_ge, fill=0.0,
                                        base=0, channel_multiplier=-1).then_inc(att_ok, 1)
            stage_end(pool, 1)

            def keep_values(c):
                pool.wait_ge(oT_ps, c + 1)
                pool.wait_ge(qkv_ok, c * NT + NT)
                pool.nop(nofuse=True)
                nc.gpsimd.tensor_copy(vcur, qkv[:, 0:PT, 256:384]).then_inc(v_ok, 1)
            with pool.Fori(0, PAIRS - 1) as c:
                keep_values(c)
            keep_values(PAIRS - 1)
            stage_end(pool, 2)
            stage_end(pool, 3)
            b2 = Steps(pool, bc2_ok)
            b2.done(nc.gpsimd.partition_broadcast(bcG1, modrow(G1)[32:33]), wait=False)
            b2.done(nc.gpsimd.partition_broadcast(bcA2, modrow(SC2)[32:33]), wait=False)
            b2.done(nc.gpsimd.partition_broadcast(bcS2, modrow(SH2)[32:33]), wait=False)
            b2.done(nc.gpsimd.partition_broadcast(g2b, modrow(G2)[32:33]), wait=False)
            nc.gpsimd.memset(zero_i, 0.0).then_inc(zero_ok, 1)
            pool.wait_ge(st_zero, 16)
            pool.wait_ge(route_ok, 1)
            for t in range(NT):
                n = rows_of(t)
                for j in range(2):
                    nc.gpsimd.indirect_dma_start(
                        slot_token, bass.IndirectOffsetOnAxis(ap=ids[0:n, 2 * t + j:2 * t + j + 1], axis=0),
                        ids[0:n, 2 * NT + t:2 * NT + t + 1], None).then_inc(st_out, 16)
            pool.wait_ge(st_out, 32 * NT)
            stage_end(pool, 4)
            pool.wait_ge(route_ok, 1)
            tiles = pool.value_load(etab[0:1, NE:NE + 1], min_val=NE, max_val=MT)
            with pool.Fori(0, tiles + 1) as t:
                pool.wait_ge(xgT_ps, t + 1)
                pool.nop(nofuse=True)
                pool.dma_start(gidx[:], slot_token[bass.ds(t * P, P), :]).then_inc(gi_in, 16)
                pool.wait_ge(gi_in, t * 16 + 16)
                pool.nop(nofuse=True)
                nc.gpsimd.indirect_dma_start(
                    xg, None, h2_rows, bass.IndirectOffsetOnAxis(ap=gidx[:], axis=0)).then_inc(xg_in, 16)
            stage_end(pool, 5)
            for t in range(NT):
                n = rows_of(t)
                if t >= 2:
                    pool.wait_ge(y_out[t % 2], 16 * (t // 2))
                for j, dst in ((0, yA), (1, yB)):
                    nc.gpsimd.indirect_dma_start(
                        dst[t % 2][0:n], None, slot_rows,
                        bass.IndirectOffsetOnAxis(ap=ids[0:n, 2 * t + j:2 * t + j + 1], axis=0)).then_inc(ya_in[t % 2], 16)

        @block.scalar
        def _(act):
            lk = Steps(act, act_link)
            A = nc.scalar.activation
            eps = C("eps")

            act.wait_ge(const_in, 16)
            act.wait_ge(crow_in, 48)
            A(csig, crow, ACT.Exp, scale=-1.0).then_inc(neg_exp_c, 1)
            act.wait_ge(csT_ps, 1)
            A(csT.rearrange("p k m -> p (k m)"), bank(7, KC * 33), ACT.Copy).then_inc(csT_ok, 1)
            for t in range(NT):
                n = rows_of(t)
                act.wait_ge(x_in[t % 2], 16 * (t // 2 + 1))
                lk.done(A(sqj[0:n], xt[t % 2][0:n], ACT.Square, accum_out=ss[0:n, t:t + 1]))
                A(rs[0:n, t:t + 1], ss[0:n, t:t + 1], ACT.Sqrt, scale=1.0 / D, bias=eps[0:n]).then_inc(x_ssq, 1)
                if t >= 1:
                    act.wait_ge(hT_ps, t)
                    b = 2 * ((t - 1) % 2)
                    A(hTh[:, :, (t - 1) * P:t * P], banks[:, 512 * b:512 * b + 1024].rearrange("p (k n) -> p k n", k=KC),
                      ACT.Copy).then_inc(hT_hi, 1)
            act.wait_ge(hT_ps, NT)
            A(hTh[:, :, S:TOK], bank(2 * (PT % 2), KC * NB).rearrange("p (k n) -> p k n", k=KC), ACT.Copy).then_inc(hT_hi, 1)
            stage_end(act, 0)

            act.wait_ge(wG_in, 32)
            A(wGh, wG, ACT.Copy, scale=WS).then_inc(whi_ok, 1)
            for t in range(NT):
                n = rows_of(t)
                act.wait_ge(gproj_ps, t + 1)
                A(proj[0:n, t, 0:512], bank(4 + 2 * (t % 2), 512, n), ACT.Copy, scale=1.0 / WS).then_inc(gprojA, 1)
            act.wait_ge(z_ps, 1)
            z = banks[:, 0:D]
            lk.done(A(T1, z, ACT.Abs))
            lk.done(A(sT1, bank(2, P, NB), ACT.Abs))
            lk.done(A(T1, T1, ACT.Exp, scale=-1.0))
            lk.done(A(sT1, sT1, ACT.Exp, scale=-1.0))
            lk.done(A(T1, T1, ACT.Ln, bias=C("one")))
            A(sT1, sT1, ACT.Ln, bias=C("one", NB)).then_inc(lnz_ok, 1)
            act.wait_ge(cum_ps, 1)
            ed = Steps(act, edec_ok)
            ed.done(A(E[0], banks[:, 0:D], ACT.Exp), wait=False)
            ed.done(A(E[1], banks[:, 0:D], ACT.Exp, scale=-1.0), wait=False)
            ed.done(A(E[2], banks[:, 1024:1024 + D], ACT.Exp), wait=False)
            ed.done(A(E[3], banks[:, 2048:2048 + D], ACT.Exp), wait=False)
            ed.done(A(eblast, bank(6, PT), ACT.Exp), wait=False)
            ed.done(A(sA, sL, ACT.Exp), wait=False)
            act.wait_ge(gT_ps, 1)
            A(k2T, banks[:, 0:D], ACT.Copy).then_inc(k2T_ok, 1)
            for t in range(PT):
                act.wait_ge(att_ps, t + 1)
                if t >= 2:
                    act.wait_ge(og_ps, t - 1)
                A(attS[t % 2], bank(t % 2), ACT.Copy).then_inc(att_cp, 1)
                act.wait_ge(og_ps, t + 1)
                A(oG[:, t], bank(2 + t % 2, 256), ACT.Copy).then_inc(og_cp, 1)
            act.wait_ge(so_ps, 1)
            act.wait_ge(cleared, 5)
            A(oG[0:NB, PT], bank(0, 256, NB), ACT.Copy).then_inc(og_cp, 1)
            act.wait_ge(og_cp, NT)
            lk.done(A(tG.rearrange("p t n -> p (t n)"), oG.rearrange("p t n -> p (t n)"), ACT.Square))
            nc.scalar.sem_inc(osq_ok, 1)
            act.wait_ge(ossq_ok, 1)
            A(rs, ss, ACT.Sqrt, scale=1.0 / DV, bias=eps).then_inc(ostd_ok, 1)
            A(tG, proj[:, :, 528:784], ACT.Exp, scale=-1.0).then_inc(rexp_ok, 1)
            act.wait_ge(ogT_ps, 1)
            for c in range(2):
                lk.done(A(mixT[:, c, 0:S], banks[:, 1024 * c:1024 * c + D], ACT.Copy), wait=False)
                lk.done(A(mixT[:, c, S:TOK], bank(4 + c, NB), ACT.Copy), wait=False)
            stage_end(act, 1)

            nc.scalar.sem_inc(pair_act, 1)

            def split_high(c, j):
                act.wait_ge(wP_in, c * 48 + 48)
                k = slice(4 * j, 4 * j + 4)
                A(wPh[:, k].rearrange("p k (g n) -> p k g n", g=3), wP[:, k], ACT.Copy, scale=WS).then_inc(whi_ok, 1)

            def store_qkv(c, t, b):
                n = rows_of(t)
                act.wait_ge(qkv_ps, c * NT + (t + 1))
                A(qkv[0:n, t], bank(b, 384, n), ACT.Copy, scale=1.0 / WS).then_inc(qkv_ok, 1)

            def store_kT(c):
                act.wait_ge(qkT_ps, c + 1)
                A(kT, banks[:, 1024:2048], ACT.Copy).then_inc(kT_ok, 1)

            def attend(c, last):
                act.wait_ge(qkv_ok, c * NT + NT)
                qs_ = qkv[0:NB, PT].rearrange("p (g n) -> p g n", g=3)
                A(sqk[:, :, bass.ds(c * P, P)], qs_[:, 0:2], ACT.Copy).then_inc(sq_ok, 1)
                A(sqv[:, bass.ds(c * P, P)], qs_[:, 2], ACT.Copy).then_inc(sq_ok, 1)

                def exp_tile(a):
                    n = (a % PT + 1) * P
                    act.wait_ge(m_ok, c * 16 + (a + 1))
                    if a >= 2:
                        act.wait_ge(pt_ps, c * 16 + (a - 1))
                    A(pB[a % 2][:, 0:n], sB[a % 2][:, 0:n], ACT.Exp, bias=nmx[:, a % 2:a % 2 + 1],
                      accum_out=den[:, a:a + 1]).then_inc(p_ok, 1)
                exp_tile(0)
                for a in range(16):
                    if a < 15:
                        exp_tile(a + 1)
                    n = min(a % PT + 1, 4) * P
                    act.wait_ge(pt_ps, c * 16 + (a + 1))
                    if a >= 2:
                        act.wait_ge(o_ps, c * 16 + (a - 1))
                    A(pTB[a % 2][:, 0:n], bank(4, n), ACT.Copy).then_inc(pt0_ok, 1)
                    if not last:
                        if a < 2:
                            split_high(c + 1, a)
                        if a in STEP_PROJ and 1 in STEP_PROJ[a][1]:
                            t = STEP_PROJ[a][0]
                            if t == 0:
                                act.wait_ge(v_ok, c + 1)
                                act.wait_ge(sq_ok, c * 2 + 2)
                                act.wait_ge(kv_out, c * 32 + 48)
                            store_qkv(c + 1, t, 7)
                if not last:
                    store_kT(c + 1)
                act.wait_ge(oT_ps, c + 2)
                A(mixT[:, bass.ds(c + 2, 1), 0:512].rearrange("p a (t n) -> p (a t) n", t=4),
                  bank(4).rearrange("p (t n) -> p t n", t=4)[:, :, ::-1], ACT.Copy).then_inc(pair_act, 1)
            split_high(0, 0)
            split_high(0, 1)
            for t in range(NT):
                store_qkv(0, t, t % 4)
            store_kT(0)
            with act.Fori(0, PAIRS - 1) as c:
                attend(c, False)
            attend(PAIRS - 1, True)
            stage_end(act, 2)

            act.wait_ge(smax_ok, 1)
            A(srow, srow, ACT.Exp, bias=V(o_stat + 1, 1, NB * HD), accum_out=V(o_stat + 2, 1, NB * HD)).then_inc(sexp_ok, 1)
            act.wait_ge(spT_ps, 1)
            lk.done(A(spT.rearrange("p c n -> p (c n)"), bank(6, 192), ACT.Copy), wait=False)
            A(pselfT, bank(7, NB * HD, NB), ACT.Copy).then_inc(spT_ok, 1)
            stage_end(act, 3)

            for t in range(NT):
                n = rows_of(t)
                act.wait_ge(x1_ok, t + 1)
                lk.done(A(sqj2[0:n], X1[0:n, t], ACT.Square, accum_out=ss[0:n, t:t + 1]))
                A(rs[0:n, t:t + 1], ss[0:n, t:t + 1], ACT.Sqrt, scale=1.0 / D, bias=eps[0:n]).then_inc(x1_std, 1)
                act.wait_ge(h2T_ps, t + 1)
                if t >= 1:
                    act.wait_ge(lr_ps, t)
                w = n
                A(h2T[:, :, 0:w], banks[:, 2048:2048 + KC * w].rearrange("p (k n) -> p k n", k=KC), ACT.Copy).then_inc(h2T_ok, 1)
            act.wait_ge(lr_ps, NT)
            A(sco[:, 0:PT * NE], bank(6, PT * NE), ACT.Exp, scale=-1.0).then_inc(rexp2, 1)
            act.wait_ge(cleared, 7)
            A(sco[0:NB, PT * NE:RE], bank(7, NE, NB), ACT.Exp, scale=-1.0).then_inc(rexp2, 1)
            stage_end(act, 4)

            nc.scalar.sem_inc(yA_cp, 1)
            nc.scalar.sem_inc(yrow_out, 16)
            act.wait_ge(route_ok, 1)

            def split_piece(e, s, p):
                act.wait_ge(piece_in[p % 3], e * 32 + 16 * (p // 3 + 1))
                A(w_hi[s][p // 2][:, (p % 2) * PIECE:(p % 2 + 1) * PIECE], stage[p % 3], ACT.Copy, scale=WS).then_inc(phi_ok, 1)

            def high_rows(t):
                act.wait_ge(xgT_ps, t + 2)
                A(xgTh.rearrange("p k n -> p (k n)"), banks[:, 0:D], ACT.Copy).then_inc(xgT_hi, 1)

            def tile(t, split):
                act.wait_ge(g_ps, t + 1)
                A(sg, bank(2), ACT.Exp, scale=-1.0 / WS).then_inc(gexp_ok, 1)
                split(0)
                split(1)
                act.wait_ge(hidT_ps, t + 2)
                A(hidTh.rearrange("p k n -> p (k n)"), bank(4), ACT.Copy).then_inc(hidT_hi, 1)
                high_rows(t + 1)
                split(2)
                split(3)
                act.wait_ge(y_ps, t + 1)
                act.wait_ge(yrow_out, t * 16 + 16)
                A(yM[:, 0:512], bank(5), ACT.Copy, scale=1.0 / WS).then_inc(yA_cp, 1)
                act.wait_ge(yA_cp, t + 2)
                act.wait_ge(yB_cp, t + 2)
                act.dma_start(slot_rows[bass.ds(t * P, P), :], yM).then_inc(yrow_out, 16)
                split(4)
                split(5)

            def expert(e, s, last):
                start = act.value_load(etab[0:1, bass.ds(e, 1)], min_val=0, max_val=MT - 1)
                end = act.value_load(etab[0:1, bass.ds(e + 1, 1)], min_val=1, max_val=MT)
                tile(start, (lambda p: None) if last else (lambda p: split_piece(e + 1, 1 - s, p)))
                with act.If(end - start - 1):
                    with act.Fori(start + 1, end) as t:
                        tile(t, lambda p: None)
            for p in range(6):
                split_piece(0, 0, p)
            high_rows(0)
            with act.Fori(0, NE // 2 - 1) as i:
                expert(i * 2, 0, False)
                expert(i * 2 + 1, 1, False)
            expert(NE - 2, 0, False)
            expert(NE - 1, 1, True)
            act.wait_ge(yrow_out, act.value_load(etab[0:1, NE:NE + 1], min_val=NE, max_val=MT) * 16 + 16)
            act.nop(nofuse=True)
            stage_end(act, 5)
            for t in range(NT):
                n = rows_of(t)
                act.wait_ge(x2_ok, t + 1)
                lk.done(A(sqj3[0:n], X1[0:n, t], ACT.Square, accum_out=ss[0:n, t:t + 1]))
                A(rs[0:n, t:t + 1], ss[0:n, t:t + 1], ACT.Sqrt, scale=1.0 / D, bias=eps[0:n]).then_inc(x2_std, 1)

        @block.vector
        def _(dve):
            v = nc.vector
            lk = Steps(dve, dve_link)
            cl = Steps(dve, cleared)
            cl.done(v.memset(crow, 0.0), wait=False)
            cl.done(v.memset(arena[32:33, o_relx:o_relx + HD], 1.0), wait=False)
            cl.done(v.memset(V(A_HT, TOK, 32), 0.0), wait=False)
            dve.wait_ge(neg_exp_c, 1)
            lk.done(v.tensor_scalar(csig, csig, 1.0, None, ALU.add))
            lk.done(v.reciprocal(csig, csig))
            v.tensor_tensor(crow, crow, csig, ALU.mult).then_inc(silu_c, 1)
            dve.wait_ge(crow_in, 48)
            bo = Steps(dve, bias_ok)
            v.tensor_copy(relr.rearrange("p (b h) -> p b h", b=NB), relx.unsqueeze(1).broadcast_to([33, NB, HD]))\
             .then_inc(bias_ps, 1)
            dve.wait_ge(bias_ps, 2)
            bo.done(v.tensor_copy(bias_rows[:, 0:D], banks[0:HD, 0:D]), wait=False)
            bo.done(v.tensor_copy(bias_rows[:, D:GN], banks[0:HD, D:GN]), wait=False)
            bo.done(v.tensor_copy(sbias, banks[0:NB * HD, 1536:1536 + CK + 1]), wait=False)
            ad = Steps(dve, ada_added)
            with dve.Fori(0, 4) as i:
                ad.enter(i, 3)
                for s in range(3):
                    dve.wait_ge(ada_ps, i * 3 + (s + 1))
                    ad.done(v.tensor_tensor(mod[:, bass.ds(i * 1536 + s * 512, 512)], bank(4 + s, 512, 33), ba[s], ALU.add), wait=False)
                ad.leave(4)
            dve.wait_ge(ada_added, 12)
            dve.wait_ge(vec_in, 96)
            mo = Steps(dve, mod_ok)
            mo.done(v.scalar_tensor_tensor(out=modrow(SC1), in0=modrow(SC1), scalar=1.0, in1=nrm[:, 0:D], op0=ALU.add, op1=ALU.mult))
            mo.done(v.scalar_tensor_tensor(out=modrow(SC2), in0=modrow(SC2), scalar=1.0, in1=nrm[:, D:2 * D], op0=ALU.add, op1=ALU.mult))
            def low_hT(t):
                n, b = rows_of(t), 2 * (t % 2)
                dve.wait_ge(hT_hi, t + 1)
                v.tensor_tensor(hTl[:, :, t * P:t * P + n], banks[:, 512 * b:512 * b + KC * n].rearrange("p (k n) -> p k n", k=KC),
                                hTh[:, :, t * P:t * P + n], ALU.subtract).then_inc(hT_ok, 1)
            for t in range(NT):
                n = rows_of(t)
                x = xt[t % 2][0:n]
                dve.wait_ge(x_ssq, t + 1)
                lk.done(v.reciprocal(rs[0:n, t:t + 1], rs[0:n, t:t + 1]))
                if t == 0:
                    dve.wait_ge(bc1_ok, 2)
                ga, sh = (bcA1, bcS1) if t < PT else (modrow(SC1, NB), modrow(SH1, NB))
                lk.done(v.scalar_tensor_tensor(out=x, in0=x, scalar=rs[0:n, t:t + 1], in1=ga, op0=ALU.mult, op1=ALU.mult))
                v.tensor_tensor(x, x, sh, ALU.add).then_inc(h_ok, 1)
                if t >= 1:
                    low_hT(t - 1)
            low_hT(PT)
            stage_end(dve, 0)

            cl.done(v.memset(proj[:, PT], 0.0), wait=False)
            lk.done(v.memset(glT, 1.0), wait=False)
            lk.done(v.memset(state[0], 0.0), wait=False)
            dve.wait_ge(cleared, 4)
            dve.wait_ge(whi_ok, 1)
            v.scalar_tensor_tensor(out=wGl, in0=wG, scalar=WS, in1=wGh, op0=ALU.mult, op1=ALU.subtract).then_inc(wlo_ok, 1)
            for t in range(NT):
                n = rows_of(t)
                dve.wait_ge(gproj_ps, t + 1)
                v.tensor_scalar(proj[0:n, t, 512:GW], bank(5 + 2 * (t % 2), GW - 512, n), 1.0 / WS, None, ALU.mult).then_inc(gprojB, 1)
            lk.done(v.memset(blkq[0], 0.0), wait=False)
            lk.done(v.memset(blkq[1], 0.0), wait=False)
            lk.done(v.memset(qz, 0.0), wait=False)
            cl.done(v.memset(oG[:, PT], 0.0), wait=False)
            dve.wait_ge(gl_ps, 1)
            dve.wait_ge(dve_link, lk.n)
            lk.done(v.tensor_copy(glT[0:RANK, 0:S], banks[0:RANK, 0:S]), wait=False)
            v.tensor_copy(glT[0:RANK, S:TOK], bank(2, NB, RANK)).then_inc(gl_ok, 1)
            dve.wait_ge(gl_ok, 1)
            dve.wait_ge(dve_link, lk.n)
            nc.vector.sem_inc(gl_ok, 1)
            dve.wait_ge(lnz_ok, 1)
            lk.done(v.tensor_scalar(L, banks[:, 0:D], 0.0, 1.0 / 16, ALU.min, ALU.mult), wait=False)
            lk.done(v.tensor_scalar(sL, bank(2, P, NB), 0.0, 1.0 / 16, ALU.min, ALU.mult))
            lo = Steps(dve, loga_ok)
            lo.done(v.scalar_tensor_tensor(out=L, in0=T1, scalar=-1.0 / 16, in1=L, op0=ALU.mult, op1=ALU.add))
            lo.done(v.scalar_tensor_tensor(out=sL, in0=sT1, scalar=-1.0 / 16, in1=sL, op0=ALU.mult, op1=ALU.add))
            E3 = [e.rearrange("p (t n) -> p t n", t=PT) for e in E]
            qv, kv = proj[:, 0:PT, 0:P], proj[:, 0:PT, P:2 * P]
            so = Steps(dve, scaled_ok)
            for n_, (e, src, is_q) in enumerate(((0, qv, 1), (1, kv, 0), (2, kv, 0), (3, qv, 1))):
                dve.wait_ge(edec_ok, e + 1)
                if is_q:
                    so.done(v.scalar_tensor_tensor(out=E3[e], in0=src, scalar=DK ** -0.5, in1=E3[e], op0=ALU.mult, op1=ALU.mult), wait=False)
                else:
                    so.done(v.tensor_tensor(E3[e], src, E3[e], ALU.mult), wait=False)
            dve.wait_ge(gT_ps, 1)
            v.tensor_copy(q4T, banks[:, 1024:1024 + D]).then_inc(q4T_ok, 1)
            nc.vector.sem_inc(state_ok, 1)
            dve.wait_ge(edec_ok, 5)
            for t in range(PT):
                if t >= 2:
                    dve.wait_ge(att_ps, t - 1)
                for h in range(HA):
                    lk.done(v.tensor_copy(blkq[t % 2][32 * h:32 * h + 32, P * h:P * h + P],
                                          banks[32 * h:32 * h + 32, 2048 + t * P:2048 + t * P + P]), wait=False)
                dve.wait_ge(dve_link, lk.n)
                nc.vector.sem_inc(blk_ok, 1)
                dve.wait_ge(ds_ps, t + 1)
                lk.done(v.tensor_tensor(dstate, bank(7, 256), C("blk"), ALU.mult))
                if t >= 1:
                    dve.wait_ge(og_ps, t)
                v.scalar_tensor_tensor(out=state[(t + 1) % 2], in0=state[t % 2], scalar=eblast[:, t:t + 1], in1=dstate,
                                       op0=ALU.mult, op1=ALU.add).then_inc(state_ok, 1)
                dve.wait_ge(state_ok, t + 2)
            dve.wait_ge(sc3_ps, 1)
            v.tensor_copy(sc3, bank(0, 3 * NB)).then_inc(sc3_ok, 1)
            dve.wait_ge(sc3_ok, 1)
            lk.done(v.tensor_tensor(kz, proj[0:NB, PT, P:2 * P].unsqueeze(1).broadcast_to([NB, NB, P]),
                                    ident[0:NB, 0:NB].unsqueeze(2).broadcast_to([NB, NB, P]), ALU.mult))
            qzv = qz.rearrange("p (h n) -> p h n", h=HA)
            for h in range(HA):
                lk.done(v.tensor_scalar(qzv[32 * h:32 * h + 32, h, 0:64:9], sc3[32 * h:32 * h + 32, 2 * NB:3 * NB], DK ** -0.5, None, ALU.mult))
            nc.vector.sem_inc(sc3_ok, 1)
            dve.wait_ge(wG_in, 32)
            sn = Steps(dve, snew_ok)
            sn.done(v.tensor_tensor(sS, sS, sc3[:, 0:NB].unsqueeze(2).broadcast_to([P, NB, DV]), ALU.mult))
            dve.wait_ge(kv_ps, 1)
            kvp = banks[:, 2048:4096].rearrange("p (b n) -> p b n", b=NB)
            for h in range(HA):
                r = slice(32 * h, 32 * h + 32)
                sn.done(v.tensor_tensor(sS[r], sS[r], kvp[r, :, DV * h:DV * h + DV], ALU.add), wait=False)
            dve.wait_ge(osq_ok, 1)
            v.tensor_reduce(ss, tG.rearrange("p t (h n) -> p (t h) n", h=HA), AX_X, ALU.add).then_inc(ossq_ok, 1)
            dve.wait_ge(ostd_ok, 1)
            lk.done(v.reciprocal(rs, rs))
            o4 = oG.rearrange("p t (h n) -> p (t h) n", h=HA)
            lk.done(v.tensor_tensor(o4, o4, rs.unsqueeze(2).broadcast_to([P, NT * HA, DV]), ALU.mult))
            lk.done(v.tensor_tensor(oG, oG, gng.unsqueeze(1).broadcast_to([P, NT, HA * DV]), ALU.mult))
            dve.wait_ge(rexp_ok, 1)
            lk.done(v.tensor_scalar(tG, tG, 1.0, None, ALU.add))
            lk.done(v.reciprocal(tG, tG))
            lk.done(v.tensor_tensor(tG, tG, proj[:, :, 528:784], ALU.mult))
            v.tensor_tensor(oG, oG, tG, ALU.mult).then_inc(og_ok, 1)
            stage_end(dve, 1)

            nc.vector.sem_inc(pair_dve, 1)
            cl.done(v.memset(zeros, 0.0), wait=False)

            def split_low(c, j):
                dve.wait_ge(whi_ok, c * 2 + (j + 2))
                k = slice(4 * j, 4 * j + 4)
                v.scalar_tensor_tensor(out=wPl[:, k].rearrange("p k n -> p (k n)"), in0=wP[:, k].rearrange("p k g n -> p (k g n)"),
                                       scalar=WS, in1=wPh[:, k].rearrange("p k n -> p (k n)"), op0=ALU.mult,
                                       op1=ALU.subtract).then_inc(wlo_ok, 1)

            def store_qT(c):
                dve.wait_ge(qkT_ps, c + 1)
                v.tensor_scalar(qT.rearrange("p (t n) -> p t n", t=PT)[:, :, ::-1],
                                banks[:, 0:1024].rearrange("p (t n) -> p t n", t=PT), DH ** -0.5, None,
                                ALU.mult).then_inc(qT_ok, 1)

            def attend(c, last):
                def bias_max(a):
                    hh, i = a // PT, a % PT
                    n = (i + 1) * P
                    b = 2 * (a % 2)
                    dve.wait_ge(s_ps, c * 16 + (a + 1))
                    if i == 0:
                        dve.wait_ge(strip_in[hh], c * 16 + 16)
                    if a >= 2:
                        dve.wait_ge(p_ok, c * 16 + (a - 1))
                    dve.nop(nofuse=True)
                    v.tensor_tensor_reduce(sB[a % 2][:, 0:n], banks[:, 512 * b:512 * b + n], strip[:, hh, P * (PT - 1 - i):D],
                                           1.0, -3e38, ALU.add, ALU.max, mx[:, a % 2:a % 2 + 1]).then_inc(s_read, 1)
                    dve.wait_ge(s_read, c * 16 + (a + 1))
                    v.tensor_scalar(nmx[:, a % 2:a % 2 + 1], mx[:, a % 2:a % 2 + 1], -1.0, None, ALU.mult).then_inc(m_ok, 1)

                def scale_out(a):
                    hh, i = a // PT, a % PT
                    dve.wait_ge(p_ok, c * 16 + (a + 1))
                    lk.done(v.reciprocal(rden[:, a:a + 1], den[:, a:a + 1]))
                    dve.wait_ge(o_ps, c * 16 + (a + 1))
                    v.tensor_scalar(oB[:, i, DH * hh:DH * hh + DH], bank(6, DH), rden[:, a:a + 1], None,
                                    ALU.mult).then_inc(o_ok, 1)
                bias_max(0)
                for a in range(16):
                    if a < 15:
                        if a >= 1:
                            dve.wait_ge(m_ok, c * 16 + (a + 1) - 1)
                        bias_max(a + 1)
                    if a >= 1:
                        scale_out(a - 1)
                    nb = a % PT + 1 - 4
                    if nb > 0:
                        dve.wait_ge(pt_ps, c * 16 + (a + 1))
                        if a >= 2:
                            dve.wait_ge(o_ps, c * 16 + (a - 1))
                        v.tensor_copy(pTB[a % 2][:, 512:512 + nb * P], bank(5, nb * P)).then_inc(pt1_ok, 1)
                    if a in (1, 2) and not last:
                        split_low(c + 1, a - 1)
                scale_out(15)
                if not last:
                    store_qT(c + 1)
                dve.wait_ge(oT_ps, c + 2)
                v.tensor_copy(mixT[:, bass.ds(c + 2, 1), 512:1024].rearrange("p a (t n) -> p (a t) n", t=4),
                              bank(5).rearrange("p (t n) -> p t n", t=4)[:, :, ::-1]).then_inc(pair_dve, 1)
            split_low(0, 0)
            split_low(0, 1)
            store_qT(0)
            with dve.Fori(0, PAIRS - 1) as c:
                lk.enter(c, 16)
                attend(c, False)
                lk.leave(PAIRS - 1)
            attend(PAIRS - 1, True)
            stage_end(dve, 2)

            v.tensor_copy(ohb, ident[0:NB, 0:NB].unsqueeze(2).broadcast_to([NB, NB, P])).then_inc(ohb_ok, 1)
            lk.done(v.tensor_tensor(selfp, sqk[:, 0], sqk[:, 1], ALU.mult))
            lk.done(v.tensor_reduce(selfl, selfp.rearrange("p (h d) -> p h d", h=HD), AX_X, ALU.add))
            v.tensor_tensor(selfd.rearrange("p (b h) -> p b h", b=NB), selfl.unsqueeze(1).broadcast_to([NB, NB, HD]),
                            C("diag8", NB).rearrange("p (b h) -> p b h", b=NB), ALU.mult).then_inc(selfd_ok, 1)
            for b in range(NB):
                dve.wait_ge(kc_in[b % 2], 48 * (b // 2 + 1))
                dve.wait_ge(qb_ps, b + 1)
                if b >= 1:
                    dve.wait_ge(slog_ok, b)
                q = banks[:, 1024 * (b % 2):1024 * (b % 2) + QW]
                v.tensor_tensor(prod.rearrange("p (c n) -> p c n", c=2), kCb[b % 2], q.unsqueeze(1).broadcast_to([P, 2, QW]),
                                ALU.mult).then_inc(sprod, 1)
                dve.wait_ge(sprod, b + 1)
                v.tensor_reduce(lg[:, :, HD * b:HD * b + HD], prod.rearrange("p (c h d) -> p c h d", c=2, h=HD), AX_X,
                                ALU.add).then_inc(slog_ok, 1)
            dve.wait_ge(slT_ps, 1)
            n = NB * HD
            lk.done(v.scalar_tensor_tensor(out=srow[:, 0:CK], in0=bank(4, CK, n), scalar=DH ** -0.5, in1=sbias[:, 0:CK],
                                           op0=ALU.mult, op1=ALU.add), wait=False)
            lk.done(v.scalar_tensor_tensor(out=srow[:, CK:CK + 1], in0=bank(5, 1, n), scalar=DH ** -0.5,
                                           in1=sbias[:, CK:CK + 1], op0=ALU.mult, op1=ALU.add))
            st = [V(o_stat + i, 1, n) for i in range(4)]
            lk.done(v.tensor_reduce(st[0], srow, AX_X, ALU.max))
            v.tensor_scalar(st[1], st[0], -1.0, None, ALU.mult).then_inc(smax_ok, 1)
            dve.wait_ge(sexp_ok, 1)
            lk.done(v.reciprocal(st[3], st[2]))
            lk.done(v.tensor_scalar(srow, srow, st[3], None, ALU.mult))
            v.tensor_tensor(pself, srow[:, CK:CK + 1].broadcast_to([n, NB]), C("seq8", n), ALU.mult).then_inc(sp_ok, 1)
            dve.wait_ge(sov_ps, 1)
            so3 = bank(0, 96).rearrange("p (c b j) -> p c b j", c=PAIRS, b=NB)
            lk.done(v.tensor_copy(mixT[0:64, 2:KC, S:TOK], so3[0:64, :, :, 0]), wait=False)
            v.tensor_copy(mixT[64:128, 2:KC, S:TOK], so3[64:128, :, :, 1]).then_inc(smix_ok, 1)
            stage_end(dve, 3)

            for t in range(NT):
                n = rows_of(t)
                dve.wait_ge(op_ps, t + 1)
                if t == 0:
                    dve.wait_ge(bc2_ok, 4)
                dve.wait_ge(x_in[t % 2], 16 * (X_LOADS[t % 2] + t // 2 + 1))
                g, ga, sh = (bcG1, bcA2, bcS2) if t < PT else (modrow(G1, NB), modrow(SC2, NB), modrow(SH2, NB))
                b = 2 * (t % 2)
                lk.done(v.tensor_tensor(X1[0:n, t], banks[0:n, 512 * b:512 * b + D], g, ALU.mult))
                v.tensor_tensor(X1[0:n, t], X1[0:n, t], xr[t % 2][0:n], ALU.add).then_inc(x1_ok, 1)
                dve.wait_ge(x1_std, t + 1)
                lk.done(v.reciprocal(rs[0:n, t:t + 1], rs[0:n, t:t + 1]))
                if t >= 2:
                    dve.wait_ge(h2_out[t % 2], 16 * (t // 2))
                    dve.wait_ge(h2T_ps, t - 1)
                h = h2[t % 2][0:n]
                lk.done(v.scalar_tensor_tensor(out=h, in0=X1[0:n, t], scalar=rs[0:n, t:t + 1], in1=ga, op0=ALU.mult, op1=ALU.mult))
                v.tensor_tensor(h, h, sh, ALU.add).then_inc(h2_ok, 1)
                dve.wait_ge(h2_ok, t + 1)
            cl.done(v.memset(sco[:, PT * NE:RE], 1.0), wait=False)
            v4 = lambda a: a.rearrange("p (t g e) -> p (t g) e", t=NT, g=NG)
            v3 = lambda a: a.rearrange("p (t e) -> p t e", t=NT)
            bcE = lambda a, k: a.unsqueeze(2).broadcast_to([P, a.shape[1], k])
            dve.wait_ge(rexp2, 2)
            lk.done(v.tensor_scalar(sco, sco, 1.0, None, ALU.add))
            lk.done(v.reciprocal(sco, sco))
            lk.done(v.tensor_tensor(v3(sel), v3(sco), V(o_rb, NE).unsqueeze(1).broadcast_to([P, NT, NE]), ALU.add))
            p6 = pair6.rearrange("p (g j) -> p g j", j=6)
            s4 = v4(sel)
            lk.done(v.tensor_tensor(p6[:, :, 0:3], s4[:, :, 0:3], s4[:, :, 1:4], ALU.add), wait=False)
            lk.done(v.tensor_tensor(p6[:, :, 3:5], s4[:, :, 0:2], s4[:, :, 2:4], ALU.add), wait=False)
            lk.done(v.tensor_tensor(p6[:, :, 5:6], s4[:, :, 0:1], s4[:, :, 3:4], ALU.add))
            lk.done(v.tensor_reduce(gsc, p6, AX_X, ALU.max))
            g3 = lambda a: a.rearrange("p (t g) -> p t g", t=NT)
            prio_g = C("gprio").unsqueeze(1).broadcast_to([P, NT, NG])
            prio_e = C("eprio").unsqueeze(1).broadcast_to([P, NT, NE])
            lk.done(v.tensor_reduce(gm, g3(gsc), AX_X, ALU.max))
            lk.done(v.tensor_tensor(g3(gsel), g3(gsc), bcE(gm, NG), ALU.is_equal))
            lk.done(v.tensor_tensor(g3(gsel), g3(gsel), prio_g, ALU.mult))
            lk.done(v.tensor_reduce(gm, g3(gsel), AX_X, ALU.max))
            lk.done(v.tensor_tensor(g3(gsel), bcE(gm, NG), prio_g, ALU.is_equal))
            lk.done(v.tensor_tensor(v4(msel), v4(sel), bcE(gsel, PG), ALU.mult))
            lk.done(v.tensor_scalar(gsel, gsel, 1.0, 1e30, ALU.subtract, ALU.mult))
            lk.done(v.tensor_tensor(v4(msel), v4(msel), bcE(gsel, PG), ALU.add))
            for one in (one1, one2):
                lk.done(v.tensor_reduce(gm, v3(msel), AX_X, ALU.max))
                lk.done(v.tensor_tensor(v3(tA), v3(msel), bcE(gm, NE), ALU.is_equal))
                lk.done(v.tensor_tensor(v3(tA), v3(tA), prio_e, ALU.mult))
                lk.done(v.tensor_reduce(gm, v3(tA), AX_X, ALU.max))
                lk.done(v.tensor_tensor(v3(one), bcE(gm, NE), prio_e, ALU.is_equal))
                if one is one1:
                    lk.done(v.tensor_scalar(tA, one, -2e30, None, ALU.mult))
                    lk.done(v.tensor_tensor(msel, msel, tA, ALU.add))
            bt = Steps(dve, both_ok)
            lk.done(v.tensor_tensor(both, one1, one2, ALU.add))
            lk.done(v.tensor_scalar(both[:, PT * NE:RE], both[:, PT * NE:RE], C("srows"), None, ALU.mult))
            nc.vector.sem_inc(both_ok, 1)
            w12v = w12.rearrange("p (t j) -> p t j", j=2)
            for j, one in enumerate((one1, one2)):
                lk.done(v.tensor_tensor(tA, sco, one, ALU.mult))
                lk.done(v.tensor_reduce(w12v[:, :, j:j + 1], v3(tA), AX_X, ALU.add))
            lk.done(v.tensor_reduce(gm, w12v, AX_X, ALU.add))
            lk.done(v.reciprocal(gm, gm))
            lk.done(v.tensor_tensor(w12v, w12v, bcE(gm, 2), ALU.mult))
            dve.wait_ge(rank_ps, 1)
            lk.done(v.tensor_copy(rank, bank(0, RE)), wait=False)
            lk.done(v.tensor_copy(cnt, bank(1, RE)), wait=False)
            lk.done(v.memset(base[:, 0:NE], 0.0))
            for t in range(PT):
                lk.done(v.tensor_tensor(base[:, (t + 1) * NE:(t + 2) * NE], base[:, t * NE:(t + 1) * NE], cnt[:, t * NE:(t + 1) * NE], ALU.add))
            lk.done(v.tensor_tensor(nE, base[:, PT * NE:RE], cnt[:, PT * NE:RE], ALU.add))
            c9 = cmp9.rearrange("p (e t) -> p e t", e=NE)
            lk.done(v.tensor_tensor(c9, bcE(nE, NT), C("thr").unsqueeze(1).broadcast_to([P, NE, NT]), ALU.is_gt))
            lk.done(v.tensor_reduce(tE, c9, AX_X, ALU.add))
            lk.done(v.tensor_scalar(tE, tE, 1.0, None, ALU.max))
            cE = cmpE.rearrange("p (e f) -> p e f", e=NE)
            lk.done(v.tensor_tensor(cE, tE.unsqueeze(1).broadcast_to([P, NE, NE]), C("before").rearrange("p (e f) -> p e f", e=NE), ALU.mult))
            lk.done(v.tensor_reduce(offE, cE, AX_X, ALU.add))
            lk.done(v.tensor_tensor(rank, rank, base, ALU.add))
            lk.done(v.tensor_scalar(nE, offE, float(P), None, ALU.mult))
            lk.done(v.tensor_tensor(v3(rank), v3(rank), nE.unsqueeze(1).broadcast_to([P, NT, NE]), ALU.add))
            sl = slotf.rearrange("p (t j) -> p t j", j=2)
            for j, one in enumerate((one1, one2)):
                lk.done(v.tensor_tensor(tA, rank, one, ALU.mult))
                lk.done(v.tensor_reduce(sl[:, :, j:j + 1], v3(tA), AX_X, ALU.add))
            lk.done(v.tensor_copy(ids[:, 0:2 * NT], slotf))
            lk.done(v.tensor_copy(ids[:, 2 * NT:3 * NT], C("tokid")))
            lk.done(v.tensor_copy(etab[0:1, 0:NE], offE[0:1]))
            lk.done(v.tensor_tensor(offE, offE, tE, ALU.add))
            v.tensor_copy(etab[0:1, NE:NE + 1], offE[0:1, NE - 1:NE]).then_inc(route_ok, 1)
            stage_end(dve, 4)

            nc.vector.sem_inc(yB_cp, 1)
            dve.wait_ge(route_ok, 1)
            first_link = lk.n

            def split_piece(e, s, p):
                dve.wait_ge(phi_ok, e * 6 + (p + 1))
                part = slice((p % 2) * PIECE, (p % 2 + 1) * PIECE)
                v.scalar_tensor_tensor(out=w_lo[s][p // 2][:, part], in0=stage[p % 3], scalar=WS,
                                       in1=w_hi[s][p // 2][:, part], op0=ALU.mult, op1=ALU.subtract).then_inc(plo_ok, 1)

            def low_rows(t):
                dve.wait_ge(xgT_hi, t + 1)
                v.tensor_tensor(xgTl.rearrange("p k n -> p (k n)"), banks[:, 0:D], xgTh.rearrange("p k n -> p (k n)"),
                                ALU.subtract).then_inc(xgT_ok, 1)

            def tile(t, split):
                lk.n = first_link
                lk.enter(t, 3)
                dve.wait_ge(gexp_ok, t + 1)
                lk.done(v.tensor_scalar(sg, sg, 1.0, None, ALU.add))
                lk.done(v.reciprocal(sg, sg))
                lk.done(v.tensor_tensor(sg, sg, bank(2), ALU.mult))
                split(0)
                dve.wait_ge(u_ps, t + 1)
                dve.wait_ge(hidT_ps, t + 1)
                v.scalar_tensor_tensor(out=hid, in0=sg, scalar=1.0 / (WS * WS), in1=bank(3), op0=ALU.mult,
                                       op1=ALU.mult).then_inc(hid_ok, 1)
                split(1)
                dve.wait_ge(hidT_hi, t + 1)
                v.tensor_tensor(hidTl.rearrange("p k n -> p (k n)"), bank(4), hidTh.rearrange("p k n -> p (k n)"),
                                ALU.subtract).then_inc(hidT_ok, 1)
                low_rows(t + 1)
                split(2)
                split(3)
                dve.wait_ge(y_ps, t + 1)
                dve.wait_ge(yrow_out, t * 16 + 16)
                v.tensor_scalar(yM[:, 512:D], bank(6), 1.0 / WS, None, ALU.mult).then_inc(yB_cp, 1)
                split(4)
                split(5)

            def expert(e, s, last):
                start = dve.value_load(etab[0:1, bass.ds(e, 1)], min_val=0, max_val=MT - 1)
                end = dve.value_load(etab[0:1, bass.ds(e + 1, 1)], min_val=1, max_val=MT)
                tile(start, (lambda p: None) if last else (lambda p: split_piece(e + 1, 1 - s, p)))
                with dve.If(end - start - 1):
                    with dve.Fori(start + 1, end) as t:
                        tile(t, lambda p: None)
            for p in range(6):
                split_piece(0, 0, p)
            low_rows(0)
            with dve.Fori(0, NE // 2 - 1) as i:
                expert(i * 2, 0, False)
                expert(i * 2 + 1, 1, False)
            expert(NE - 2, 0, False)
            expert(NE - 1, 1, True)
            stage_end(dve, 5)
            lk = Steps(dve, mix_link)
            dve.wait_ge(vec_in, 112)
            for t in range(NT):
                n = rows_of(t)
                ya, yb = yA[t % 2][0:n], yB[t % 2][0:n]
                dve.wait_ge(ya_in[t % 2], 32 * (t // 2 + 1))
                lk.done(v.tensor_scalar(ya, ya, w12[0:n, 2 * t:2 * t + 1], None, ALU.mult))
                lk.done(v.scalar_tensor_tensor(out=ya, in0=yb, scalar=w12[0:n, 2 * t + 1:2 * t + 2], in1=ya, op0=ALU.mult, op1=ALU.add))
                lk.done(v.tensor_tensor(ya, ya, g2b if t < PT else modrow(G2, NB), ALU.mult))
                v.tensor_tensor(X1[0:n, t], X1[0:n, t], ya, ALU.add).then_inc(x2_ok, 1)
                dve.wait_ge(x2_std, t + 1)
                lk.done(v.reciprocal(rs[0:n, t:t + 1], rs[0:n, t:t + 1]))
                v.scalar_tensor_tensor(out=ya, in0=X1[0:n, t], scalar=rs[0:n, t:t + 1], in1=fng[0:n], op0=ALU.mult,
                                       op1=ALU.mult).then_inc(y_ok, 1)

        @block.tensor
        def _(pe):
            mm, tr = nc.tensor.matmul, nc.tensor.transpose
            pe.wait_ge(const_in, 16)
            pe.wait_ge(crow_in, 48)
            pe.wait_ge(cleared, 2)
            pe.wait_ge(bias_ps, 1)
            oh, ohs = C("oh", 33), C("ohs", 33)
            for o in range(0, GN, 512):
                w = min(512, GN - o)
                mm(banks[0:HD, o:o + w], relx, oh[:, o:o + w], start=True, stop=True)
            mm(banks[0:NB * HD, 1536:1536 + CK + 1], relr, ohs, start=True, stop=True).then_inc(bias_ps, 1)
            pe.wait_ge(silu_c, 1)
            for k in range(KC):
                last = tr(bank(7, KC * 33)[:, k * 33:(k + 1) * 33], crow[:, k * P:(k + 1) * P], ident[0:33, 0:33])
            last.then_inc(csT_ps, 1)
            pe.wait_ge(csT_ok, 1)
            with pe.Fori(0, 4) as i:
                for s in range(3):
                    pe.wait_ge(ada_in[s], i * 32 + 32)
                    for k in range(KC):
                        last = mm(bank(4 + s, 512, 33), csT[:, k], wa[s][:, k], start=(k == 0), stop=(k == KC - 1))
                    last.then_inc(ada_ps, 1)
            pe.wait_ge(bias_ok, 3)
            for t in range(NT):
                n = rows_of(t)
                pe.wait_ge(h_ok, t + 1)
                if t >= 2:
                    pe.wait_ge(hT_ok, t - 1)
                b = 2 * (t % 2)
                for k in range(KC):
                    last = tr(banks[:, 512 * b + n * k:512 * b + n * k + n], xt[t % 2][0:n, k * P:(k + 1) * P], ident[0:n, 0:n])
                last.then_inc(hT_ps, 1)
            stage_end(pe, 0)

            def products(out, t, wh, wl, ks, first, last):
                n = rows_of(t)
                tok = slice(t * P, t * P + n)
                for k in ks:
                    mm(out, hTh[:, k, tok], wh(k), start=(first and k == ks[0]), stop=False)
                    mm(out, hTh[:, k, tok], wl(k), start=False, stop=False)
                    done = mm(out, hTl[:, k, tok], wh(k), start=False, stop=(last and k == ks[-1]))
                return done
            pe.wait_ge(wlo_ok, 1)
            for t in range(NT):
                n = rows_of(t)
                if t >= 2:
                    pe.wait_ge(gprojA, t - 1)
                    pe.wait_ge(gprojB, t - 1)
                b = 4 + 2 * (t % 2)
                for o, w, bb in ((0, 512, b), (512, GW - 512, b + 1)):
                    last = products(bank(bb, w, n), t, lambda k: wGh[:, k, o:o + w], lambda k: wGl[:, k, o:o + w],
                                    range(KC), True, True)
                last.then_inc(gproj_ps, 1)
            pe.wait_ge(gprojB, NT)
            pe.wait_ge(gprojA, NT)
            for t in range(PT):
                tr(banks[0:RANK, t * P:(t + 1) * P], proj[:, t, 512:528], ident)
            tr(bank(2, NB, RANK), proj[0:NB, PT, 512:528], ident[0:NB, 0:NB]).then_inc(gl_ps, 1)
            pe.wait_ge(gl_ok, 2)
            wgu = V(o_wgu, P, RANK + 1)
            pe.wait_ge(vec_in, 96)
            for t in range(PT):
                mm(banks[:, t * P:(t + 1) * P], glT[0:RANK + 1, t * P:(t + 1) * P], wgu, start=True, stop=True)
            mm(bank(2, P, NB), glT[0:RANK + 1, S:TOK], wgu, start=True, stop=True).then_inc(z_ps, 1)
            pe.wait_ge(loga_ok, 2)
            for j, name in enumerate(("cum_mid", "cum_rest", "cum")):
                for h in range(2):
                    mm(bank(2 * j + h), C(name), L[:, 512 * h:512 * h + 512], start=True, stop=True)
            for t in range(PT):
                last = mm(bank(6, PT)[:, t:t + 1], L[:, t * P:(t + 1) * P], C("ones")[:, 0:1], start=True, stop=True)
            last.then_inc(cum_ps, 1)
            pe.wait_ge(scaled_ok, 4)
            pe.wait_ge(edec_ok, 6)
            for t in range(PT):
                tr(banks[:, t * P:(t + 1) * P], E[1][:, t * P:(t + 1) * P], ident)
            for t in range(PT):
                tr(banks[:, 1024 + t * P:1024 + (t + 1) * P], E[3][:, t * P:(t + 1) * P], ident)
            for t in range(PT):
                last = tr(banks[:, 2048 + t * P:2048 + (t + 1) * P], E[0][:, t * P:(t + 1) * P], ident)
            last.then_inc(gT_ps, 1)
            pe.wait_ge(k2T_ok, 1)
            pe.wait_ge(q4T_ok, 1)
            for t in range(PT):
                pe.wait_ge(blk_ok, t + 1)
                if t >= 2:
                    pe.wait_ge(att_cp, t - 1)
                mm(bank(t % 2), k2T[:, t * P:(t + 1) * P], blkq[t % 2], start=True, stop=True).then_inc(att_ps, 1)
                if t >= 1:
                    pe.wait_ge(state_ok, t + 1)
                mm(bank(7, 256), E[2][:, t * P:(t + 1) * P], proj[:, t, 256:512], start=True, stop=True).then_inc(ds_ps, 1)
                pe.wait_ge(att_ok, t + 1)
                pe.wait_ge(state_ok, t + 1)
                if t >= 2:
                    pe.wait_ge(og_cp, t - 1)
                ob = bank(2 + t % 2, 256)
                mm(ob, q4T[:, t * P:(t + 1) * P], state[t % 2], start=True, stop=True, skip_group_check=True)
                for h in range(HA):
                    last = mm(ob[:, DV * h:DV * h + DV], attS[t % 2][:, P * h:P * h + P], proj[:, t, 256 + DV * h:256 + DV * h + DV],
                              start=False, stop=True, skip_group_check=True)
                last.then_inc(og_ps, 1)
            pe.wait_ge(att_cp, PT)
            for j, src in enumerate((sA, proj[0:NB, PT, P:2 * P], proj[0:NB, PT, 0:P])):
                last = tr(bank(0, 3 * NB)[:, j * NB:(j + 1) * NB], src, ident[0:NB, 0:NB])
            last.then_inc(sc3_ps, 1)
            pe.wait_ge(sc3_ok, 2)
            pe.wait_ge(state_ok, PT + 1)
            for b in range(NB):
                last = mm(banks[:, 2048 + 256 * b:2048 + 256 * b + 256], kz[:, b], proj[0:NB, PT, 256:512], start=True, stop=True)
            last.then_inc(kv_ps, 1)
            pe.wait_ge(snew_ok, 5)
            for h in range(HA):
                for b in range(NB):
                    last = mm(bank(0, 256, NB)[:, DV * h:DV * h + DV], qz[:, (h * NB + b) * NB:(h * NB + b + 1) * NB], sS[:, b],
                              start=(b == 0), stop=(b == NB - 1))
            last.then_inc(so_ps, 1)
            pe.wait_ge(og_ok, 1)
            for c in range(2):
                for t in range(PT):
                    tr(banks[:, 1024 * c + t * P:1024 * c + (t + 1) * P], oG[:, t, c * P:(c + 1) * P], ident)
                last = tr(bank(4 + c, NB), oG[0:NB, PT, c * P:(c + 1) * P], ident[0:NB, 0:NB])
            last.then_inc(ogT_ps, 1)
            stage_end(pe, 1)

            nc.tensor.sem_inc(oT_ps, 1)

            def project_tile(c, t, halves, b):
                if 0 in halves:
                    if t == 0:
                        pe.wait_ge(wlo_ok, c * 2 + 3)
                    elif b == 7:
                        pe.wait_ge(qkv_ok, c * NT + t)
                    elif t >= 4:
                        pe.wait_ge(qkv_ok, c * NT + (t - 3))
                for h in halves:
                    last = products(bank(b, 384, rows_of(t)), t, lambda k: wPh[:, k], lambda k: wPl[:, k],
                                    range(4 * h, 4 * h + 4), h == 0, h == 1)
                if 1 in halves:
                    last.then_inc(qkv_ps, 1)

            def turn_qk(c):
                pe.wait_ge(qkv_ok, c * NT + NT)
                for j in range(2):
                    for t in range(PT):
                        last = tr(banks[:, 1024 * j + t * P:1024 * j + (t + 1) * P], qkv[:, t, j * P:(j + 1) * P], ident)
                last.then_inc(qkT_ps, 1)

            def attend(c, last_pair):
                def scores(a):
                    hh, i = a // PT, a % PT
                    r = slice(DH * hh, DH * hh + DH)
                    if a == 0:
                        pe.wait_ge(qT_ok, c + 1)
                        pe.wait_ge(kT_ok, c + 1)
                    if a >= 2:
                        pe.wait_ge(s_read, c * 16 + (a - 1))
                    for o in range(0, (i + 1) * P, 512):
                        w = min(512, (i + 1) * P - o)
                        b = 2 * (a % 2)
                        last = mm(banks[:, 512 * b + o:512 * b + o + w], qT[r, i * P:(i + 1) * P], kT[r, o:o + w], start=True, stop=True)
                    last.then_inc(s_ps, 1)

                def turn(a):
                    i = a % PT
                    pe.wait_ge(p_ok, c * 16 + (a + 1))
                    if a == 0:
                        pe.wait_ge(pair_dve, c + 1)
                        pe.wait_ge(pair_act, c + 1)
                    for j in range(i + 1):
                        last = tr(banks[:, 2048 + j * P:2048 + (j + 1) * P], pB[a % 2][:, j * P:(j + 1) * P], ident)
                    last.then_inc(pt_ps, 1)

                def values(a):
                    hh, i = a // PT, a % PT
                    pe.wait_ge(pt0_ok, c * 16 + (a + 1))
                    if i >= 4:
                        pe.wait_ge(pt1_ok, c * 8 + (hh * 4 + i - 3))
                    if a == 0:
                        pe.wait_ge(v_ok, c + 1)
                    else:
                        pe.wait_ge(o_ok, c * 16 + a)
                    for j in range(i + 1):
                        last = mm(bank(6, DH), pTB[a % 2][:, j * P:(j + 1) * P], vcur[:, j, DH * hh:DH * hh + DH],
                                  start=(j == 0), stop=(j == i))
                    last.then_inc(o_ps, 1)
                scores(0)
                scores(1)
                for a in range(16):
                    if a >= 1:
                        values(a - 1)
                    if a in STEP_PROJ and not last_pair:
                        project_tile(c + 1, *STEP_PROJ[a], 7)
                    turn(a)
                    if a + 2 < 16:
                        scores(a + 2)
                values(15)
                if not last_pair:
                    pe.wait_ge(s_read, c * 16 + 16)
                    turn_qk(c + 1)
                pe.wait_ge(o_ok, c * 16 + 16)
                for t in range(PT):
                    last = tr(banks[:, 2048 + t * P:2048 + (t + 1) * P], oB[:, t], ident)
                last.then_inc(oT_ps, 1)
            for t in range(NT):
                project_tile(0, t, (0, 1), t % 4)
            turn_qk(0)
            with pe.Fori(0, PAIRS - 1) as c:
                attend(c, False)
            attend(PAIRS - 1, True)
            stage_end(pe, 2)

            pe.wait_ge(ohb_ok, 1)
            for b in range(NB):
                if b >= 2:
                    pe.wait_ge(sprod, b - 1)
                o = 1024 * (b % 2)
                mm(banks[:, o:o + 512], ohb[:, b], sqk[:, 0, 0:512], start=True, stop=True)
                mm(banks[:, o + 512:o + QW], ohb[:, b], sqk[:, 0, 512:QW], start=True, stop=True).then_inc(qb_ps, 1)
            pe.wait_ge(slog_ok, NB)
            pe.wait_ge(selfd_ok, 1)
            n = NB * HD
            for j in range(2):
                tr(bank(4, CK, n)[:, j * P:(j + 1) * P], lg[:, j], ident)
            mm(bank(5, 1, n), selfd, C("ones", NB)[:, 0:1], start=True, stop=True).then_inc(slT_ps, 1)
            pe.wait_ge(sp_ok, 1)
            for j in range(2):
                tr(bank(6, 2 * n)[:, j * n:(j + 1) * n], srow[:, j * P:(j + 1) * P], ident[0:n, 0:n])
            tr(bank(7, n, NB), pself, ident[0:n, 0:n]).then_inc(spT_ps, 1)
            pe.wait_ge(spT_ok, 1)
            pe.wait_ge(vc_in, 48 * NB)
            for c in range(PAIRS):
                rhs = pselfT.rearrange("p (b h) -> p b h", b=NB)[:, :, 2 * c:2 * c + 2]
                mm(bank(0, 96)[:, 16 * c:16 * c + 16], sqv[:, c * P:(c + 1) * P], rhs, start=(c == 0), stop=True, skip_group_check=True)
            for b in range(NB):
                for c in range(PAIRS):
                    for j in range(2):
                        o = 16 * c + 2 * b
                        last = mm(bank(0, 96)[:, o:o + 2], vC[b][:, j, c * P:(c + 1) * P], spT[:, j, HD * b + 2 * c:HD * b + 2 * c + 2],
                                  start=False, stop=(j == 1), skip_group_check=True)
            last.then_inc(sov_ps, 1)
            stage_end(pe, 3)

            pe.wait_ge(wO_in, 32)

            def project(t):
                n = rows_of(t)
                if t >= 2:
                    pe.wait_ge(x1_ok, t - 1)
                b = 2 * (t % 2)
                for h in range(2):
                    for k in range(KC):
                        last = mm(bank(b + h, 512, n), mixT[:, k, t * P:t * P + n], wO[:, k, 512 * h:512 * h + 512], start=(k == 0), stop=(k == KC - 1))
                last.then_inc(op_ps, 1)

            def route(t):
                n = rows_of(t)
                pe.wait_ge(h2_ok, t + 1)
                if t >= 1:
                    pe.wait_ge(h2T_ok, t)
                for k in range(KC):
                    last = tr(banks[:, 2048 + n * k:2048 + n * k + n], h2[t % 2][0:n, k * P:(k + 1) * P], ident[0:n, 0:n])
                last.then_inc(h2T_ps, 1)
                pe.wait_ge(h2T_ok, t + 1)
                out = bank(6, PT * NE)[:, t * NE:(t + 1) * NE] if t < PT else bank(7, NE, NB)
                for k in range(KC):
                    last = mm(out, h2T[:, k, 0:n], rw[:, k], start=(k == 0), stop=(k == KC - 1))
                last.then_inc(lr_ps, 1)
            project(0)
            for t in range(NT):
                if t + 1 < NT:
                    project(t + 1)
                route(t)
            pe.wait_ge(both_ok, 1)
            mm(bank(0, RE), C("strict"), both, start=True, stop=True)
            mm(bank(1, RE), C("ones"), both, start=True, stop=True).then_inc(rank_ps, 1)
            stage_end(pe, 4)

            nc.tensor.sem_inc(xgT_ps, 1)
            nc.tensor.sem_inc(hidT_ps, 1)
            pe.wait_ge(route_ok, 1)

            def pairs(out, xh, xl, wh, wl, ks):
                for k in ks:
                    mm(out, xh[:, k], wh(k), start=(k == 0), stop=False)
                    mm(out, xh[:, k], wl(k), start=False, stop=False)
                    done = mm(out, xl[:, k], wh(k), start=False, stop=(k == ks[-1]))
                return done

            def rows_T(t):
                pe.wait_ge(xg_in, t * 16 + 16)
                for k in range(KC):
                    last = tr(banks[:, k * P:(k + 1) * P], xg[:, k * P:(k + 1) * P], ident)
                last.then_inc(xgT_ps, 1)

            def tile(t, s, e):
                pe.wait_ge(xgT_ok, t + 1)
                for i, (b, sig) in enumerate(((2, g_ps), (3, u_ps))):
                    if e is not None:
                        pe.wait_ge(plo_ok, e * 6 + (2 * i + 2))
                    pairs(bank(b), xgTh, xgTl, lambda k: w_hi[s][i][:, k * FF:(k + 1) * FF],
                          lambda k: w_lo[s][i][:, k * FF:(k + 1) * FF], range(KC)).then_inc(sig, 1)
                rows_T(t + 1)
                pe.wait_ge(hid_ok, t + 1)
                for k in range(4):
                    last = tr(bank(4)[:, k * P:(k + 1) * P], hid[:, k * P:(k + 1) * P], ident)
                last.then_inc(hidT_ps, 1)
                pe.wait_ge(hidT_ok, t + 1)
                if e is not None:
                    pe.wait_ge(plo_ok, e * 6 + 6)
                pe.wait_ge(yA_cp, t + 1)
                pe.wait_ge(yB_cp, t + 1)
                for h in range(2):
                    last = pairs(bank(5 + h), hidTh, hidTl, lambda k: w_hi[s][2][:, k * D + h * 512:k * D + h * 512 + 512],
                                 lambda k: w_lo[s][2][:, k * D + h * 512:k * D + h * 512 + 512], range(4))
                last.then_inc(y_ps, 1)

            def expert(e, s):
                start = pe.value_load(etab[0:1, bass.ds(e, 1)], min_val=0, max_val=MT - 1)
                end = pe.value_load(etab[0:1, bass.ds(e + 1, 1)], min_val=1, max_val=MT)
                tile(start, s, e)
                with pe.If(end - start - 1):
                    with pe.Fori(start + 1, end) as t:
                        tile(t, s, None)
            rows_T(0)
            with pe.Fori(0, NE // 2 - 1) as i:
                expert(i * 2, 0)
                expert(i * 2 + 1, 1)
            expert(NE - 2, 0)
            expert(NE - 1, 1)
            stage_end(pe, 5)


def shape_constants():
    import math
    import numpy as np
    t = np.zeros((P, CONST_COLS), np.float32)

    def put(name, a, rows=P):
        o, w = _cols[name]
        t[:rows, o:o + w] = np.asarray(a, np.float32).reshape(rows, w)
    r, c = np.arange(P)[:, None], np.arange(P)[None, :]
    put("ident", r == c)
    put("ones", np.ones((P, P)))
    put("cum_mid", (r <= c).astype(np.float32) - (r <= P // 2 - 1))
    put("cum", r <= c)
    put("cum_rest", r > c)
    put("strict", r < c)
    put("blk", r // DK == np.arange(HA * DV)[None, :] // DV)

    def columns(dist):
        d = np.maximum(dist, 0)
        df = np.maximum(d, 1).astype(np.float32)
        large = 16 + (np.log(df / np.float32(16)) / np.float32(math.log(128.0)) * np.float32(16)).astype(np.int32)
        bucket = np.where(d < 16, d, np.minimum(large, 31))
        count = (dist <= 128).astype(int) + ((dist <= 512) & (dist % 4 == 0)) + (dist % 16 == 0)
        count = np.where(dist >= 0, count, 0)
        out = np.zeros((33, dist.size), np.float32)
        out[bucket, np.arange(dist.size)] = 1.0
        out[32] = np.where(count > 0, np.log(np.maximum(count, 1)), NEG)
        return out
    put("oh", columns(S - 1 - np.arange(GN)), 33)
    pos = np.concatenate([np.arange(896, 1024), np.arange(512, 896, 4), np.arange(0, 512, 16), [1024]])
    put("ohs", columns(1024 - pos), 33)
    n = NB * HD
    put("seq8", np.arange(n)[:, None] // HD == np.arange(NB)[None, :], n)
    put("diag8", np.arange(NB)[:, None] == np.arange(n)[None, :] // HD, NB)
    put("eprio", np.tile(NE - np.arange(NE), (P, 1)))
    put("gprio", np.tile(NG - np.arange(NG), (P, 1)))
    put("thr", np.tile(P * np.arange(NT), (P, 1)))
    put("before", np.tile((np.arange(NE)[None, :] < np.arange(NE)[:, None]).reshape(1, -1), (P, 1)))
    put("srows", r < NB)
    put("tokid", np.arange(NT)[None, :] * P + np.arange(P)[:, None])
    put("eps", np.full((P, 1), EPS))
    put("one", np.ones((P, 1)))
    return t


_INS = ["x_prompt", "x_sample", "state_gla", "cache_win_k", "cache_win_v", "c_prompt", "c_sample", "w_ada", "b_ada",
        "norm1_g", "norm2_g", "w_in", "w_gate_up", "b_gate", "gla_norm_g", "w_o", "rel_bias", "router_w", "router_b",
        "moe_w_gate", "moe_w_up", "moe_w_down", "final_norm_g"]
_OUTS = [(1, 1024, 1024), (8, 1, 1024), (1, 1, 4, 32, 64), (1, 1, 1024, 12, 64), (1, 1, 1024, 12, 64),
         (1, 8, 4, 32, 64), (1, 8, 1, 12, 64), (1, 8, 1, 12, 64)]


def kernel(**inputs):
    import numpy as _np
    import concourse.bacc as _bacc
    from concourse import mybir as _mybir
    from concourse.bass_utils import run_bass_kernel_spmd as _run

    nc = _bacc.Bacc("TRN2", target_bir_lowering=False, num_devices=1)
    arrays, args = {}, []
    for name in _INS:
        a = _np.ascontiguousarray(inputs[name])
        arrays[f"in_{name}_dram"] = a
        args.append(nc.dram_tensor(f"in_{name}_dram", a.shape, _mybir.dt.from_np(a.dtype), kind="ExternalInput").ap())
    table = shape_constants()
    arrays["in_consts_dram"] = table
    args.append(nc.dram_tensor("in_consts_dram", table.shape, _mybir.dt.float32, kind="ExternalInput").ap())
    for i, shape in enumerate(_OUTS):
        args.append(nc.dram_tensor(f"out_{i}_dram", shape, _mybir.dt.float32, kind="ExternalOutput").ap())
    build(nc, *args)
    r = _run(nc, [arrays], core_ids=[0])
    return tuple(r.results[0][f"out_{i}_dram"] for i in range(len(_OUTS)))
```

```python
import concourse.bass as bass
from concourse import mybir
from contextlib import ExitStack

F32 = mybir.dt.float32
F16 = mybir.dt.float16
I32 = mybir.dt.int32
U32 = mybir.dt.uint32
ALU = mybir.AluOpType
ACT = mybir.ActivationFunctionType
AX_X = mybir.AxisListType.X

P = 128
D = 1024
KC = D // P
S = 1024
NB = 8
PT = S // P
NT = PT + 1
TOK = S + NB
HA, DK, DV = 4, 32, 64
RANK = 16
HD, DH = 12, 64
PAIRS = HD // 2
GW = 2 * HA * DK + 2 * HA * DV + RANK
QW = HD * DH
NE, NG, PG = 16, 4, 4
FF = 512
MT = 2 * TOK // P + NE
SLOTS = MT * P
YS = 4
PIECE = 2048
PIECES = 4
EPS = 1e-6
X_LOADS = ((NT + 1) // 2, NT // 2)
GN = S + P - 1
CK = 256
NEG = -1e30
WS = 1024.0
STEP_PROJ = {3 + n: (n, (0, 1)) for n in range(5)} | {8 + n: (5 + n // 2, (n % 2,)) for n in range(8)}

_cols = {}
_at = 0
for _name, _w in (("ident", P), ("ones", P), ("cum_mid", P), ("cum", P), ("cum_rest", P), ("strict", P),
                  ("blk", HA * DV), ("oh", GN), ("ohs", CK + 1), ("seq8", NB), ("diag8", NB * HD),
                  ("eprio", NE), ("gprio", NG), ("thr", NT), ("before", NE * NE), ("srows", 1), ("tokid", NT),
                  ("eps", 1), ("one", 1)):
    _cols[_name] = (_at, _w)
    _at += _w
CONST_COLS = _at

A_CONST = 0
A_SMALL = (CONST_COLS + 31) // 32 * 32
A_MOD = A_SMALL + 1184
A_G2 = A_MOD + 6 * D
A_F = A_G2 + D
A_HT = A_F
A_X1 = A_F
A_MIX = A_F + NT * D
A_T = A_MIX + KC * TOK
ARENA = 53120
A_MOE = A_MIX
A_STAGE = ARENA - 3 * PIECE


class Steps:

    def __init__(self, eng, sem):
        self.eng, self.sem, self.n, self.at, self.turn, self.per = eng, sem, 0, 0, None, 0

    def value(self):
        return self.n if self.turn is None else self.turn * self.per + self.n

    def done(self, ins, wait=True):
        ins.then_inc(self.sem, 1)
        self.n += 1
        if wait:
            self.eng.wait_ge(self.sem, self.value())

    def enter(self, turn, per):
        self.turn, self.per, self.at = turn, per, self.n

    def leave(self, turns):
        assert self.n - self.at == self.per, (self.n - self.at, self.per)
        self.turn = None
        self.n = self.at + turns * self.per


def build(nc, x_prompt, x_sample, state_gla, cache_win_k, cache_win_v, c_prompt, c_sample, w_ada, b_ada, norm1_g,
          norm2_g, w_in, w_gate_up, b_gate, gla_norm_g, w_o, rel_bias, router_w, router_b, moe_w_gate, moe_w_up,
          moe_w_down, final_norm_g, consts, y_prompt, y_sample, gla_state_p, win_k_p, win_v_p, gla_state_s,
          new_k_s, new_v_s):
    xp = x_prompt.rearrange("a s d -> (a s) d")
    xs = x_sample.rearrange("a s d -> (a s) d")
    yp = y_prompt.rearrange("a s d -> (a s) d")
    ys = y_sample.rearrange("a s d -> (a s) d")
    w_ada_v = w_ada.rearrange("l (k p) n -> p (l k) n", p=P)
    w_in_v = w_in.rearrange("l (k p) n -> p (l k) n", p=P)
    w_o_v = w_o.rearrange("l (k p) n -> p (l k) n", p=P)
    wg_flat = moe_w_gate.rearrange("l e d f -> (l e d) f")
    wu_flat = moe_w_up.rearrange("l e d f -> (l e d) f")
    wd_flat = moe_w_down.rearrange("l e f d -> (l e f) d")
    kp_v = win_k_p.rearrange("l b (t p) h d -> p (l b t) (h d)", p=P)
    vp_v = win_v_p.rearrange("l b (t p) h d -> p (l b t) (h d)", p=P)
    ck = cache_win_k.rearrange("l b s h d -> (l b) s (h d)")
    cv = cache_win_v.rearrange("l b s h d -> (l b) s (h d)")
    sgla = state_gla.rearrange("l b h k v -> (h k) (l b) v")
    sgla_out = gla_state_s.rearrange("l b h k v -> (h k) (l b) v")

    dist_bias = nc.dram_tensor("dist_bias", [HD * GN], F32, kind="Internal").ap()
    h2_rows = nc.dram_tensor("h2_rows", [TOK, D], F32, kind="Internal").ap()
    slot_token = nc.dram_tensor("slot_token", [SLOTS + 2 * P, 1], U32, kind="Internal").ap()
    slot_rows = nc.dram_tensor("slot_rows", [SLOTS, D], F32, kind="Internal").ap()

    with ExitStack() as ctx:
        def sem(name):
            return ctx.enter_context(nc.semaphore(name))

        arena = ctx.enter_context(nc.sbuf_tensor("arena", [P, ARENA], F32))
        banks = ctx.enter_context(nc.psum_tensor("banks", [P, 8 * 512], F32))
        ids = ctx.enter_context(nc.sbuf_tensor("ids", [P, 2 * NT + NT + 2], U32))
        etab = ctx.enter_context(nc.sbuf_tensor("etab", [1, NE + 1], I32))
        gidx = ctx.enter_context(nc.sbuf_tensor("gidx", [P, 1], U32))

        def V(off, cols, rows=P):
            return arena[0:rows, off:off + cols]

        def C(name, rows=P):
            o, w = _cols[name]
            return V(A_CONST + o, w, rows)

        def bank(b, cols=512, rows=P, n=1):
            return banks[0:rows, 512 * b:512 * b + cols]

        _s = [A_SMALL]

        def small(cols):
            _s[0] += cols
            assert _s[0] <= A_MOD
            return _s[0] - cols

        ident = C("ident")
        o_relx = small(HD)
        o_relr = small(NB * HD)
        o_sbias = small(CK + 1)
        o_gng = small(HA * DV)
        o_csT = small(KC * 33)
        o_ss = small(NT * HA)
        o_rs = small(NT * HA)
        o_den = small(2 * PT)
        o_rden = small(2 * PT)
        o_mx = small(2)
        o_nmx = small(2)
        o_w12 = small(2 * NT)
        o_wgu = small(HA * DK)
        o_stat = small(4)
        o_rb = small(NE)
        relx, relr, sbias = V(o_relx, HD, 33), V(o_relr, NB * HD, 33), V(o_sbias, CK + 1, NB * HD)
        gng = V(o_gng, HA * DV)
        csT = V(o_csT, KC * 33).rearrange("p (k m) -> p k m", k=KC)
        ss, rs = V(o_ss, NT * HA), V(o_rs, NT * HA)
        den, mx, nmx = V(o_den, 2 * PT), V(o_mx, 2), V(o_nmx, 2)
        rden = V(o_rden, 2 * PT)
        w12 = V(o_w12, 2 * NT)
        mod = V(A_MOD, 6 * D, 33)
        SH1, SC1, G1, SH2, SC2, G2 = range(6)
        hTh = V(A_HT, KC * TOK // 2).bitcast(F16).rearrange("p (k n) -> p k n", k=KC)
        hTl = V(A_HT + KC * TOK // 2, KC * TOK // 2).bitcast(F16).rearrange("p (k n) -> p k n", k=KC)
        mixT = V(A_MIX, KC * TOK).rearrange("p (k n) -> p k n", k=KC)

        def modrow(i, rows=33):
            return mod[0:rows, i * D:(i + 1) * D]

        def rows_of(t):
            return P if t < PT else NB

        crow = V(A_T, D, 33)
        csig = V(A_T + D, D, 33)
        wa = [V(A_T + 2 * D + s * 4096, 4096).rearrange("p (k n) -> p k n", k=KC) for s in range(3)]
        ba = [V(A_T + 2 * D + 3 * 4096 + s * 512, 512, 33) for s in range(3)]
        nrm = V(A_T + 2 * D + 3 * 4096 + 1536, 2 * D, 33)
        o_x = A_T + 2 * D + 3 * 4096 + 1536 + 2 * D
        xt = [V(o_x + s * D, D) for s in range(2)]
        bias_rows = V(A_MIX, GN, HD)
        bcA1, bcS1, sqj = V(A_MIX + 2 * D, D), V(A_MIX + 3 * D, D), V(A_MIX + 4 * D, D)

        wGh = V(A_T, KC * GW // 2).bitcast(F16).rearrange("p (k n) -> p k n", k=KC)
        wGl = V(A_T + KC * GW // 2, KC * GW // 2).bitcast(F16).rearrange("p (k n) -> p k n", k=KC)
        proj = V(A_T + KC * GW, NT * GW).rearrange("p (t n) -> p t n", t=NT)
        g0 = A_T + KC * GW + NT * GW
        wG = V(A_T + KC * GW, KC * GW).rearrange("p (k n) -> p k n", k=KC)
        o_T1, o_L, o_E = g0, g0 + D, g0 + 2 * D
        T1, L = V(o_T1, D), V(o_L, D)
        E = [V(o_E + i * D, D) for i in range(4)]
        k2T, q4T = V(g0 + 6 * D, D), V(g0 + 7 * D, D)
        attS = [V(g0 + 8 * D + s * 512, 512) for s in range(2)]
        state = [V(g0 + 9 * D + s * 256, 256) for s in range(2)]
        dstate = V(g0 + 9 * D + 512, 256)
        g1 = g0 + 9 * D + 768
        o_sc3 = g1
        sS = V(A_CONST + _cols["oh"][0], NB * DV).rearrange("p (b v) -> p b v", b=NB)
        sc3 = V(o_sc3, 3 * NB)
        eblast = V(g1 + 24, PT)
        assert g1 + 32 <= ARENA, (g1, ARENA)
        oG = V(A_T, NT * 256).rearrange("p (t n) -> p t n", t=NT)
        tG = V(A_T + NT * 256, NT * 256).rearrange("p (t n) -> p t n", t=NT)
        blkq = [V(A_T + 2 * NT * 256 + s * 512, 512) for s in range(2)]
        qz = V(A_T + 2 * NT * 256 + 1024, HA * NB * NB)
        o_st = A_T + 2 * NT * 256 + 1024 + HA * NB * NB
        sT1, sL, sA = V(o_st, P, NB), V(o_st + P, P, NB), V(o_st + 2 * P, P, NB)
        kz = V(o_E + 3 * D, NB * P, NB).rearrange("q (b n) -> q b n", b=NB)
        glT = V(A_MIX, TOK, 32)

        def pair_weights(at):
            return (V(at, KC * 384).rearrange("p (k g n) -> p k g n", k=KC, g=3),
                    V(at + KC * 384, KC * 192).bitcast(F16).rearrange("p (k n) -> p k n", k=KC),
                    V(at + KC * 576, KC * 192).bitcast(F16).rearrange("p (k n) -> p k n", k=KC))
        wP, wPh, wPl = pair_weights(A_T)
        w0, w0h, w0l = pair_weights(A_MIX + 2 * TOK)
        a0 = A_T + KC * 768
        vcur = V(a0, D).rearrange("p (t n) -> p t n", t=PT); a0 += D
        qT, kT = V(a0, D), V(a0 + D, D); a0 += 2 * D
        strip = V(a0, 2 * D).rearrange("p (h n) -> p h n", h=2); a0 += 2 * D
        sB = [V(a0 + s * D, D) for s in range(2)]; a0 += 2 * D
        assert a0 <= g0
        a0 = g0
        qkv = V(a0, NT * 384).rearrange("p (t n) -> p t n", t=NT); a0 += NT * 384
        assert a0 <= o_E + 2 * D
        pB = [V(a0 + s * D, D) for s in range(2)]; a0 += 2 * D
        pTB = [V(a0 + s * D, D) for s in range(2)]; a0 += 2 * D
        oB = V(a0, D).rearrange("p (t n) -> p t n", t=PT); a0 += D
        assert a0 <= ARENA
        zeros = V(ARENA - 512, 512)
        assert a0 <= ARENA - 512
        sqk = V(A_MOD, 2 * QW, NB).rearrange("p (g n) -> p g n", g=2)
        sqv = V(A_G2, QW, NB)
        o_sa = A_T
        vC = [V(o_sa + b * 1536, 1536).rearrange("p (c n) -> p c n", c=2) for b in range(NB)]
        o_sb2 = o_sa + NB * 1536
        kCb = [V(o_sb2 + s * 1536, 1536).rearrange("p (c n) -> p c n", c=2) for s in range(2)]
        prod = V(o_sb2 + 3072, 1536)
        assert o_sb2 + 3072 + 1536 <= ARENA
        o_sc = A_HT
        ohb = V(o_sc, NB * P, NB).rearrange("q (b n) -> q b n", b=NB)
        lg = V(o_sc + 1024, 192).rearrange("p (c n) -> p c n", c=2)
        selfp = V(o_sc + 1216, QW, NB)
        selfl = V(o_sc + 1984, HD, NB)
        selfd = V(o_sc + 1996, NB * HD, NB)
        srow = V(o_sc + 2092, CK + 1, NB * HD)
        spT = V(o_sc + 2349, 192).rearrange("p (c n) -> p c n", c=2)
        pself = V(o_sc + 2541, NB, NB * HD)
        pselfT = V(o_sc + 2549, NB * HD, NB)

        a1 = A_T
        wO = V(a1, KC * D).rearrange("p (k n) -> p k n", k=KC); a1 += KC * D
        xr = [V(a1 + s * D, D) for s in range(2)]; a1 += 2 * D
        h2 = [V(a1 + s * D, D) for s in range(2)]; a1 += 2 * D
        h2T = V(a1, D).rearrange("p (k n) -> p k n", k=KC); a1 += D
        rw = V(a1, KC * NE).rearrange("p (k n) -> p k n", k=KC); a1 += KC * NE
        bcG1, bcA2, bcS2 = (V(a1 + i * D, D) for i in range(3)); a1 += 3 * D
        sqj2 = V(a1, D); a1 += D

        assert a1 <= A_STAGE, (a1, A_STAGE, A_T, A_MOD, A_SMALL, _s)
        free = [[A_MOD, A_MOD + 2 * D], [A_CONST + _cols["oh"][0], A_CONST + _cols["oh"][0] + GN]]

        def R(cols):
            r = next(r for r in free if r[1] - r[0] >= cols)
            r[0] += cols
            return V(r[0] - cols, cols)
        RE = NT * NE
        sco, sel, msel, tA, tB, one1, one2, both = (R(RE) for _ in range(8))
        pair6 = R(NT * NG * 6)
        gsc, gsel, gm = R(NT * NG), R(NT * NG), R(NT)
        rank, cnt, base = R(RE), R(RE), R(RE)
        nE, tE, offE = R(NE), R(NE), R(NE)
        cmp9, cmpE = R(NE * NT), R(NE * NE)
        slotf = R(2 * NT)
        s12 = R(2 * NT)
        zero_i = R(SLOTS // P + 2)
        X1 = V(A_X1, NT * D).rearrange("p (t n) -> p t n", t=NT)
        g2b = V(A_G2, D)

        m0 = A_MOE
        w_hi, w_lo, wD = [], [], []
        for s in range(2):
            for parts in (w_hi, w_lo):
                parts.append([V(m0 + i * PIECE, PIECE).bitcast(F16) for i in range(2)])
                m0 += 2 * PIECE
            wD.append(V(m0, 4 * D))
            m0 += 4 * D
        gmin = V(A_MOD + 4 * D, FF)
        sg, hid, hidT = V(m0, FF), V(m0 + FF, FF), V(m0 + 2 * FF, FF)
        assert m0 + 3 * FF <= A_STAGE
        o_used = A_CONST + _cols["cum_mid"][0]
        assert o_used + PIECE <= A_CONST + _cols["seq8"][0]
        stage = [V(A_STAGE + r * PIECE, PIECE) for r in range(3)] + [V(o_used, PIECE)]
        xg = V(A_MOD, D)
        xgTh = V(A_MOD + D, D // 2).bitcast(F16).rearrange("p (k n) -> p k n", k=KC)
        xgTl = V(A_MOD + D + D // 2, D // 2).bitcast(F16).rearrange("p (k n) -> p k n", k=KC)
        yM = V(A_MOD + 2 * D, D)
        c0 = A_MOE
        yA = [V(c0 + s * D, D) for s in range(YS)]
        yB = [V(c0 + (YS + s) * D, D) for s in range(YS)]
        sqj3 = V(c0 + 2 * YS * D, D)
        fng = V(A_MOD + 3 * D, D)

        const_in = sem("const_in"); crow_in = sem("crow_in"); vec_in = sem("vec_in")
        cleared = sem("cleared"); neg_exp_c = sem("neg_exp_c"); silu_c = sem("silu_c"); csT_ps = sem("csT_ps")
        csT_ok = sem("csT_ok"); ada_in = [sem(f"ada_in{s}") for s in range(3)]; ada_ps = sem("ada_ps")
        ada_added = sem("ada_added"); mod_ok = sem("mod_ok"); bc_ok = sem("bc_ok")
        bias_ps = sem("bias_ps"); bias_ok = sem("bias_ok")
        x_in = [sem(f"x_in{s}") for s in range(2)]; rms_ok = sem("rms_ok"); norm_ok = sem("norm_ok");
        hT_ps = sem("hT_ps")
        hT_ok = sem("hT_ok"); act_link = sem("act_link"); dve_link = sem("dve_link"); 
        wG_in = sem("wG_in"); gproj_ps = sem("gproj_ps"); gprojA = sem("gprojA"); gprojB = sem("gprojB")
        gl_ps = sem("gl_ps"); gl_ok = sem("gl_ok"); z_ps = sem("z_ps"); lnz_ok = sem("lnz_ok"); loga_ok = sem("loga_ok")
        cum_ps = sem("cum_ps"); edec_ok = sem("edec_ok"); scaled_ok = sem("scaled_ok"); gT_ps = sem("gT_ps")
        k2T_ok = sem("k2T_ok"); q4T_ok = sem("q4T_ok"); blk_ok = sem("blk_ok"); att_ps = sem("att_ps")
        att_cp = sem("att_cp"); att_ok = sem("att_ok"); og_ps = sem("og_ps"); ds_ps = sem("ds_ps")
        state_ok = sem("state_ok"); og_cp = sem("og_cp"); gout = sem("gout")
        sc3_ps = sem("sc3_ps"); sc3_ok = sem("sc3_ok"); kv_ps = sem("kv_ps"); snew_ok = sem("snew_ok")
        so_ps = sem("so_ps"); osq_ok = sem("osq_ok"); ossq_ok = sem("ossq_ok"); ostd_ok = sem("ostd_ok")
        rexp_ok = sem("rexp_ok"); og_ok = sem("og_ok"); ogT_ps = sem("ogT_ps"); ogT_ok = sem("ogT_ok")
        wP_in = sem("wP_in"); strip_in = [sem(f"strip_in{h}") for h in range(2)]; pair_dve = sem("pair_dve"); pair_act = sem("pair_act")
        qkv_ps = sem("qkv_ps"); qkv_ok = sem("qkv_ok"); kv_out = sem("kv_out"); sq_ok = sem("sq_ok")
        qkT_ps = sem("qkT_ps"); qT_ok = sem("qT_ok"); kT_ok = sem("kT_ok"); s_ps = sem("s_ps"); s_read = sem("s_read")
        m_ok = sem("m_ok"); p_ok = sem("p_ok"); pt_ps = sem("pt_ps"); pt0_ok = sem("pt0_ok"); pt1_ok = sem("pt1_ok")
        o_ps = sem("o_ps"); o_ok = sem("o_ok"); oT_ps = sem("oT_ps"); whi_ok = sem("whi_ok"); wlo_ok = sem("wlo_ok"); v_ok = sem("v_ok")
        hT_hi = sem("hT_hi")
        kc_in = [sem(f"kc_in{s}") for s in range(2)]; vc_in = sem("vc_in")
        ohb_ok = sem("ohb_ok"); qb_ps = sem("qb_ps"); slog_ok = sem("slog_ok"); sprod = sem("sprod")
        selfd_ok = sem("selfd_ok"); slT_ps = sem("slT_ps"); smax_ok = sem("smax_ok"); sexp_ok = sem("sexp_ok")
        sp_ok = sem("sp_ok"); spT_ps = sem("spT_ps"); spT_ok = sem("spT_ok"); sov_ps = sem("sov_ps")
        smix_ok = sem("smix_ok")
        wO_in = sem("wO_in")
        op_ps = sem("op_ps"); res_ok = sem("res_ok")
        h2_out = [sem(f"h2_out{s}") for s in range(2)]; h2T_ps = sem("h2T_ps"); h2T_ok = sem("h2T_ok"); lr_ps = sem("lr_ps")
        rexp2 = sem("rexp2"); both_ok = sem("both_ok"); rank_ps = sem("rank_ps"); route_ok = sem("route_ok")
        zero_ok = sem("zero_ok"); st_zero = sem("st_zero"); st_out = sem("st_out")
        gi_in = sem("gi_in"); xg_in = sem("xg_in"); piece_in = [sem(f"piece_in{r}") for r in range(4)]; down_in = [sem(f"down_in{r}") for r in range(2)]
        phi_ok = sem("phi_ok"); plo_ok = sem("plo_ok")
        gabs_ok = sem("gabs_ok"); gln_ok = sem("gln_ok"); gsub_ok = sem("gsub_ok"); ya_sc = sem("ya_sc")
        xgT_ps = sem("xgT_ps"); xgT_hi = sem("xgT_hi"); xgT_ok = sem("xgT_ok"); g_ps = sem("g_ps"); u_ps = sem("u_ps")
        gexp_ok = sem("gexp_ok"); hid_ok = sem("hid_ok"); hidT_ps = sem("hidT_ps"); 
        hidT_ok = sem("hidT_ok"); y_ps = sem("y_ps"); y_cp = sem("y_cp"); yrow_out = sem("yrow_out")
        ya_in = [sem(f"ya_in{s}") for s in range(YS)]; mix_link = sem("mix_link"); rows_zero = sem("rows_zero")
        y_out = [sem(f"y_out{s}") for s in range(YS)]
        stage_done = sem("stage_done")

        block = ctx.enter_context(nc.Block())

        def low_made(eng, e, p):
            eng.wait_ge(plo_ok, e * PIECES + (p + 1))

        def stage_end(eng, i):
            eng.drain().then_inc(stage_done, 1)
            eng.wait_ge(stage_done, 5 * (i + 1))

        @block.sync
        def _(sp):
            sp.dma_start(V(A_CONST, CONST_COLS), consts).then_inc(const_in, 16)
            sp.wait_ge(cleared, 3)
            sp.dma_start(crow[0:NB], c_sample).then_inc(crow_in, 16)
            sp.dma_start(crow[32:33], c_prompt).then_inc(crow_in, 16)
            sp.dma_start(relx[0:32], rel_bias).then_inc(crow_in, 16)

            def load_ada(j, s):
                sp.dma_start(wa[s], w_ada_v[:, :, bass.ds(j * 512, 512)]).then_inc(ada_in[s], 16)
                sp.dma_start(ba[s], b_ada[0:1, bass.ds(j * 512, 512)].partition_broadcast(33)).then_inc(ada_in[s], 16)
            for s in range(3):
                load_ada(s, s)
            sp.dma_start(nrm[:, 0:D], norm1_g[0:1, :].partition_broadcast(33)).then_inc(vec_in, 16)
            sp.dma_start(nrm[:, D:2 * D], norm2_g[0:1, :].partition_broadcast(33)).then_inc(vec_in, 16)
            sp.dma_start(gng, gla_norm_g[0:1, :].partition_broadcast(P)).then_inc(vec_in, 16)
            sp.dma_start(V(o_wgu, P, RANK), w_gate_up[0]).then_inc(vec_in, 16)
            sp.dma_start(arena[RANK:RANK + 1, o_wgu:o_wgu + P], b_gate[0:1, :]).then_inc(vec_in, 16)
            rb_v = router_b.rearrange("(a n) -> a n", a=1)
            sp.dma_start(V(o_rb, NE), rb_v.partition_broadcast(P)).then_inc(vec_in, 16)
            with sp.Fori(0, 3) as i:
                for s in range(3):
                    sp.wait_ge(ada_added, i * 3 + (s + 1))
                    sp.nop(nofuse=True)
                    load_ada(i * 3 + (s + 3), s)
            for t in range(NT):
                if t >= 2:
                    sp.wait_ge(hT_ps, t - 1)
                sp.dma_start(xt[t % 2][0:rows_of(t)], xp[t * P:(t + 1) * P] if t < PT else xs).then_inc(x_in[t % 2], 16)
                if t in (2, 4):
                    sp.wait_ge(ada_ps, 12)
                    k = slice(2 * t - 4, 2 * t)
                    sp.dma_start(wG[:, k], w_in_v[:, k, 0:GW]).then_inc(wG_in, 16)
            sp.wait_ge(bias_ok, 3)
            sp.dma_start(dist_bias.rearrange("(h n) -> h n", h=HD), bias_rows).then_inc(gout, 16)
            sp.wait_ge(gout, 16)
            stage_end(sp, 0)

            sp.dma_start(sS, sgla).then_inc(wG_in, 16)
            w_pair = w_in_v[:, :, GW:GW + 3 * QW].rearrange("p k (g n) -> p k g n", g=3)

            def load_w(c, w):
                for g in range(3):
                    sp.dma_start(w[:, :, g], w_pair[:, :, g, bass.ds(c * P, P)]).then_inc(wP_in, 16)
            load_w(0, w0)
            sp.wait_ge(state_ok, 1 + PT)
            for h in range(HA):
                sp.dma_start(gla_state_p[0, 0, h], state[PT % 2][32 * h:32 * h + 32, DV * h:DV * h + DV]).then_inc(gout, 16)
            sp.wait_ge(snew_ok, 5)
            sp.dma_start(sgla_out, sS).then_inc(gout, 16)
            sp.wait_ge(gout, 16 * (HA + 2))
            stage_end(sp, 1)

            sp.sem_inc(kv_out, 16)

            def load_strip(c, hh):
                v = dist_bias[bass.ds(c * (2 * GN) + hh * GN, D)]
                sp.dma_start(strip[:, hh], bass.AP(tensor=v.tensor, offset=v.offset, ap=[[1, P], [1, D]]))\
                  .then_inc(strip_in[hh], 16)

            def pair_dmas(c, last, more):
                sp.wait_ge(qkv_ok, c * NT + NT)
                sp.nop(nofuse=True)
                sp.dma_start(kp_v[:, :, bass.ds(c * P, P)], qkv[:, 0:PT, 128:256]).then_inc(kv_out, 16)
                sp.dma_start(vp_v[:, :, bass.ds(c * P, P)], qkv[:, 0:PT, 256:384]).then_inc(kv_out, 16)
                if last:
                    return
                sp.wait_ge(s_read, c * 16 + 8)
                sp.nop(nofuse=True)
                load_strip(c + 1, 0)
                if more:
                    sp.wait_ge(wlo_ok, c * 2 + 6)
                    sp.nop(nofuse=True)
                    load_w(c + 2, wP)
                sp.wait_ge(s_read, c * 16 + 16)
                sp.nop(nofuse=True)
                load_strip(c + 1, 1)
            load_strip(0, 0)
            load_strip(0, 1)
            load_w(1, wP)
            sp.wait_ge(cleared, 6)
            for h in range(2):
                sp.dma_start(slot_rows[NE * P:, 512 * h:512 * h + 512].rearrange("(t p) n -> p t n", p=P),
                             zeros.unsqueeze(1).broadcast_to([P, MT - NE, 512])).then_inc(rows_zero, 16)
            with sp.Fori(0, PAIRS - 2) as c:
                pair_dmas(c, False, True)
            pair_dmas(PAIRS - 2, False, False)
            pair_dmas(PAIRS - 1, True, False)
            sp.wait_ge(kv_out, 32 * PAIRS + 16)
            sp.wait_ge(rows_zero, 32)
            sp.wait_ge(sq_ok, 2 * PAIRS)
            sp.dma_start(new_k_s.rearrange("l b s h d -> (l b s) (h d)"), sqk[:, 1]).then_inc(kv_out, 16)
            sp.dma_start(new_v_s.rearrange("l b s h d -> (l b s) (h d)"), sqv).then_inc(kv_out, 16)
            stage_end(sp, 2)

            def load_cache(dst, src, b, s_in):
                sp.dma_start(dst[:, 0], src[b, 896:1024]).then_inc(s_in, 16)
                sp.dma_start(dst[0:96, 1], src[b, 512:896].rearrange("(n r) d -> n r d", r=4)[:, 0]).then_inc(s_in, 16)
                sp.dma_start(dst[96:128, 1], src[b, 0:512].rearrange("(n r) d -> n r d", r=16)[:, 0]).then_inc(s_in, 16)
            for b in range(NB):
                if b >= 2:
                    sp.wait_ge(sprod, b - 1)
                load_cache(kCb[b % 2], ck, b, kc_in[b % 2])
            for b in range(NB):
                load_cache(vC[b], cv, b, vc_in)
            sp.wait_ge(kv_out, 32 * PAIRS + 48)
            stage_end(sp, 3)

            def load_piece(e, p):
                src = (wg_flat, wu_flat)[p // 2][bass.ds(e * D + (p % 2) * (D // 2), D // 2), :]
                sp.dma_start(stage[p].rearrange("p (k n) -> p k n", n=FF), src.rearrange("(k p) n -> p k n", p=P))\
                  .then_inc(piece_in[p], 16)

            def load_down(e, s):
                sp.dma_start(wD[s].rearrange("p (k n) -> p k n", n=D),
                             wd_flat[bass.ds(e * FF, FF), :].rearrange("(k p) n -> p k n", p=P)).then_inc(down_in[s], 16)

            sp.dma_start(wO, w_o_v).then_inc(wO_in, 16)
            sp.dma_start(rw, router_w.rearrange("(k p) n -> p k n", p=P)).then_inc(wO_in, 16)
            for t in range(NT):
                if t >= 2:
                    sp.wait_ge(res_ok, t - 1)
                sp.dma_start(xr[t % 2][0:rows_of(t)], xp[t * P:(t + 1) * P] if t < PT else xs).then_inc(x_in[t % 2], 16)
                if t >= 1:
                    sp.wait_ge(norm_ok, NT + t)
                    sp.dma_start(h2_rows[(t - 1) * P:t * P], h2[(t - 1) % 2]).then_inc(h2_out[(t - 1) % 2], 16)
            sp.wait_ge(norm_ok, 2 * NT)
            sp.dma_start(h2_rows[S:TOK], h2[PT % 2][0:NB]).then_inc(h2_out[PT % 2], 16)
            for p in range(3):
                load_piece(0, p)
            sp.dma_start(fng, final_norm_g.rearrange("(a n) -> a n", a=1).partition_broadcast(P)).then_inc(vec_in, 16)
            sp.wait_ge(zero_ok, 1)
            sp.dma_start(slot_token.rearrange("(p n) a -> p (n a)", p=P), zero_i.bitcast(U32)).then_inc(st_zero, 16)
            sp.wait_ge(h2_out[0], 16 * ((NT + 1) // 2))
            sp.wait_ge(h2_out[1], 16 * (NT // 2))
            sp.wait_ge(st_zero, 16)

            sp.wait_ge(op_ps, NT)
            load_down(0, 0)
            stage_end(sp, 4)

            load_piece(0, 3)

            def load_expert(e, s, wait):
                for p in range(PIECES):
                    low_made(sp, e - 1, p)
                    sp.nop(nofuse=True)
                    load_piece(e, p)
                if wait:
                    done = sp.value_load(etab[0:1, bass.ds(e - 1, 1)], min_val=1, max_val=MT)
                    sp.wait_ge(y_ps, done)
                    sp.nop(nofuse=True)
                load_down(e, s)
            load_expert(1, 1, False)
            sp.wait_ge(route_ok, 1)
            with sp.Fori(1, NE // 2) as i:
                load_expert(i * 2, 0, True)
                load_expert(i * 2 + 1, 1, True)
            stage_end(sp, 5)
            for t in range(NT):
                sp.wait_ge(norm_ok, 2 * NT + t + 1)
                sp.dma_start(yp[t * P:(t + 1) * P] if t < PT else ys, yA[t % YS][0:rows_of(t)]).then_inc(y_out[t % YS], 16)
            for s in range(YS):
                sp.wait_ge(y_out[s], 16 * ((NT - s + YS - 1) // YS))

        @block.gpsimd
        def _(pool):
            bc = Steps(pool, bc_ok)
            pool.wait_ge(mod_ok, 2)
            bc.done(nc.gpsimd.partition_broadcast(bcA1, modrow(SC1)[32:33]), wait=False)
            bc.done(nc.gpsimd.partition_broadcast(bcS1, modrow(SH1)[32:33]), wait=False)
            stage_end(pool, 0)
            for t in range(PT):
                pool.wait_ge(att_cp, t + 1)
                v = attS[t % 2].rearrange("p (h n) -> p h n", h=HA)
                nc.gpsimd.affine_select(out=v, in_=v, pattern=[[0, HA], [1, P]], compare_op=ALU.is_ge, fill=0.0,
                                        base=0, channel_multiplier=-1).then_inc(att_ok, 1)
            stage_end(pool, 1)

            def keep_values(c):
                pool.wait_ge(oT_ps, c + 1)
                pool.wait_ge(qkv_ok, c * NT + NT)
                pool.nop(nofuse=True)
                nc.gpsimd.tensor_copy(vcur, qkv[:, 0:PT, 256:384]).then_inc(v_ok, 1)
            with pool.Fori(0, PAIRS - 1) as c:
                keep_values(c)
            keep_values(PAIRS - 1)
            stage_end(pool, 2)
            stage_end(pool, 3)
            bc.done(nc.gpsimd.partition_broadcast(bcG1, modrow(G1)[32:33]), wait=False)
            bc.done(nc.gpsimd.partition_broadcast(bcA2, modrow(SC2)[32:33]), wait=False)
            bc.done(nc.gpsimd.partition_broadcast(bcS2, modrow(SH2)[32:33]), wait=False)
            bc.done(nc.gpsimd.partition_broadcast(g2b, modrow(G2)[32:33]), wait=False)
            nc.gpsimd.memset(zero_i, 0.0).then_inc(zero_ok, 1)
            pool.wait_ge(st_zero, 16)
            pool.wait_ge(route_ok, 1)
            for t in range(NT):
                n = rows_of(t)
                for j in range(2):
                    nc.gpsimd.indirect_dma_start(
                        slot_token, bass.IndirectOffsetOnAxis(ap=ids[0:n, 2 * t + j:2 * t + j + 1], axis=0),
                        ids[0:n, 2 * NT + t:2 * NT + t + 1], None).then_inc(st_out, 16)
            pool.wait_ge(st_out, 32 * NT)
            stage_end(pool, 4)

            pool.wait_ge(route_ok, 1)

            def gather(t):
                pool.wait_ge(xgT_ps, t + 1)
                pool.nop(nofuse=True)
                nc.gpsimd.indirect_dma_start(
                    xg, None, h2_rows, bass.IndirectOffsetOnAxis(ap=gidx[:], axis=0)).then_inc(xg_in, 16)
                pool.wait_ge(xg_in, t * 16 + 16)
                pool.nop(nofuse=True)
                load_ids(t + 1)

            def load_ids(t):
                pool.dma_start(gidx[:], slot_token[bass.ds(t * P, P), :]).then_inc(gi_in, 16)
                pool.wait_ge(gi_in, t * 16 + 16)
                pool.nop(nofuse=True)

            def expert(e):
                start = pool.value_load(etab[0:1, bass.ds(e, 1)], min_val=0, max_val=MT - 1)
                end = pool.value_load(etab[0:1, bass.ds(e + 1, 1)], min_val=1, max_val=MT)
                gather(start + 1)
                with pool.If(end - start - 1):
                    with pool.Fori(start + 1, end) as t:
                        gather(t + 1)
            load_ids(0)
            gather(0)
            with pool.Fori(0, NE // 2 - 1) as i:
                expert(i * 2)
                expert(i * 2 + 1)
            expert(NE - 2)
            expert(NE - 1)
            stage_end(pool, 5)
            for t in range(NT):
                n = rows_of(t)
                if t >= YS:
                    pool.wait_ge(y_out[t % YS], 16 * (t // YS))
                for j, dst in ((0, yA), (1, yB)):
                    nc.gpsimd.indirect_dma_start(
                        dst[t % YS][0:n], None, slot_rows,
                        bass.IndirectOffsetOnAxis(ap=ids[0:n, 2 * t + j:2 * t + j + 1], axis=0)).then_inc(ya_in[t % YS], 16)

        @block.scalar
        def _(act):
            lk = Steps(act, act_link)
            A = nc.scalar.activation
            eps = C("eps")

            act.wait_ge(const_in, 16)
            act.wait_ge(crow_in, 48)
            A(csig, crow, ACT.Exp, scale=-1.0).then_inc(neg_exp_c, 1)
            act.wait_ge(csT_ps, 1)
            A(csT.rearrange("p k m -> p (k m)"), bank(7, KC * 33), ACT.Copy).then_inc(csT_ok, 1)
            for t in range(NT):
                n = rows_of(t)
                act.wait_ge(x_in[t % 2], 16 * (t // 2 + 1))
                lk.done(A(sqj[0:n], xt[t % 2][0:n], ACT.Square, accum_out=ss[0:n, t:t + 1]))
                A(rs[0:n, t:t + 1], ss[0:n, t:t + 1], ACT.Sqrt, scale=1.0 / D, bias=eps[0:n]).then_inc(rms_ok, 1)
                if t >= 1:
                    act.wait_ge(hT_ps, t)
                    b = 2 * ((t - 1) % 2)
                    A(hTh[:, :, (t - 1) * P:t * P], banks[:, 512 * b:512 * b + 1024].rearrange("p (k n) -> p k n", k=KC),
                      ACT.Copy).then_inc(hT_hi, 1)
            act.wait_ge(hT_ps, NT)
            A(hTh[:, :, S:TOK], bank(2 * (PT % 2), KC * NB).rearrange("p (k n) -> p k n", k=KC), ACT.Copy).then_inc(hT_hi, 1)
            act.wait_ge(wG_in, 32)
            for j in range(2):
                k = slice(4 * j, 4 * j + 4)
                A(wGh[:, k], wG[:, k], ACT.Copy, scale=WS).then_inc(whi_ok, 1)
            stage_end(act, 0)

            def split_high_part(j, w, high):
                k = slice(4 * j, 4 * j + 4)
                A(high[:, k].rearrange("p k (g n) -> p k g n", g=3), w[:, k], ACT.Copy, scale=WS).then_inc(whi_ok, 1)

            def store_qkv(c, t, b):
                n = rows_of(t)
                act.wait_ge(qkv_ps, c * NT + (t + 1))
                A(qkv[0:n, t], bank(b, 384, n), ACT.Copy, scale=1.0 / WS).then_inc(qkv_ok, 1)
            for t in range(NT):
                n = rows_of(t)
                act.wait_ge(gproj_ps, t + 1)
                A(proj[0:n, t, 0:512], bank(4 + 2 * (t % 2), 512, n), ACT.Copy, scale=1.0 / WS).then_inc(gprojA, 1)
            act.wait_ge(wP_in, 48)
            for j in range(2):
                split_high_part(j, w0, w0h)
            act.wait_ge(z_ps, 1)
            z = banks[:, 0:D]
            lk.done(A(T1, z, ACT.Abs))
            lk.done(A(sT1, bank(2, P, NB), ACT.Abs))
            lk.done(A(T1, T1, ACT.Exp, scale=-1.0))
            lk.done(A(sT1, sT1, ACT.Exp, scale=-1.0))
            lk.done(A(T1, T1, ACT.Ln, bias=C("one")))
            A(sT1, sT1, ACT.Ln, bias=C("one", NB)).then_inc(lnz_ok, 1)
            act.wait_ge(cum_ps, 1)
            ed = Steps(act, edec_ok)
            ed.done(A(E[0], banks[:, 0:D], ACT.Exp), wait=False)
            ed.done(A(E[1], banks[:, 0:D], ACT.Exp, scale=-1.0), wait=False)
            ed.done(A(E[2], banks[:, 1024:1024 + D], ACT.Exp), wait=False)
            ed.done(A(E[3], banks[:, 2048:2048 + D], ACT.Exp), wait=False)
            ed.done(A(eblast, bank(6, PT), ACT.Exp), wait=False)
            ed.done(A(sA, sL, ACT.Exp), wait=False)
            act.wait_ge(gT_ps, 1)
            A(k2T, banks[:, 0:D], ACT.Copy).then_inc(k2T_ok, 1)
            for t in range(PT):
                act.wait_ge(att_ps, t + 1)
                if t >= 2:
                    act.wait_ge(og_ps, t - 1)
                A(attS[t % 2], bank(t % 2), ACT.Copy).then_inc(att_cp, 1)
                store_qkv(0, t, 6)
                act.wait_ge(og_ps, t + 1)
                A(oG[:, t], bank(2 + t % 2, 256), ACT.Copy).then_inc(og_cp, 1)
            store_qkv(0, PT, 6)
            act.wait_ge(so_ps, 1)
            act.wait_ge(cleared, 5)
            A(oG[0:NB, PT], bank(0, 256, NB), ACT.Copy).then_inc(og_cp, 1)
            act.wait_ge(og_cp, NT)
            lk.done(A(tG.rearrange("p t n -> p (t n)"), oG.rearrange("p t n -> p (t n)"), ACT.Square))
            nc.scalar.sem_inc(osq_ok, 1)
            act.wait_ge(ossq_ok, 1)
            A(rs, ss, ACT.Sqrt, scale=1.0 / DV, bias=eps).then_inc(ostd_ok, 1)
            A(tG, proj[:, :, 528:784], ACT.Exp, scale=-1.0).then_inc(rexp_ok, 1)
            act.wait_ge(ogT_ps, 1)
            for c in range(2):
                lk.done(A(mixT[:, c, 0:S], banks[:, 1024 * c:1024 * c + D], ACT.Copy), wait=False)
                lk.done(A(mixT[:, c, S:TOK], bank(4 + c, NB), ACT.Copy), wait=False)
            stage_end(act, 1)

            nc.scalar.sem_inc(pair_act, 1)

            def split_high(c, j):
                act.wait_ge(wP_in, c * 48 + 48)
                split_high_part(j, wP, wPh)

            def store_kT(c):
                act.wait_ge(qkT_ps, c + 1)
                A(kT, banks[:, 1024:2048], ACT.Copy).then_inc(kT_ok, 1)

            def attend(c, last):
                act.wait_ge(qkv_ok, c * NT + NT)
                qs_ = qkv[0:NB, PT].rearrange("p (g n) -> p g n", g=3)
                A(sqk[:, :, bass.ds(c * P, P)], qs_[:, 0:2], ACT.Copy).then_inc(sq_ok, 1)
                A(sqv[:, bass.ds(c * P, P)], qs_[:, 2], ACT.Copy).then_inc(sq_ok, 1)

                def exp_tile(a):
                    n = (a % PT + 1) * P
                    act.wait_ge(m_ok, c * 16 + (a + 1))
                    if a >= 2:
                        act.wait_ge(pt_ps, c * 16 + (a - 1))
                    A(pB[a % 2][:, 0:n], sB[a % 2][:, 0:n], ACT.Exp, bias=nmx[:, a % 2:a % 2 + 1],
                      accum_out=den[:, a:a + 1]).then_inc(p_ok, 1)
                exp_tile(0)
                for a in range(16):
                    if a < 15:
                        exp_tile(a + 1)
                    n = min(a % PT + 1, 4) * P
                    act.wait_ge(pt_ps, c * 16 + (a + 1))
                    if a >= 2:
                        act.wait_ge(o_ps, c * 16 + (a - 1))
                    A(pTB[a % 2][:, 0:n], bank(4, n), ACT.Copy).then_inc(pt0_ok, 1)
                    if not last:
                        if a < 2:
                            split_high(c + 1, a)
                        if a in STEP_PROJ and 1 in STEP_PROJ[a][1]:
                            t = STEP_PROJ[a][0]
                            if t == 0:
                                act.wait_ge(v_ok, c + 1)
                                act.wait_ge(sq_ok, c * 2 + 2)
                                act.wait_ge(kv_out, c * 32 + 48)
                            store_qkv(c + 1, t, 7)
                if not last:
                    store_kT(c + 1)
                act.wait_ge(oT_ps, c + 2)
                A(mixT[:, bass.ds(c + 2, 1), 0:512].rearrange("p a (t n) -> p (a t) n", t=4),
                  bank(4).rearrange("p (t n) -> p t n", t=4)[:, :, ::-1], ACT.Copy).then_inc(pair_act, 1)
            store_kT(0)
            with act.Fori(0, PAIRS - 1) as c:
                attend(c, False)
            attend(PAIRS - 1, True)
            stage_end(act, 2)

            act.wait_ge(smax_ok, 1)
            A(srow, srow, ACT.Exp, bias=V(o_stat + 1, 1, NB * HD), accum_out=V(o_stat + 2, 1, NB * HD)).then_inc(sexp_ok, 1)
            act.wait_ge(spT_ps, 1)
            lk.done(A(spT.rearrange("p c n -> p (c n)"), bank(6, 192), ACT.Copy), wait=False)
            A(pselfT, bank(7, NB * HD, NB), ACT.Copy).then_inc(spT_ok, 1)
            stage_end(act, 3)

            for t in range(NT):
                n = rows_of(t)
                act.wait_ge(res_ok, t + 1)
                lk.done(A(sqj2[0:n], X1[0:n, t], ACT.Square, accum_out=ss[0:n, t:t + 1]))
                A(rs[0:n, t:t + 1], ss[0:n, t:t + 1], ACT.Sqrt, scale=1.0 / D, bias=eps[0:n]).then_inc(rms_ok, 1)
                act.wait_ge(h2T_ps, t + 1)
                if t >= 1:
                    act.wait_ge(lr_ps, t)
                w = n
                A(h2T[:, :, 0:w], banks[:, 2048:2048 + KC * w].rearrange("p (k n) -> p k n", k=KC), ACT.Copy).then_inc(h2T_ok, 1)
            act.wait_ge(lr_ps, NT)
            A(sco[:, 0:PT * NE], bank(6, PT * NE), ACT.Exp, scale=-1.0).then_inc(rexp2, 1)
            act.wait_ge(cleared, 7)
            A(sco[0:NB, PT * NE:RE], bank(7, NE, NB), ACT.Exp, scale=-1.0).then_inc(rexp2, 1)

            def split_piece(e, s, p):
                act.wait_ge(piece_in[p], e * 16 + 16)
                A(w_hi[s][p // 2][:, (p % 2) * PIECE:(p % 2 + 1) * PIECE], stage[p], ACT.Copy, scale=WS).then_inc(phi_ok, 1)
            for p in range(3):
                split_piece(0, 0, p)
            stage_end(act, 4)
            split_piece(0, 0, 3)

            nc.scalar.sem_inc(y_cp, 1)
            nc.scalar.sem_inc(yrow_out, 16)
            act.wait_ge(route_ok, 1)

            def high_rows(t):
                act.wait_ge(xgT_ps, t + 2)
                A(xgTh.rearrange("p k n -> p (k n)"), banks[:, 0:D], ACT.Copy).then_inc(xgT_hi, 1)

            def tile(t, split):
                split(0)
                gl = Steps(act, gabs_ok)
                gl.enter(t, 2)
                act.wait_ge(g_ps, t + 1)
                gl.done(A(sg, bank(2), ACT.Abs, scale=1.0 / WS))
                gl.done(A(sg, sg, ACT.Exp, scale=-1.0))
                A(sg, sg, ACT.Ln, bias=C("one")).then_inc(gln_ok, 1)
                act.wait_ge(gsub_ok, t + 1)
                A(sg, sg, ACT.Exp).then_inc(gexp_ok, 1)
                act.wait_ge(hidT_ps, t + 2)
                A(hidT, bank(4), ACT.Copy).then_inc(hidT_ok, 1)
                high_rows(t + 1)
                split(1)
                split(2)
                split(3)
                act.wait_ge(y_ps, t + 1)
                act.wait_ge(yrow_out, t * 16 + 16)
                A(yM, banks[:, 512 * 5:512 * 7], ACT.Copy).then_inc(y_cp, 1)
                act.wait_ge(y_cp, t + 2)
                act.dma_start(slot_rows[bass.ds(t * P, P), :], yM).then_inc(yrow_out, 16)

            def expert(e, s, last):
                start = act.value_load(etab[0:1, bass.ds(e, 1)], min_val=0, max_val=MT - 1)
                end = act.value_load(etab[0:1, bass.ds(e + 1, 1)], min_val=1, max_val=MT)
                tile(start, (lambda p: None) if last else (lambda p: split_piece(e + 1, 1 - s, p)))
                with act.If(end - start - 1):
                    with act.Fori(start + 1, end) as t:
                        tile(t, lambda p: None)
            high_rows(0)
            with act.Fori(0, NE // 2 - 1) as i:
                expert(i * 2, 0, False)
                expert(i * 2 + 1, 1, False)
            expert(NE - 2, 0, False)
            expert(NE - 1, 1, True)
            act.wait_ge(yrow_out, act.value_load(etab[0:1, NE:NE + 1], min_val=NE, max_val=MT) * 16 + 16)
            act.nop(nofuse=True)
            stage_end(act, 5)
            for t in range(NT + 1):
                if t < NT:
                    n = rows_of(t)
                    act.wait_ge(ya_in[t % YS], 32 * (t // YS + 1))
                    ya = yA[t % YS][0:n]
                    A(ya, ya, ACT.Copy, scale=w12[0:n, 2 * t:2 * t + 1]).then_inc(ya_sc, 1)
                if t == 0:
                    continue
                u = t - 1
                n = rows_of(u)
                act.wait_ge(res_ok, NT + t)
                lk.done(A(sqj3[0:n], X1[0:n, u], ACT.Square, accum_out=ss[0:n, u:u + 1]))
                A(rs[0:n, u:u + 1], ss[0:n, u:u + 1], ACT.Sqrt, scale=1.0 / D, bias=eps[0:n]).then_inc(rms_ok, 1)

        @block.vector
        def _(dve):
            v = nc.vector
            lk = Steps(dve, dve_link)
            cl = Steps(dve, cleared)
            cl.done(v.memset(crow, 0.0), wait=False)
            cl.done(v.memset(arena[32:33, o_relx:o_relx + HD], 1.0), wait=False)
            cl.done(v.memset(V(A_HT, TOK, 32), 0.0), wait=False)
            dve.wait_ge(neg_exp_c, 1)
            lk.done(v.tensor_scalar(csig, csig, 1.0, None, ALU.add))
            lk.done(v.reciprocal(csig, csig))
            v.tensor_tensor(crow, crow, csig, ALU.mult).then_inc(silu_c, 1)
            dve.wait_ge(crow_in, 48)
            bo = Steps(dve, bias_ok)
            v.tensor_copy(relr.rearrange("p (b h) -> p b h", b=NB), relx.unsqueeze(1).broadcast_to([33, NB, HD]))\
             .then_inc(bias_ps, 1)
            dve.wait_ge(bias_ps, 2)
            bo.done(v.tensor_copy(bias_rows[:, 0:D], banks[0:HD, 0:D]), wait=False)
            bo.done(v.tensor_copy(bias_rows[:, D:GN], banks[0:HD, D:GN]), wait=False)
            bo.done(v.tensor_copy(sbias, banks[0:NB * HD, 1536:1536 + CK + 1]), wait=False)
            ad = Steps(dve, ada_added)
            with dve.Fori(0, 4) as i:
                ad.enter(i, 3)
                for s in range(3):
                    dve.wait_ge(ada_ps, i * 3 + (s + 1))
                    ad.done(v.tensor_tensor(mod[:, bass.ds(i * 1536 + s * 512, 512)], bank(4 + s, 512, 33), ba[s], ALU.add), wait=False)
                ad.leave(4)
            dve.wait_ge(ada_added, 12)
            dve.wait_ge(vec_in, 96)
            mo = Steps(dve, mod_ok)
            mo.done(v.scalar_tensor_tensor(out=modrow(SC1), in0=modrow(SC1), scalar=1.0, in1=nrm[:, 0:D], op0=ALU.add, op1=ALU.mult))
            mo.done(v.scalar_tensor_tensor(out=modrow(SC2), in0=modrow(SC2), scalar=1.0, in1=nrm[:, D:2 * D], op0=ALU.add, op1=ALU.mult))
            def low_hT(t):
                n, b = rows_of(t), 2 * (t % 2)
                dve.wait_ge(hT_hi, t + 1)
                v.tensor_tensor(hTl[:, :, t * P:t * P + n], banks[:, 512 * b:512 * b + KC * n].rearrange("p (k n) -> p k n", k=KC),
                                hTh[:, :, t * P:t * P + n], ALU.subtract).then_inc(hT_ok, 1)
            for t in range(NT):
                n = rows_of(t)
                x = xt[t % 2][0:n]
                dve.wait_ge(rms_ok, t + 1)
                lk.done(v.reciprocal(rs[0:n, t:t + 1], rs[0:n, t:t + 1]))
                if t == 0:
                    dve.wait_ge(bc_ok, 2)
                ga, sh = (bcA1, bcS1) if t < PT else (modrow(SC1, NB), modrow(SH1, NB))
                lk.done(v.scalar_tensor_tensor(out=x, in0=x, scalar=rs[0:n, t:t + 1], in1=ga, op0=ALU.mult, op1=ALU.mult))
                v.tensor_tensor(x, x, sh, ALU.add).then_inc(norm_ok, 1)
                if t >= 1:
                    low_hT(t - 1)
            low_hT(PT)
            stage_end(dve, 0)

            for j in range(2):
                k = slice(4 * j, 4 * j + 4)
                dve.wait_ge(whi_ok, j + 1)
                v.scalar_tensor_tensor(out=wGl[:, k], in0=wG[:, k], scalar=WS, in1=wGh[:, k], op0=ALU.mult,
                                       op1=ALU.subtract).then_inc(wlo_ok, 1)
            dve.wait_ge(wlo_ok, 2)
            cl.done(v.memset(proj[:, PT], 0.0), wait=False)
            lk.done(v.memset(glT, 1.0), wait=False)
            lk.done(v.memset(state[0], 0.0), wait=False)
            dve.wait_ge(cleared, 4)

            def split_low_part(j, w, high, low):
                k = slice(4 * j, 4 * j + 4)
                v.scalar_tensor_tensor(out=low[:, k].rearrange("p k n -> p (k n)"), in0=w[:, k].rearrange("p k g n -> p (k g n)"),
                                       scalar=WS, in1=high[:, k].rearrange("p k n -> p (k n)"), op0=ALU.mult,
                                       op1=ALU.subtract).then_inc(wlo_ok, 1)
            for t in range(NT):
                n = rows_of(t)
                dve.wait_ge(gproj_ps, t + 1)
                v.tensor_scalar(proj[0:n, t, 512:GW], bank(5 + 2 * (t % 2), GW - 512, n), 1.0 / WS, None, ALU.mult).then_inc(gprojB, 1)
            lk.done(v.memset(blkq[0], 0.0), wait=False)
            lk.done(v.memset(blkq[1], 0.0), wait=False)
            lk.done(v.memset(qz, 0.0), wait=False)
            cl.done(v.memset(oG[:, PT], 0.0), wait=False)
            dve.wait_ge(gl_ps, 1)
            dve.wait_ge(dve_link, lk.n)
            lk.done(v.tensor_copy(glT[0:RANK, 0:S], banks[0:RANK, 0:S]), wait=False)
            v.tensor_copy(glT[0:RANK, S:TOK], bank(2, NB, RANK)).then_inc(gl_ok, 1)
            dve.wait_ge(gl_ok, 1)
            dve.wait_ge(dve_link, lk.n)
            nc.vector.sem_inc(gl_ok, 1)
            dve.wait_ge(lnz_ok, 1)
            lk.done(v.tensor_scalar(L, banks[:, 0:D], 0.0, 1.0 / 16, ALU.min, ALU.mult), wait=False)
            lk.done(v.tensor_scalar(sL, bank(2, P, NB), 0.0, 1.0 / 16, ALU.min, ALU.mult))
            lo = Steps(dve, loga_ok)
            lo.done(v.scalar_tensor_tensor(out=L, in0=T1, scalar=-1.0 / 16, in1=L, op0=ALU.mult, op1=ALU.add))
            lo.done(v.scalar_tensor_tensor(out=sL, in0=sT1, scalar=-1.0 / 16, in1=sL, op0=ALU.mult, op1=ALU.add))
            for j in range(2):
                dve.wait_ge(whi_ok, j + 3)
                split_low_part(j, w0, w0h, w0l)
            E3 = [e.rearrange("p (t n) -> p t n", t=PT) for e in E]
            qv, kv = proj[:, 0:PT, 0:P], proj[:, 0:PT, P:2 * P]
            so = Steps(dve, scaled_ok)
            for n_, (e, src, is_q) in enumerate(((0, qv, 1), (1, kv, 0), (2, kv, 0), (3, qv, 1))):
                dve.wait_ge(edec_ok, e + 1)
                if is_q:
                    so.done(v.scalar_tensor_tensor(out=E3[e], in0=src, scalar=DK ** -0.5, in1=E3[e], op0=ALU.mult, op1=ALU.mult), wait=False)
                else:
                    so.done(v.tensor_tensor(E3[e], src, E3[e], ALU.mult), wait=False)
            dve.wait_ge(gT_ps, 1)
            v.tensor_copy(q4T, banks[:, 1024:1024 + D]).then_inc(q4T_ok, 1)
            nc.vector.sem_inc(state_ok, 1)
            dve.wait_ge(edec_ok, 5)
            for t in range(PT):
                if t >= 2:
                    dve.wait_ge(att_ps, t - 1)
                for h in range(HA):
                    lk.done(v.tensor_copy(blkq[t % 2][32 * h:32 * h + 32, P * h:P * h + P],
                                          banks[32 * h:32 * h + 32, 2048 + t * P:2048 + t * P + P]), wait=False)
                dve.wait_ge(dve_link, lk.n)
                nc.vector.sem_inc(blk_ok, 1)
                dve.wait_ge(ds_ps, t + 1)
                lk.done(v.tensor_tensor(dstate, bank(7, 256), C("blk"), ALU.mult))
                if t >= 1:
                    dve.wait_ge(og_ps, t)
                v.scalar_tensor_tensor(out=state[(t + 1) % 2], in0=state[t % 2], scalar=eblast[:, t:t + 1], in1=dstate,
                                       op0=ALU.mult, op1=ALU.add).then_inc(state_ok, 1)
                dve.wait_ge(state_ok, t + 2)
            dve.wait_ge(sc3_ps, 1)
            v.tensor_copy(sc3, bank(0, 3 * NB)).then_inc(sc3_ok, 1)
            dve.wait_ge(sc3_ok, 1)
            lk.done(v.tensor_tensor(kz, proj[0:NB, PT, P:2 * P].unsqueeze(1).broadcast_to([NB, NB, P]),
                                    ident[0:NB, 0:NB].unsqueeze(2).broadcast_to([NB, NB, P]), ALU.mult))
            qzv = qz.rearrange("p (h n) -> p h n", h=HA)
            for h in range(HA):
                lk.done(v.tensor_scalar(qzv[32 * h:32 * h + 32, h, 0:64:9], sc3[32 * h:32 * h + 32, 2 * NB:3 * NB], DK ** -0.5, None, ALU.mult))
            nc.vector.sem_inc(sc3_ok, 1)
            dve.wait_ge(wG_in, 48)
            sn = Steps(dve, snew_ok)
            sn.done(v.tensor_tensor(sS, sS, sc3[:, 0:NB].unsqueeze(2).broadcast_to([P, NB, DV]), ALU.mult))
            dve.wait_ge(kv_ps, 1)
            kvp = banks[:, 2048:4096].rearrange("p (b n) -> p b n", b=NB)
            for h in range(HA):
                r = slice(32 * h, 32 * h + 32)
                sn.done(v.tensor_tensor(sS[r], sS[r], kvp[r, :, DV * h:DV * h + DV], ALU.add), wait=False)
            dve.wait_ge(osq_ok, 1)
            v.tensor_reduce(ss, tG.rearrange("p t (h n) -> p (t h) n", h=HA), AX_X, ALU.add).then_inc(ossq_ok, 1)
            dve.wait_ge(ostd_ok, 1)
            lk.done(v.reciprocal(rs, rs))
            o4 = oG.rearrange("p t (h n) -> p (t h) n", h=HA)
            lk.done(v.tensor_tensor(o4, o4, rs.unsqueeze(2).broadcast_to([P, NT * HA, DV]), ALU.mult))
            lk.done(v.tensor_tensor(oG, oG, gng.unsqueeze(1).broadcast_to([P, NT, HA * DV]), ALU.mult))
            dve.wait_ge(rexp_ok, 1)
            lk.done(v.tensor_scalar(tG, tG, 1.0, None, ALU.add))
            lk.done(v.reciprocal(tG, tG))
            lk.done(v.tensor_tensor(tG, tG, proj[:, :, 528:784], ALU.mult))
            v.tensor_tensor(oG, oG, tG, ALU.mult).then_inc(og_ok, 1)
            stage_end(dve, 1)

            nc.vector.sem_inc(pair_dve, 1)
            cl.done(v.memset(zeros, 0.0), wait=False)

            def split_low(c, j):
                dve.wait_ge(whi_ok, c * 2 + (j + 3))
                split_low_part(j, wP, wPh, wPl)

            def store_qT(c):
                dve.wait_ge(qkT_ps, c + 1)
                v.tensor_scalar(qT.rearrange("p (t n) -> p t n", t=PT)[:, :, ::-1],
                                banks[:, 0:1024].rearrange("p (t n) -> p t n", t=PT), DH ** -0.5, None,
                                ALU.mult).then_inc(qT_ok, 1)

            def attend(c, last):
                def bias_max(a):
                    hh, i = a // PT, a % PT
                    n = (i + 1) * P
                    b = 2 * (a % 2)
                    dve.wait_ge(s_ps, c * 16 + (a + 1))
                    if i == 0:
                        dve.wait_ge(strip_in[hh], c * 16 + 16)
                    if a >= 2:
                        dve.wait_ge(p_ok, c * 16 + (a - 1))
                    dve.nop(nofuse=True)
                    v.tensor_tensor_reduce(sB[a % 2][:, 0:n], banks[:, 512 * b:512 * b + n], strip[:, hh, P * (PT - 1 - i):D],
                                           1.0, -3e38, ALU.add, ALU.max, mx[:, a % 2:a % 2 + 1]).then_inc(s_read, 1)
                    dve.wait_ge(s_read, c * 16 + (a + 1))
                    v.tensor_scalar(nmx[:, a % 2:a % 2 + 1], mx[:, a % 2:a % 2 + 1], -1.0, None, ALU.mult).then_inc(m_ok, 1)

                def scale_out(a):
                    hh, i = a // PT, a % PT
                    dve.wait_ge(p_ok, c * 16 + (a + 1))
                    lk.done(v.reciprocal(rden[:, a:a + 1], den[:, a:a + 1]))
                    dve.wait_ge(o_ps, c * 16 + (a + 1))
                    v.tensor_scalar(oB[:, i, DH * hh:DH * hh + DH], bank(6, DH), rden[:, a:a + 1], None,
                                    ALU.mult).then_inc(o_ok, 1)
                bias_max(0)
                for a in range(16):
                    if a < 15:
                        if a >= 1:
                            dve.wait_ge(m_ok, c * 16 + (a + 1) - 1)
                        bias_max(a + 1)
                    if a >= 1:
                        scale_out(a - 1)
                    nb = a % PT + 1 - 4
                    if nb > 0:
                        dve.wait_ge(pt_ps, c * 16 + (a + 1))
                        if a >= 2:
                            dve.wait_ge(o_ps, c * 16 + (a - 1))
                        v.tensor_copy(pTB[a % 2][:, 512:512 + nb * P], bank(5, nb * P)).then_inc(pt1_ok, 1)
                    if a in (1, 2) and not last:
                        split_low(c + 1, a - 1)
                scale_out(15)
                if not last:
                    store_qT(c + 1)
                dve.wait_ge(oT_ps, c + 2)
                v.tensor_copy(mixT[:, bass.ds(c + 2, 1), 512:1024].rearrange("p a (t n) -> p (a t) n", t=4),
                              bank(5).rearrange("p (t n) -> p t n", t=4)[:, :, ::-1]).then_inc(pair_dve, 1)
            store_qT(0)
            with dve.Fori(0, PAIRS - 1) as c:
                lk.enter(c, 16)
                attend(c, False)
                lk.leave(PAIRS - 1)
            attend(PAIRS - 1, True)
            stage_end(dve, 2)

            v.tensor_copy(ohb, ident[0:NB, 0:NB].unsqueeze(2).broadcast_to([NB, NB, P])).then_inc(ohb_ok, 1)
            lk.done(v.tensor_tensor(selfp, sqk[:, 0], sqk[:, 1], ALU.mult))
            lk.done(v.tensor_reduce(selfl, selfp.rearrange("p (h d) -> p h d", h=HD), AX_X, ALU.add))
            v.tensor_tensor(selfd.rearrange("p (b h) -> p b h", b=NB), selfl.unsqueeze(1).broadcast_to([NB, NB, HD]),
                            C("diag8", NB).rearrange("p (b h) -> p b h", b=NB), ALU.mult).then_inc(selfd_ok, 1)
            for b in range(NB):
                dve.wait_ge(kc_in[b % 2], 48 * (b // 2 + 1))
                dve.wait_ge(qb_ps, b + 1)
                if b >= 1:
                    dve.wait_ge(slog_ok, b)
                q = banks[:, 1024 * (b % 2):1024 * (b % 2) + QW]
                v.tensor_tensor(prod.rearrange("p (c n) -> p c n", c=2), kCb[b % 2], q.unsqueeze(1).broadcast_to([P, 2, QW]),
                                ALU.mult).then_inc(sprod, 1)
                dve.wait_ge(sprod, b + 1)
                v.tensor_reduce(lg[:, :, HD * b:HD * b + HD], prod.rearrange("p (c h d) -> p c h d", c=2, h=HD), AX_X,
                                ALU.add).then_inc(slog_ok, 1)
            dve.wait_ge(slT_ps, 1)
            n = NB * HD
            lk.done(v.scalar_tensor_tensor(out=srow[:, 0:CK], in0=bank(4, CK, n), scalar=DH ** -0.5, in1=sbias[:, 0:CK],
                                           op0=ALU.mult, op1=ALU.add), wait=False)
            lk.done(v.scalar_tensor_tensor(out=srow[:, CK:CK + 1], in0=bank(5, 1, n), scalar=DH ** -0.5,
                                           in1=sbias[:, CK:CK + 1], op0=ALU.mult, op1=ALU.add))
            st = [V(o_stat + i, 1, n) for i in range(4)]
            lk.done(v.tensor_reduce(st[0], srow, AX_X, ALU.max))
            v.tensor_scalar(st[1], st[0], -1.0, None, ALU.mult).then_inc(smax_ok, 1)
            dve.wait_ge(sexp_ok, 1)
            lk.done(v.reciprocal(st[3], st[2]))
            lk.done(v.tensor_scalar(srow, srow, st[3], None, ALU.mult))
            v.tensor_tensor(pself, srow[:, CK:CK + 1].broadcast_to([n, NB]), C("seq8", n), ALU.mult).then_inc(sp_ok, 1)
            dve.wait_ge(sov_ps, 1)
            so3 = bank(0, 96).rearrange("p (c b j) -> p c b j", c=PAIRS, b=NB)
            lk.done(v.tensor_copy(mixT[0:64, 2:KC, S:TOK], so3[0:64, :, :, 0]), wait=False)
            v.tensor_copy(mixT[64:128, 2:KC, S:TOK], so3[64:128, :, :, 1]).then_inc(smix_ok, 1)
            stage_end(dve, 3)

            for t in range(NT):
                n = rows_of(t)
                dve.wait_ge(op_ps, t + 1)
                if t == 0:
                    dve.wait_ge(bc_ok, 6)
                dve.wait_ge(x_in[t % 2], 16 * (X_LOADS[t % 2] + t // 2 + 1))
                g, ga, sh = (bcG1, bcA2, bcS2) if t < PT else (modrow(G1, NB), modrow(SC2, NB), modrow(SH2, NB))
                b = 2 * (t % 2)
                lk.done(v.tensor_tensor(X1[0:n, t], banks[0:n, 512 * b:512 * b + D], g, ALU.mult))
                v.tensor_tensor(X1[0:n, t], X1[0:n, t], xr[t % 2][0:n], ALU.add).then_inc(res_ok, 1)
                dve.wait_ge(rms_ok, NT + t + 1)
                lk.done(v.reciprocal(rs[0:n, t:t + 1], rs[0:n, t:t + 1]))
                if t >= 2:
                    dve.wait_ge(h2_out[t % 2], 16 * (t // 2))
                    dve.wait_ge(h2T_ps, t - 1)
                h = h2[t % 2][0:n]
                lk.done(v.scalar_tensor_tensor(out=h, in0=X1[0:n, t], scalar=rs[0:n, t:t + 1], in1=ga, op0=ALU.mult, op1=ALU.mult))
                v.tensor_tensor(h, h, sh, ALU.add).then_inc(norm_ok, 1)
                dve.wait_ge(norm_ok, NT + t + 1)
            cl.done(v.memset(sco[:, PT * NE:RE], 1.0), wait=False)
            v4 = lambda a: a.rearrange("p (t g e) -> p (t g) e", t=NT, g=NG)
            v3 = lambda a: a.rearrange("p (t e) -> p t e", t=NT)
            bcE = lambda a, k: a.unsqueeze(2).broadcast_to([P, a.shape[1], k])
            dve.wait_ge(rexp2, 2)
            lk.done(v.tensor_scalar(sco, sco, 1.0, None, ALU.add))
            lk.done(v.reciprocal(sco, sco))
            lk.done(v.tensor_tensor(v3(sel), v3(sco), V(o_rb, NE).unsqueeze(1).broadcast_to([P, NT, NE]), ALU.add))
            p6 = pair6.rearrange("p (g j) -> p g j", j=6)
            s4 = v4(sel)
            lk.done(v.tensor_tensor(p6[:, :, 0:3], s4[:, :, 0:3], s4[:, :, 1:4], ALU.add), wait=False)
            lk.done(v.tensor_tensor(p6[:, :, 3:5], s4[:, :, 0:2], s4[:, :, 2:4], ALU.add), wait=False)
            lk.done(v.tensor_tensor(p6[:, :, 5:6], s4[:, :, 0:1], s4[:, :, 3:4], ALU.add))
            lk.done(v.tensor_reduce(gsc, p6, AX_X, ALU.max))
            g3 = lambda a: a.rearrange("p (t g) -> p t g", t=NT)
            prio_g = C("gprio").unsqueeze(1).broadcast_to([P, NT, NG])
            prio_e = C("eprio").unsqueeze(1).broadcast_to([P, NT, NE])
            lk.done(v.tensor_reduce(gm, g3(gsc), AX_X, ALU.max))
            lk.done(v.tensor_tensor(g3(gsel), g3(gsc), bcE(gm, NG), ALU.is_equal))
            lk.done(v.tensor_tensor(g3(gsel), g3(gsel), prio_g, ALU.mult))
            lk.done(v.tensor_reduce(gm, g3(gsel), AX_X, ALU.max))
            lk.done(v.tensor_tensor(g3(gsel), bcE(gm, NG), prio_g, ALU.is_equal))
            lk.done(v.tensor_tensor(v4(msel), v4(sel), bcE(gsel, PG), ALU.mult))
            lk.done(v.tensor_scalar(gsel, gsel, 1.0, 1e30, ALU.subtract, ALU.mult))
            lk.done(v.tensor_tensor(v4(msel), v4(msel), bcE(gsel, PG), ALU.add))
            for one in (one1, one2):
                lk.done(v.tensor_reduce(gm, v3(msel), AX_X, ALU.max))
                lk.done(v.tensor_tensor(v3(tA), v3(msel), bcE(gm, NE), ALU.is_equal))
                lk.done(v.tensor_tensor(v3(tA), v3(tA), prio_e, ALU.mult))
                lk.done(v.tensor_reduce(gm, v3(tA), AX_X, ALU.max))
                lk.done(v.tensor_tensor(v3(one), bcE(gm, NE), prio_e, ALU.is_equal))
                if one is one1:
                    lk.done(v.tensor_scalar(tA, one, -2e30, None, ALU.mult))
                    lk.done(v.tensor_tensor(msel, msel, tA, ALU.add))
            bt = Steps(dve, both_ok)
            lk.done(v.tensor_tensor(both, one1, one2, ALU.add))
            lk.done(v.tensor_scalar(both[:, PT * NE:RE], both[:, PT * NE:RE], C("srows"), None, ALU.mult))
            nc.vector.sem_inc(both_ok, 1)
            w12v = w12.rearrange("p (t j) -> p t j", j=2)
            for j, one in enumerate((one1, one2)):
                lk.done(v.tensor_tensor(tA, sco, one, ALU.mult))
                lk.done(v.tensor_reduce(w12v[:, :, j:j + 1], v3(tA), AX_X, ALU.add))
            lk.done(v.tensor_reduce(gm, w12v, AX_X, ALU.add))
            lk.done(v.reciprocal(gm, gm))
            lk.done(v.tensor_tensor(w12v, w12v, bcE(gm, 2), ALU.mult))
            dve.wait_ge(rank_ps, 1)
            lk.done(v.tensor_copy(rank, bank(0, RE)), wait=False)
            lk.done(v.tensor_copy(cnt, bank(1, RE)), wait=False)
            lk.done(v.memset(base[:, 0:NE], 0.0))
            for t in range(PT):
                lk.done(v.tensor_tensor(base[:, (t + 1) * NE:(t + 2) * NE], base[:, t * NE:(t + 1) * NE], cnt[:, t * NE:(t + 1) * NE], ALU.add))
            lk.done(v.tensor_tensor(nE, base[:, PT * NE:RE], cnt[:, PT * NE:RE], ALU.add))
            c9 = cmp9.rearrange("p (e t) -> p e t", e=NE)
            lk.done(v.tensor_tensor(c9, bcE(nE, NT), C("thr").unsqueeze(1).broadcast_to([P, NE, NT]), ALU.is_gt))
            lk.done(v.tensor_reduce(tE, c9, AX_X, ALU.add))
            lk.done(v.tensor_scalar(tE, tE, 1.0, None, ALU.max))
            cE = cmpE.rearrange("p (e f) -> p e f", e=NE)
            lk.done(v.tensor_tensor(cE, tE.unsqueeze(1).broadcast_to([P, NE, NE]), C("before").rearrange("p (e f) -> p e f", e=NE), ALU.mult))
            lk.done(v.tensor_reduce(offE, cE, AX_X, ALU.add))
            lk.done(v.tensor_tensor(rank, rank, base, ALU.add))
            lk.done(v.tensor_scalar(nE, offE, float(P), None, ALU.mult))
            lk.done(v.tensor_tensor(v3(rank), v3(rank), nE.unsqueeze(1).broadcast_to([P, NT, NE]), ALU.add))
            sl = slotf.rearrange("p (t j) -> p t j", j=2)
            for j, one in enumerate((one1, one2)):
                lk.done(v.tensor_tensor(tA, rank, one, ALU.mult))
                lk.done(v.tensor_reduce(sl[:, :, j:j + 1], v3(tA), AX_X, ALU.add))
            lk.done(v.tensor_copy(ids[:, 0:2 * NT], slotf))
            lk.done(v.tensor_copy(ids[:, 2 * NT:3 * NT], C("tokid")))
            lk.done(v.tensor_copy(etab[0:1, 0:NE], offE[0:1]))
            lk.done(v.tensor_tensor(offE, offE, tE, ALU.add))
            v.tensor_copy(etab[0:1, NE:NE + 1], offE[0:1, NE - 1:NE]).then_inc(route_ok, 1)

            def split_piece(e, s, p):
                dve.wait_ge(phi_ok, e * PIECES + (p + 1))
                part = slice((p % 2) * PIECE, (p % 2 + 1) * PIECE)
                v.scalar_tensor_tensor(out=w_lo[s][p // 2][:, part], in0=stage[p], scalar=WS,
                                       in1=w_hi[s][p // 2][:, part], op0=ALU.mult, op1=ALU.subtract).then_inc(plo_ok, 1)
            for p in range(3):
                split_piece(0, 0, p)
            stage_end(dve, 4)
            split_piece(0, 0, 3)

            dve.wait_ge(route_ok, 1)
            first_link = lk.n

            def low_rows(t):
                dve.wait_ge(xgT_hi, t + 1)
                v.tensor_tensor(xgTl.rearrange("p k n -> p (k n)"), banks[:, 0:D], xgTh.rearrange("p k n -> p (k n)"),
                                ALU.subtract).then_inc(xgT_ok, 1)

            def tile(t, split):
                lk.n = first_link
                lk.enter(t, 2)
                split(0)
                dve.wait_ge(gabs_ok, t * 2 + 1)
                lk.done(v.tensor_scalar(gmin, bank(2), 0.0, 1.0 / WS, ALU.min, ALU.mult))
                dve.wait_ge(gln_ok, t + 1)
                v.tensor_tensor(sg, gmin, sg, ALU.subtract).then_inc(gsub_ok, 1)
                dve.wait_ge(gexp_ok, t + 1)
                lk.done(v.tensor_tensor(sg, sg, bank(2), ALU.mult))
                dve.wait_ge(u_ps, t + 1)
                dve.wait_ge(hidT_ps, t + 1)
                v.scalar_tensor_tensor(out=hid, in0=sg, scalar=1.0 / (WS * WS), in1=bank(3), op0=ALU.mult,
                                       op1=ALU.mult).then_inc(hid_ok, 1)
                low_rows(t + 1)
                split(1)
                split(2)
                split(3)

            def expert(e, s, last):
                start = dve.value_load(etab[0:1, bass.ds(e, 1)], min_val=0, max_val=MT - 1)
                end = dve.value_load(etab[0:1, bass.ds(e + 1, 1)], min_val=1, max_val=MT)
                tile(start, (lambda p: None) if last else (lambda p: split_piece(e + 1, 1 - s, p)))
                with dve.If(end - start - 1):
                    with dve.Fori(start + 1, end) as t:
                        tile(t, lambda p: None)
            low_rows(0)
            with dve.Fori(0, NE // 2 - 1) as i:
                expert(i * 2, 0, False)
                expert(i * 2 + 1, 1, False)
            expert(NE - 2, 0, False)
            expert(NE - 1, 1, True)
            stage_end(dve, 5)
            lk = Steps(dve, mix_link)
            dve.wait_ge(vec_in, 112)
            for t in range(NT + 1):
                if t < NT:
                    n = rows_of(t)
                    ya, yb = yA[t % YS][0:n], yB[t % YS][0:n]
                    dve.wait_ge(ya_sc, t + 1)
                    dve.wait_ge(ya_in[t % YS], 32 * (t // YS + 1))
                    lk.done(v.scalar_tensor_tensor(out=ya, in0=yb, scalar=w12[0:n, 2 * t + 1:2 * t + 2], in1=ya, op0=ALU.mult, op1=ALU.add))
                    lk.done(v.tensor_tensor(ya, ya, g2b if t < PT else modrow(G2, NB), ALU.mult))
                    v.tensor_tensor(X1[0:n, t], X1[0:n, t], ya, ALU.add).then_inc(res_ok, 1)
                if t == 0:
                    continue
                u = t - 1
                n = rows_of(u)
                dve.wait_ge(rms_ok, 2 * NT + t)
                lk.done(v.reciprocal(rs[0:n, u:u + 1], rs[0:n, u:u + 1]))
                v.scalar_tensor_tensor(out=yA[u % YS][0:n], in0=X1[0:n, u], scalar=rs[0:n, u:u + 1], in1=fng[0:n],
                                       op0=ALU.mult, op1=ALU.mult).then_inc(norm_ok, 1)

        @block.tensor
        def _(pe):
            mm, tr = nc.tensor.matmul, nc.tensor.transpose
            pe.wait_ge(const_in, 16)
            pe.wait_ge(crow_in, 48)
            pe.wait_ge(cleared, 2)
            pe.wait_ge(bias_ps, 1)
            oh, ohs = C("oh", 33), C("ohs", 33)
            for o in range(0, GN, 512):
                w = min(512, GN - o)
                mm(banks[0:HD, o:o + w], relx, oh[:, o:o + w], start=True, stop=True)
            mm(banks[0:NB * HD, 1536:1536 + CK + 1], relr, ohs, start=True, stop=True).then_inc(bias_ps, 1)
            pe.wait_ge(silu_c, 1)
            for k in range(KC):
                last = tr(bank(7, KC * 33)[:, k * 33:(k + 1) * 33], crow[:, k * P:(k + 1) * P], ident[0:33, 0:33])
            last.then_inc(csT_ps, 1)
            pe.wait_ge(csT_ok, 1)
            with pe.Fori(0, 4) as i:
                for s in range(3):
                    pe.wait_ge(ada_in[s], i * 32 + 32)
                    for k in range(KC):
                        last = mm(bank(4 + s, 512, 33), csT[:, k], wa[s][:, k], start=(k == 0), stop=(k == KC - 1))
                    last.then_inc(ada_ps, 1)
            pe.wait_ge(bias_ok, 3)
            for t in range(NT):
                n = rows_of(t)
                pe.wait_ge(norm_ok, t + 1)
                if t >= 2:
                    pe.wait_ge(hT_ok, t - 1)
                b = 2 * (t % 2)
                for k in range(KC):
                    last = tr(banks[:, 512 * b + n * k:512 * b + n * k + n], xt[t % 2][0:n, k * P:(k + 1) * P], ident[0:n, 0:n])
                last.then_inc(hT_ps, 1)
            stage_end(pe, 0)

            def products(out, t, wh, wl, ks, first, last):
                n = rows_of(t)
                tok = slice(t * P, t * P + n)
                for k in ks:
                    mm(out, hTh[:, k, tok], wh(k), start=(first and k == ks[0]), stop=False)
                    mm(out, hTh[:, k, tok], wl(k), start=False, stop=False)
                    done = mm(out, hTl[:, k, tok], wh(k), start=False, stop=(last and k == ks[-1]))
                return done
            for t in range(NT):
                n = rows_of(t)
                if t >= 2:
                    pe.wait_ge(gprojA, t - 1)
                    pe.wait_ge(gprojB, t - 1)
                b = 4 + 2 * (t % 2)
                for j in range(2):
                    if t == 0:
                        pe.wait_ge(wlo_ok, j + 1)
                    for o, w, bb in ((0, 512, b), (512, GW - 512, b + 1)):
                        last = products(bank(bb, w, n), t, lambda k: wGh[:, k, o:o + w], lambda k: wGl[:, k, o:o + w],
                                        range(4 * j, 4 * j + 4), j == 0, j == 1)
                last.then_inc(gproj_ps, 1)
            pe.wait_ge(gprojB, NT)
            pe.wait_ge(gprojA, NT)
            for t in range(PT):
                tr(banks[0:RANK, t * P:(t + 1) * P], proj[:, t, 512:528], ident)
            tr(bank(2, NB, RANK), proj[0:NB, PT, 512:528], ident[0:NB, 0:NB]).then_inc(gl_ps, 1)
            pe.wait_ge(gl_ok, 2)
            wgu = V(o_wgu, P, RANK + 1)
            pe.wait_ge(vec_in, 96)
            for t in range(PT):
                mm(banks[:, t * P:(t + 1) * P], glT[0:RANK + 1, t * P:(t + 1) * P], wgu, start=True, stop=True)
            mm(bank(2, P, NB), glT[0:RANK + 1, S:TOK], wgu, start=True, stop=True).then_inc(z_ps, 1)
            pe.wait_ge(loga_ok, 2)
            for j, name in enumerate(("cum_mid", "cum_rest", "cum")):
                for h in range(2):
                    mm(bank(2 * j + h), C(name), L[:, 512 * h:512 * h + 512], start=True, stop=True)
            for t in range(PT):
                last = mm(bank(6, PT)[:, t:t + 1], L[:, t * P:(t + 1) * P], C("ones")[:, 0:1], start=True, stop=True)
            last.then_inc(cum_ps, 1)
            pe.wait_ge(scaled_ok, 4)
            pe.wait_ge(edec_ok, 6)
            for t in range(PT):
                tr(banks[:, t * P:(t + 1) * P], E[1][:, t * P:(t + 1) * P], ident)
            for t in range(PT):
                tr(banks[:, 1024 + t * P:1024 + (t + 1) * P], E[3][:, t * P:(t + 1) * P], ident)
            for t in range(PT):
                last = tr(banks[:, 2048 + t * P:2048 + (t + 1) * P], E[0][:, t * P:(t + 1) * P], ident)
            last.then_inc(gT_ps, 1)
            pe.wait_ge(k2T_ok, 1)
            pe.wait_ge(q4T_ok, 1)

            def project_first(t):
                if t == 0:
                    pe.wait_ge(wlo_ok, 4)
                else:
                    pe.wait_ge(qkv_ok, t)
                products(bank(6, 384, rows_of(t)), t, lambda k: w0h[:, k], lambda k: w0l[:, k], range(KC), True,
                         True).then_inc(qkv_ps, 1)
            for t in range(PT):
                pe.wait_ge(blk_ok, t + 1)
                if t >= 2:
                    pe.wait_ge(att_cp, t - 1)
                mm(bank(t % 2), k2T[:, t * P:(t + 1) * P], blkq[t % 2], start=True, stop=True).then_inc(att_ps, 1)
                if t >= 1:
                    pe.wait_ge(state_ok, t + 1)
                mm(bank(7, 256), E[2][:, t * P:(t + 1) * P], proj[:, t, 256:512], start=True, stop=True).then_inc(ds_ps, 1)
                project_first(t)
                pe.wait_ge(att_ok, t + 1)
                pe.wait_ge(state_ok, t + 1)
                if t >= 2:
                    pe.wait_ge(og_cp, t - 1)
                ob = bank(2 + t % 2, 256)
                mm(ob, q4T[:, t * P:(t + 1) * P], state[t % 2], start=True, stop=True, skip_group_check=True)
                for h in range(HA):
                    last = mm(ob[:, DV * h:DV * h + DV], attS[t % 2][:, P * h:P * h + P], proj[:, t, 256 + DV * h:256 + DV * h + DV],
                              start=False, stop=True, skip_group_check=True)
                last.then_inc(og_ps, 1)
            project_first(PT)
            pe.wait_ge(att_cp, PT)
            for j, src in enumerate((sA, proj[0:NB, PT, P:2 * P], proj[0:NB, PT, 0:P])):
                last = tr(bank(0, 3 * NB)[:, j * NB:(j + 1) * NB], src, ident[0:NB, 0:NB])
            last.then_inc(sc3_ps, 1)
            pe.wait_ge(sc3_ok, 2)
            pe.wait_ge(state_ok, PT + 1)
            pe.wait_ge(qkv_ok, NT)
            for b in range(NB):
                last = mm(banks[:, 2048 + 256 * b:2048 + 256 * b + 256], kz[:, b], proj[0:NB, PT, 256:512], start=True, stop=True)
            last.then_inc(kv_ps, 1)
            pe.wait_ge(snew_ok, 5)
            for h in range(HA):
                for b in range(NB):
                    last = mm(bank(0, 256, NB)[:, DV * h:DV * h + DV], qz[:, (h * NB + b) * NB:(h * NB + b + 1) * NB], sS[:, b],
                              start=(b == 0), stop=(b == NB - 1))
            last.then_inc(so_ps, 1)
            pe.wait_ge(og_ok, 1)
            for c in range(2):
                for t in range(PT):
                    tr(banks[:, 1024 * c + t * P:1024 * c + (t + 1) * P], oG[:, t, c * P:(c + 1) * P], ident)
                last = tr(bank(4 + c, NB), oG[0:NB, PT, c * P:(c + 1) * P], ident[0:NB, 0:NB])
            last.then_inc(ogT_ps, 1)
            stage_end(pe, 1)

            nc.tensor.sem_inc(oT_ps, 1)

            def project_tile(c, t, halves, b):
                if 0 in halves:
                    if t == 0:
                        pe.wait_ge(wlo_ok, c * 2 + 4)
                    else:
                        pe.wait_ge(qkv_ok, c * NT + t)
                for h in halves:
                    last = products(bank(b, 384, rows_of(t)), t, lambda k: wPh[:, k], lambda k: wPl[:, k],
                                    range(4 * h, 4 * h + 4), h == 0, h == 1)
                if 1 in halves:
                    last.then_inc(qkv_ps, 1)

            def turn_qk(c):
                pe.wait_ge(qkv_ok, c * NT + NT)
                for j in range(2):
                    for t in range(PT):
                        last = tr(banks[:, 1024 * j + t * P:1024 * j + (t + 1) * P], qkv[:, t, j * P:(j + 1) * P], ident)
                last.then_inc(qkT_ps, 1)

            def attend(c, last_pair):
                def scores(a):
                    hh, i = a // PT, a % PT
                    r = slice(DH * hh, DH * hh + DH)
                    if a == 0:
                        pe.wait_ge(qT_ok, c + 1)
                        pe.wait_ge(kT_ok, c + 1)
                    if a >= 2:
                        pe.wait_ge(s_read, c * 16 + (a - 1))
                    for o in range(0, (i + 1) * P, 512):
                        w = min(512, (i + 1) * P - o)
                        b = 2 * (a % 2)
                        last = mm(banks[:, 512 * b + o:512 * b + o + w], qT[r, i * P:(i + 1) * P], kT[r, o:o + w], start=True, stop=True)
                    last.then_inc(s_ps, 1)

                def turn(a):
                    i = a % PT
                    pe.wait_ge(p_ok, c * 16 + (a + 1))
                    if a == 0:
                        pe.wait_ge(pair_dve, c + 1)
                        pe.wait_ge(pair_act, c + 1)
                    for j in range(i + 1):
                        last = tr(banks[:, 2048 + j * P:2048 + (j + 1) * P], pB[a % 2][:, j * P:(j + 1) * P], ident)
                    last.then_inc(pt_ps, 1)

                def values(a):
                    hh, i = a // PT, a % PT
                    pe.wait_ge(pt0_ok, c * 16 + (a + 1))
                    if i >= 4:
                        pe.wait_ge(pt1_ok, c * 8 + (hh * 4 + i - 3))
                    if a == 0:
                        pe.wait_ge(v_ok, c + 1)
                    else:
                        pe.wait_ge(o_ok, c * 16 + a)
                    for j in range(i + 1):
                        last = mm(bank(6, DH), pTB[a % 2][:, j * P:(j + 1) * P], vcur[:, j, DH * hh:DH * hh + DH],
                                  start=(j == 0), stop=(j == i))
                    last.then_inc(o_ps, 1)
                scores(0)
                scores(1)
                for a in range(16):
                    if a >= 1:
                        values(a - 1)
                    if a in STEP_PROJ and not last_pair:
                        project_tile(c + 1, *STEP_PROJ[a], 7)
                    turn(a)
                    if a + 2 < 16:
                        scores(a + 2)
                values(15)
                if not last_pair:
                    pe.wait_ge(s_read, c * 16 + 16)
                    turn_qk(c + 1)
                pe.wait_ge(o_ok, c * 16 + 16)
                for t in range(PT):
                    last = tr(banks[:, 2048 + t * P:2048 + (t + 1) * P], oB[:, t], ident)
                last.then_inc(oT_ps, 1)
            turn_qk(0)
            with pe.Fori(0, PAIRS - 1) as c:
                attend(c, False)
            attend(PAIRS - 1, True)
            stage_end(pe, 2)

            pe.wait_ge(ohb_ok, 1)
            for b in range(NB):
                if b >= 2:
                    pe.wait_ge(sprod, b - 1)
                o = 1024 * (b % 2)
                mm(banks[:, o:o + 512], ohb[:, b], sqk[:, 0, 0:512], start=True, stop=True)
                mm(banks[:, o + 512:o + QW], ohb[:, b], sqk[:, 0, 512:QW], start=True, stop=True).then_inc(qb_ps, 1)
            pe.wait_ge(slog_ok, NB)
            pe.wait_ge(selfd_ok, 1)
            n = NB * HD
            for j in range(2):
                tr(bank(4, CK, n)[:, j * P:(j + 1) * P], lg[:, j], ident)
            mm(bank(5, 1, n), selfd, C("ones", NB)[:, 0:1], start=True, stop=True).then_inc(slT_ps, 1)
            pe.wait_ge(sp_ok, 1)
            for j in range(2):
                tr(bank(6, 2 * n)[:, j * n:(j + 1) * n], srow[:, j * P:(j + 1) * P], ident[0:n, 0:n])
            tr(bank(7, n, NB), pself, ident[0:n, 0:n]).then_inc(spT_ps, 1)
            pe.wait_ge(spT_ok, 1)
            pe.wait_ge(vc_in, 48 * NB)
            for c in range(PAIRS):
                rhs = pselfT.rearrange("p (b h) -> p b h", b=NB)[:, :, 2 * c:2 * c + 2]
                mm(bank(0, 96)[:, 16 * c:16 * c + 16], sqv[:, c * P:(c + 1) * P], rhs, start=(c == 0), stop=True, skip_group_check=True)
            for b in range(NB):
                for c in range(PAIRS):
                    for j in range(2):
                        o = 16 * c + 2 * b
                        last = mm(bank(0, 96)[:, o:o + 2], vC[b][:, j, c * P:(c + 1) * P], spT[:, j, HD * b + 2 * c:HD * b + 2 * c + 2],
                                  start=False, stop=(j == 1), skip_group_check=True)
            last.then_inc(sov_ps, 1)
            stage_end(pe, 3)

            pe.wait_ge(wO_in, 32)

            def project(t):
                n = rows_of(t)
                if t >= 2:
                    pe.wait_ge(res_ok, t - 1)
                b = 2 * (t % 2)
                for h in range(2):
                    for k in range(KC):
                        last = mm(bank(b + h, 512, n), mixT[:, k, t * P:t * P + n], wO[:, k, 512 * h:512 * h + 512], start=(k == 0), stop=(k == KC - 1))
                last.then_inc(op_ps, 1)

            def route(t):
                n = rows_of(t)
                pe.wait_ge(norm_ok, NT + t + 1)
                if t >= 1:
                    pe.wait_ge(h2T_ok, t)
                for k in range(KC):
                    last = tr(banks[:, 2048 + n * k:2048 + n * k + n], h2[t % 2][0:n, k * P:(k + 1) * P], ident[0:n, 0:n])
                last.then_inc(h2T_ps, 1)
                pe.wait_ge(h2T_ok, t + 1)
                out = bank(6, PT * NE)[:, t * NE:(t + 1) * NE] if t < PT else bank(7, NE, NB)
                for k in range(KC):
                    last = mm(out, h2T[:, k, 0:n], rw[:, k], start=(k == 0), stop=(k == KC - 1))
                last.then_inc(lr_ps, 1)
            project(0)
            for t in range(NT):
                if t + 1 < NT:
                    project(t + 1)
                route(t)
            pe.wait_ge(both_ok, 1)
            mm(bank(0, RE), C("strict"), both, start=True, stop=True)
            mm(bank(1, RE), C("ones"), both, start=True, stop=True).then_inc(rank_ps, 1)
            stage_end(pe, 4)

            nc.tensor.sem_inc(xgT_ps, 1)
            nc.tensor.sem_inc(hidT_ps, 1)
            pe.wait_ge(route_ok, 1)

            def pairs(out, xh, xl, wh, wl, ks):
                for k in ks:
                    mm(out, xh[:, k], wh(k), start=(k == 0), stop=False)
                    mm(out, xh[:, k], wl(k), start=False, stop=False)
                    done = mm(out, xl[:, k], wh(k), start=False, stop=(k == ks[-1]))
                return done

            def rows_T(t):
                pe.wait_ge(xg_in, t * 16 + 16)
                for k in range(KC):
                    last = tr(banks[:, k * P:(k + 1) * P], xg[:, k * P:(k + 1) * P], ident)
                last.then_inc(xgT_ps, 1)

            def tile(t, s, e, down_count=None):
                pe.wait_ge(xgT_ok, t + 1)
                for i, (b, sig) in enumerate(((2, g_ps), (3, u_ps))):
                    if e is not None:
                        low_made(pe, e, 2 * i + 1)
                    pairs(bank(b), xgTh, xgTl, lambda k: w_hi[s][i][:, k * FF:(k + 1) * FF],
                          lambda k: w_lo[s][i][:, k * FF:(k + 1) * FF], range(KC)).then_inc(sig, 1)
                rows_T(t + 1)
                pe.wait_ge(hid_ok, t + 1)
                for k in range(4):
                    last = tr(bank(4)[:, k * P:(k + 1) * P], hid[:, k * P:(k + 1) * P], ident)
                last.then_inc(hidT_ps, 1)
                pe.wait_ge(hidT_ok, t + 1)
                if e is not None:
                    pe.wait_ge(down_in[s], down_count)
                pe.wait_ge(y_cp, t + 1)
                for h in range(2):
                    for k in range(4):
                        last = mm(bank(5 + h), hidT[:, k * P:(k + 1) * P], wD[s][:, k * D + h * 512:k * D + h * 512 + 512],
                                  start=(k == 0), stop=(k == 3))
                last.then_inc(y_ps, 1)

            def expert(e, s, turn):
                start = pe.value_load(etab[0:1, bass.ds(e, 1)], min_val=0, max_val=MT - 1)
                end = pe.value_load(etab[0:1, bass.ds(e + 1, 1)], min_val=1, max_val=MT)
                tile(start, s, e, turn * 16 + 16)
                with pe.If(end - start - 1):
                    with pe.Fori(start + 1, end) as t:
                        tile(t, s, None)
            rows_T(0)
            with pe.Fori(0, NE // 2) as i:
                expert(i * 2, 0, i)
                expert(i * 2 + 1, 1, i)
            stage_end(pe, 5)


def shape_constants():
    import math
    import numpy as np
    t = np.zeros((P, CONST_COLS), np.float32)

    def put(name, a, rows=P):
        o, w = _cols[name]
        t[:rows, o:o + w] = np.asarray(a, np.float32).reshape(rows, w)
    r, c = np.arange(P)[:, None], np.arange(P)[None, :]
    put("ident", r == c)
    put("ones", np.ones((P, P)))
    put("cum_mid", (r <= c).astype(np.float32) - (r <= P // 2 - 1))
    put("cum", r <= c)
    put("cum_rest", r > c)
    put("strict", r < c)
    put("blk", r // DK == np.arange(HA * DV)[None, :] // DV)

    def columns(dist):
        d = np.maximum(dist, 0)
        df = np.maximum(d, 1).astype(np.float32)
        large = 16 + (np.log(df / np.float32(16)) / np.float32(math.log(128.0)) * np.float32(16)).astype(np.int32)
        bucket = np.where(d < 16, d, np.minimum(large, 31))
        count = (dist <= 128).astype(int) + ((dist <= 512) & (dist % 4 == 0)) + (dist % 16 == 0)
        count = np.where(dist >= 0, count, 0)
        out = np.zeros((33, dist.size), np.float32)
        out[bucket, np.arange(dist.size)] = 1.0
        out[32] = np.where(count > 0, np.log(np.maximum(count, 1)), NEG)
        return out
    put("oh", columns(S - 1 - np.arange(GN)), 33)
    pos = np.concatenate([np.arange(896, 1024), np.arange(512, 896, 4), np.arange(0, 512, 16), [1024]])
    put("ohs", columns(1024 - pos), 33)
    n = NB * HD
    put("seq8", np.arange(n)[:, None] // HD == np.arange(NB)[None, :], n)
    put("diag8", np.arange(NB)[:, None] == np.arange(n)[None, :] // HD, NB)
    put("eprio", np.tile(NE - np.arange(NE), (P, 1)))
    put("gprio", np.tile(NG - np.arange(NG), (P, 1)))
    put("thr", np.tile(P * np.arange(NT), (P, 1)))
    put("before", np.tile((np.arange(NE)[None, :] < np.arange(NE)[:, None]).reshape(1, -1), (P, 1)))
    put("srows", r < NB)
    put("tokid", np.arange(NT)[None, :] * P + np.arange(P)[:, None])
    put("eps", np.full((P, 1), EPS))
    put("one", np.ones((P, 1)))
    return t


_INS = ["x_prompt", "x_sample", "state_gla", "cache_win_k", "cache_win_v", "c_prompt", "c_sample", "w_ada", "b_ada",
        "norm1_g", "norm2_g", "w_in", "w_gate_up", "b_gate", "gla_norm_g", "w_o", "rel_bias", "router_w", "router_b",
        "moe_w_gate", "moe_w_up", "moe_w_down", "final_norm_g"]
_OUTS = [(1, 1024, 1024), (8, 1, 1024), (1, 1, 4, 32, 64), (1, 1, 1024, 12, 64), (1, 1, 1024, 12, 64),
         (1, 8, 4, 32, 64), (1, 8, 1, 12, 64), (1, 8, 1, 12, 64)]


def kernel(**inputs):
    import numpy as _np
    import concourse.bacc as _bacc
    from concourse import mybir as _mybir
    from concourse.bass_utils import run_bass_kernel_spmd as _run

    nc = _bacc.Bacc("TRN2", target_bir_lowering=False, num_devices=1)
    arrays, args = {}, []
    for name in _INS:
        a = _np.ascontiguousarray(inputs[name])
        arrays[f"in_{name}_dram"] = a
        args.append(nc.dram_tensor(f"in_{name}_dram", a.shape, _mybir.dt.from_np(a.dtype), kind="ExternalInput").ap())
    table = shape_constants()
    arrays["in_consts_dram"] = table
    args.append(nc.dram_tensor("in_consts_dram", table.shape, _mybir.dt.float32, kind="ExternalInput").ap())
    for i, shape in enumerate(_OUTS):
        args.append(nc.dram_tensor(f"out_{i}_dram", shape, _mybir.dt.float32, kind="ExternalOutput").ap())
    build(nc, *args)
    r = _run(nc, [arrays], core_ids=[0])
    return tuple(r.results[0][f"out_{i}_dram"] for i in range(len(_OUTS)))
```
